# Optimizing a Trainium2 kernel written in Bass

```python
import math
import jax
import jax.numpy as jnp
from jax import lax
import numpy as np

D_MODEL = 1024
BATCH = 1
SEQ = 2048
DEPTH = 1

N_MIXERS = 4
HEAD_DIM = 64
ROPE_THETA = 10000.0
Q_BLOCK = 128
EPS = 1e-6
NEG_INF = -1e30
TINY = 1e-30

FOX_HEADS = D_MODEL // HEAD_DIM
FOX_IN = 3 * FOX_HEADS * HEAD_DIM + FOX_HEADS

NSA_HEADS = D_MODEL // HEAD_DIM
NSA_KV_GROUPS = 4
NSA_HPG = NSA_HEADS // NSA_KV_GROUPS
NSA_BLOCK = 64
NSA_TOPN = 16
NSA_WINDOW = 512
NSA_CMP_HIDDEN = 2 * HEAD_DIM
NSA_SEL_CHUNK = 32
NSA_IN = NSA_HEADS * HEAD_DIM + 6 * NSA_KV_GROUPS * HEAD_DIM + 3 * NSA_HEADS

DIL_PAIRS = ((128, 1), (512, 4), (2048, 16))
DIL_HEADS = D_MODEL // HEAD_DIM
DIL_CHUNK = 64
DIL_IN = len(DIL_PAIRS) * 3 * DIL_HEADS * HEAD_DIM

DIFF_HEADS = D_MODEL // (2 * HEAD_DIM)
DIFF_IN = 6 * DIFF_HEADS * HEAD_DIM

N_EXPERTS = 16
N_EXPERT_GROUPS = 4
EXPERTS_PER_GROUP = N_EXPERTS // N_EXPERT_GROUPS
TOP_K = 2
EXPERT_FF = 512
MOE_BLOCK = 128

LAYERS_PER_MIXER = tuple(len(range(m, DEPTH, N_MIXERS)) for m in range(N_MIXERS))
N_FOX, N_NSA, N_DIL, N_DIFF = LAYERS_PER_MIXER

kernel_name = 'hybrid_fox_nsa_dilated_diff_moe'

def rms_norm(x, gain):
    xf = x.astype(jnp.float32)
    y = xf * lax.rsqrt(jnp.mean(xf * xf, axis=-1, keepdims=True) + EPS)
    return (y * gain.astype(jnp.float32)).astype(x.dtype)

def rope_tables(positions, dim):
    inv = ROPE_THETA ** (-jnp.arange(0, dim, 2, dtype=jnp.float32) / dim)
    ang = positions.astype(jnp.float32)[:, None] * inv[None, :]
    return jnp.cos(ang), jnp.sin(ang)

def apply_rope(x, cos, sin):
    x1, x2 = jnp.split(x.astype(jnp.float32), 2, axis=-1)
    return jnp.concatenate([x1 * cos - x2 * sin, x1 * sin + x2 * cos], axis=-1).astype(x.dtype)

def masked_softmax(s, mask):
    s = jnp.where(mask, s, NEG_INF)
    m = jnp.max(s, axis=-1, keepdims=True)
    e = jnp.where(mask, jnp.exp(s - m), 0.0)
    den = jnp.maximum(jnp.sum(e, axis=-1, keepdims=True), TINY)
    return e / den, (m + jnp.log(den))[..., 0]

def split_cols(t, sizes):
    outs, off = [], 0
    for n in sizes:
        outs.append(t[..., off:off + n])
        off += n
    return outs

def to_heads(t, n_heads):
    b, s, _ = t.shape
    return t.reshape(b, s, n_heads, -1).transpose(0, 2, 1, 3)

def from_heads(t):
    b, h, s, d = t.shape
    return t.transpose(0, 2, 1, 3).reshape(b, s, h * d)

def to_blocks(t, n, axis):
    shp = t.shape
    t = t.reshape(shp[:axis] + (n, shp[axis] // n) + shp[axis + 1:])
    return jnp.moveaxis(t, axis, 0)

def from_blocks(t, axis):
    t = jnp.moveaxis(t, 0, axis)
    shp = t.shape
    return t.reshape(shp[:axis] + (shp[axis] * shp[axis + 1],) + shp[axis + 2:])

def sweep_blocks(fn, n_blocks, *blocked):
    return lax.map(lambda a: fn(*a), (jnp.arange(n_blocks),) + tuple(blocked))

def fox_mixer(u, w_in, b_f, q_gain, k_gain, w_out):
    B, S, _ = u.shape
    H, nb, scale = FOX_HEADS, S // Q_BLOCK, HEAD_DIM ** -0.5
    q, k, v, f = split_cols(u @ w_in, [H * HEAD_DIM] * 3 + [H])
    q = rms_norm(to_heads(q, H), q_gain)
    k = rms_norm(to_heads(k, H), k_gain)
    v = to_heads(v, H)
    log_f = jax.nn.log_sigmoid((f + b_f).astype(jnp.float32))
    cum = jnp.cumsum(log_f, axis=1).transpose(0, 2, 1)
    kpos = jnp.arange(S)

    def block(i, qi, ci):
        s = jnp.einsum('bhqd,bhkd->bhqk', qi, k).astype(jnp.float32) * scale
        s = s + ci[..., None] - cum[:, :, None, :]
        qpos = i * Q_BLOCK + jnp.arange(Q_BLOCK)
        p, _ = masked_softmax(s, kpos[None, :] <= qpos[:, None])
        return jnp.einsum('bhqk,bhkd->bhqd', p.astype(v.dtype), v)

    o = from_blocks(sweep_blocks(block, nb, to_blocks(q, nb, 2), to_blocks(cum, nb, 2)), 2)
    return from_heads(o) @ w_out

def nsa_mixer(u, cos, sin, w_in, q_gain, k_gain, cmp_pos, cmp_w1, cmp_w2, w_out):
    B, S, _ = u.shape
    H, G, P, L, HD = NSA_HEADS, NSA_KV_GROUPS, NSA_HPG, NSA_BLOCK, HEAD_DIM
    NB = S // L
    n_sel = min(NSA_TOPN, NB)
    scale = HD ** -0.5
    q, kc, vc, ks, vs, kw, vw, gl = split_cols(u @ w_in, [H * HD] + [G * HD] * 6 + [3 * H])
    q = apply_rope(rms_norm(q.reshape(B, S, G, P, HD).transpose(0, 2, 3, 1, 4), q_gain), cos, sin)
    ks = apply_rope(rms_norm(to_heads(ks, G), k_gain[1]), cos, sin)
    kw = apply_rope(rms_norm(to_heads(kw, G), k_gain[2]), cos, sin)
    vs, vw = to_heads(vs, G), to_heads(vw, G)

    def compress(t, which):
        blk = t.reshape(B, G, NB, L, HD) + cmp_pos[which]
        hid = jax.nn.silu(blk.reshape(B, G, NB, L * HD) @ cmp_w1[which])
        return hid @ cmp_w2[which]

    kc = apply_rope(rms_norm(compress(to_heads(kc, G), 0), k_gain[0]), cos[L - 1::L], sin[L - 1::L])
    vc = compress(to_heads(vc, G), 1)
    t_pos = jnp.arange(S)
    j_blk = jnp.arange(NB)
    s_c = jnp.einsum('bgpsd,bgnd->bgpsn', q, kc).astype(jnp.float32) * scale
    p_c, _ = masked_softmax(s_c, (j_blk[None, :] + 1) * L <= t_pos[:, None] + 1)
    o_cmp = jnp.einsum('bgpsn,bgnd->bgpsd', p_c.astype(vc.dtype), vc)

    cur = t_pos // L
    imp = jnp.sum(p_c, axis=2)
    forced = (j_blk[None, :] == 0) | (j_blk[None, :] == cur[:, None]) | (j_blk[None, :] == cur[:, None] - 1)
    future = j_blk[None, :] > cur[:, None]
    imp = jnp.where(future, -1.0, jnp.where(forced, P + 1.0, imp))
    _, sel = lax.top_k(imp, n_sel)

    C = NSA_SEL_CHUNK
    nch = S // C
    ks_b = ks.reshape(B, G, NB, L, HD)
    vs_b = vs.reshape(B, G, NB, L, HD)
    bi = jnp.arange(B)[:, None, None, None]
    gi = jnp.arange(G)[None, :, None, None]

    def sel_block(i, qi, si):
        kg = ks_b[bi, gi, si].reshape(B, G, C, n_sel * L, HD)
        vg = vs_b[bi, gi, si].reshape(B, G, C, n_sel * L, HD)
        s = jnp.einsum('bgpcd,bgcmd->bgpcm', qi, kg).astype(jnp.float32) * scale
        tok = (si[..., None] * L + jnp.arange(L)).reshape(B, G, C, n_sel * L)
        qpos = i * C + jnp.arange(C)
        p, _ = masked_softmax(s, (tok <= qpos[:, None])[:, :, None])
        return jnp.einsum('bgpcm,bgcmd->bgpcd', p.astype(vg.dtype), vg)

    o_sel = from_blocks(sweep_blocks(sel_block, nch, to_blocks(q, nch, 3), to_blocks(sel, nch, 2)), 3)

    W = NSA_WINDOW
    nb = S // Q_BLOCK
    span = W + Q_BLOCK
    kw_p = jnp.pad(kw, ((0, 0), (0, 0), (W, 0), (0, 0)))
    vw_p = jnp.pad(vw, ((0, 0), (0, 0), (W, 0), (0, 0)))

    def win_block(i, qi):
        kb = lax.dynamic_slice_in_dim(kw_p, i * Q_BLOCK, span, axis=2)
        vb = lax.dynamic_slice_in_dim(vw_p, i * Q_BLOCK, span, axis=2)
        s = jnp.einsum('bgpqd,bgkd->bgpqk', qi, kb).astype(jnp.float32) * scale
        qpos = i * Q_BLOCK + jnp.arange(Q_BLOCK)
        kpos = i * Q_BLOCK - W + jnp.arange(span)
        dist = qpos[:, None] - kpos[None, :]
        p, _ = masked_softmax(s, (dist >= 0) & (dist < W) & (kpos[None, :] >= 0))
        return jnp.einsum('bgpqk,bgkd->bgpqd', p.astype(vb.dtype), vb)

    o_win = from_blocks(sweep_blocks(win_block, nb, to_blocks(q, nb, 3)), 3)

    g = jax.nn.sigmoid(gl.astype(jnp.float32)).reshape(B, S, 3, G, P).transpose(2, 0, 3, 4, 1)[..., None].astype(u.dtype)
    o = g[0] * o_cmp + g[1] * o_sel + g[2] * o_win
    return o.transpose(0, 3, 1, 2, 4).reshape(B, S, H * HD) @ w_out

def dilated_group(q, k, v, window, dilation):
    B, H, S, HD = q.shape
    C = DIL_CHUNK
    nb = S // C
    n_keys = window // dilation + 1
    span = C + window
    scale = HD ** -0.5
    k_p = jnp.pad(k, ((0, 0), (0, 0), (window, 0), (0, 0)))
    v_p = jnp.pad(v, ((0, 0), (0, 0), (window, 0), (0, 0)))
    ql = np.arange(C)[:, None]
    mm = np.arange(n_keys)[None, :]
    local = jnp.asarray(ql + window - mm * dilation)
    rel = jnp.asarray(ql - mm * dilation)

    def block(i, qi):
        kb = lax.dynamic_slice_in_dim(k_p, i * C, span, axis=2)[:, :, local]
        vb = lax.dynamic_slice_in_dim(v_p, i * C, span, axis=2)[:, :, local]
        s = jnp.einsum('bhqd,bhqnd->bhqn', qi, kb).astype(jnp.float32) * scale
        p, lse = masked_softmax(s, i * C + rel >= 0)
        return jnp.einsum('bhqn,bhqnd->bhqd', p.astype(vb.dtype), vb), lse

    o, lse = sweep_blocks(block, nb, to_blocks(q, nb, 2))
    return from_blocks(o, 2), from_blocks(lse, 2)

def dilated_mixer(u, cos, sin, w_in, q_gain, k_gain, w_out):
    B, S, _ = u.shape
    NG = len(DIL_PAIRS)
    proj = (u @ w_in).reshape(B, S, NG, 3, DIL_HEADS, HEAD_DIM).transpose(2, 3, 0, 4, 1, 5)
    outs, lses = [], []
    for gi, (window, dilation) in enumerate(DIL_PAIRS):
        q = apply_rope(rms_norm(proj[gi, 0], q_gain), cos, sin)
        k = apply_rope(rms_norm(proj[gi, 1], k_gain), cos, sin)
        o, lse = dilated_group(q, k, proj[gi, 2], window, dilation)
        outs.append(o)
        lses.append(lse)
    alpha = jax.nn.softmax(jnp.stack(lses, axis=0), axis=0)
    o = jnp.sum(alpha[..., None].astype(u.dtype) * jnp.stack(outs, axis=0), axis=0)
    return from_heads(o) @ w_out

def diff_mixer(u, cos, sin, w_in, q_gain, k_gain, lambdas, sub_gain, w_out, layer_idx):
    B, S, _ = u.shape
    H, HD = DIFF_HEADS, HEAD_DIM
    nb = S // Q_BLOCK
    scale = HD ** -0.5
    q, k, v = split_cols(u @ w_in, [2 * H * HD] * 3)
    q = apply_rope(rms_norm(to_heads(q, 2 * H), q_gain), cos, sin).reshape(B, H, 2, S, HD)
    k = apply_rope(rms_norm(to_heads(k, 2 * H), k_gain), cos, sin).reshape(B, H, 2, S, HD)
    v = to_heads(v, H)
    lam_init = 0.8 - 0.6 * math.exp(-0.3 * layer_idx)
    lam = (jnp.exp(jnp.sum(lambdas[0] * lambdas[1]).astype(jnp.float32))
           - jnp.exp(jnp.sum(lambdas[2] * lambdas[3]).astype(jnp.float32)) + lam_init)
    kpos = jnp.arange(S)

    def block(i, qi):
        s = jnp.einsum('bhcqd,bhckd->bhcqk', qi, k).astype(jnp.float32) * scale
        qpos = i * Q_BLOCK + jnp.arange(Q_BLOCK)
        p, _ = masked_softmax(s, kpos[None, :] <= qpos[:, None])
        a = p[:, :, 0] - lam * p[:, :, 1]
        return jnp.einsum('bhqk,bhkd->bhqd', a.astype(v.dtype), v)

    o = from_blocks(sweep_blocks(block, nb, to_blocks(q, nb, 3)), 2)
    o = rms_norm(o, sub_gain) * (1.0 - lam_init)
    return from_heads(o) @ w_out

def expert_dispatch(xt, eidx, w_gate, w_up, w_down):
    T, D = xt.shape
    NP = T * TOP_K
    E = w_gate.shape[0]
    R = NP + E * MOE_BLOCK
    NBK = R // MOE_BLOCK
    e_flat = eidx.reshape(-1)
    order = jnp.argsort(e_flat)
    e_sorted = e_flat[order]
    counts = jnp.bincount(e_flat, length=E)
    padded = (counts + MOE_BLOCK - 1) // MOE_BLOCK * MOE_BLOCK
    pad_end = jnp.cumsum(padded)
    pad_start = pad_end - padded
    start = jnp.cumsum(counts) - counts
    dest = pad_start[e_sorted] + (jnp.arange(NP) - start[e_sorted])
    row_token = jnp.full((R,), T, jnp.int32).at[dest].set((order // TOP_K).astype(jnp.int32))
    x_pad = jnp.concatenate([xt, jnp.zeros((1, D), xt.dtype)], axis=0)
    xs = x_pad[row_token].reshape(NBK, MOE_BLOCK, D)
    blk_expert = jnp.minimum(jnp.searchsorted(pad_end, jnp.arange(NBK) * MOE_BLOCK, side='right'), E - 1)

    def run(args):
        xb, e = args
        hid = jax.nn.silu(xb @ w_gate[e]) * (xb @ w_up[e])
        return hid @ w_down[e]

    ys = lax.map(run, (xs, blk_expert)).reshape(R, D)
    dest_orig = jnp.zeros((NP,), jnp.int32).at[order].set(dest.astype(jnp.int32))
    return ys[dest_orig].reshape(T, TOP_K, D)

def moe_ffn(u, router_w, router_b, w_gate, w_up, w_down):
    B, S, D = u.shape
    T = B * S
    xt = u.reshape(T, D)
    scores = jax.nn.sigmoid((xt @ router_w).astype(jnp.float32))
    sel = (scores + router_b.astype(jnp.float32)).reshape(T, N_EXPERT_GROUPS, EXPERTS_PER_GROUP)
    grp_score = jnp.sum(lax.top_k(sel, TOP_K)[0], axis=-1)
    grp = jnp.argmax(grp_score, axis=-1)
    in_grp = jnp.take_along_axis(sel, grp[:, None, None], axis=1)[:, 0]
    _, local = lax.top_k(in_grp, TOP_K)
    eidx = grp[:, None] * EXPERTS_PER_GROUP + local
    w = jnp.take_along_axis(scores, eidx, axis=1)
    w = w / jnp.sum(w, axis=-1, keepdims=True)
    y = expert_dispatch(xt, eidx, w_gate, w_up, w_down)
    return jnp.einsum('tk,tkd->td', w.astype(u.dtype), y).reshape(B, S, D)

def setup_inputs(seed: int = 0) -> dict:
    key = jax.random.key(seed)
    keys = jax.random.split(key, 40)
    counter = [0]

    def nxt():
        k = keys[counter[0]]
        counter[0] += 1
        return k

    def nrm(shape, scale):
        return scale * jax.random.normal(nxt(), shape, jnp.float32)

    def gain(shape):
        return 1.0 + 0.1 * jax.random.normal(nxt(), shape, jnp.float32)

    D, HD, L = D_MODEL, HEAD_DIM, NSA_BLOCK
    return {
        'x': nrm((BATCH, SEQ, D), 1.0),
        'c': nrm((BATCH, D), 1.0),
        'fox_w_in': nrm((N_FOX, D, FOX_IN), D ** -0.5),
        'fox_b_f': 2.0 + nrm((N_FOX, FOX_HEADS), 0.5),
        'fox_q_gain': gain((N_FOX, HD)),
        'fox_k_gain': gain((N_FOX, HD)),
        'fox_w_out': nrm((N_FOX, FOX_HEADS * HD, D), (FOX_HEADS * HD) ** -0.5),
        'nsa_w_in': nrm((N_NSA, D, NSA_IN), D ** -0.5),
        'nsa_q_gain': gain((N_NSA, HD)),
        'nsa_k_gain': gain((N_NSA, 3, HD)),
        'nsa_cmp_pos': nrm((N_NSA, 2, L, HD), 0.1),
        'nsa_cmp_w1': nrm((N_NSA, 2, L * HD, NSA_CMP_HIDDEN), (L * HD) ** -0.5),
        'nsa_cmp_w2': nrm((N_NSA, 2, NSA_CMP_HIDDEN, HD), NSA_CMP_HIDDEN ** -0.5),
        'nsa_w_out': nrm((N_NSA, NSA_HEADS * HD, D), (NSA_HEADS * HD) ** -0.5),
        'dil_w_in': nrm((N_DIL, D, DIL_IN), D ** -0.5),
        'dil_q_gain': gain((N_DIL, HD)),
        'dil_k_gain': gain((N_DIL, HD)),
        'dil_w_out': nrm((N_DIL, DIL_HEADS * HD, D), (DIL_HEADS * HD) ** -0.5),
        'diff_w_in': nrm((N_DIFF, D, DIFF_IN), D ** -0.5),
        'diff_q_gain': gain((N_DIFF, HD)),
        'diff_k_gain': gain((N_DIFF, HD)),
        'diff_lambda': nrm((N_DIFF, 4, HD), 0.1),
        'diff_sub_gain': gain((N_DIFF, 2 * HD)),
        'diff_w_out': nrm((N_DIFF, 2 * DIFF_HEADS * HD, D), (2 * DIFF_HEADS * HD) ** -0.5),
        'norm_gain': gain((DEPTH, 2, D)),
        'ada_w': nrm((DEPTH, D, 6 * D), 0.5 * D ** -0.5),
        'ada_b': nrm((DEPTH, 6 * D), 0.02),
        'router_w': nrm((D, N_EXPERTS), D ** -0.5),
        'router_b': nrm((N_EXPERTS,), 0.01),
        'moe_w_gate': nrm((DEPTH, N_EXPERTS, D, EXPERT_FF), D ** -0.5),
        'moe_w_up': nrm((DEPTH, N_EXPERTS, D, EXPERT_FF), D ** -0.5),
        'moe_w_down': nrm((DEPTH, N_EXPERTS, EXPERT_FF, D), EXPERT_FF ** -0.5),
    }

def reference(x, c, fox_w_in, fox_b_f, fox_q_gain, fox_k_gain, fox_w_out,
              nsa_w_in, nsa_q_gain, nsa_k_gain, nsa_cmp_pos, nsa_cmp_w1, nsa_cmp_w2, nsa_w_out,
              dil_w_in, dil_q_gain, dil_k_gain, dil_w_out,
              diff_w_in, diff_q_gain, diff_k_gain, diff_lambda, diff_sub_gain, diff_w_out,
              norm_gain, ada_w, ada_b, router_w, router_b, moe_w_gate, moe_w_up, moe_w_down):
    S = x.shape[1]
    cos, sin = rope_tables(jnp.arange(S), HEAD_DIM)
    cond = jax.nn.silu(c)
    h = x
    for i in range(DEPTH):
        mod = cond @ ada_w[i] + ada_b[i]
        sh1, sc1, g1, sh2, sc2, g2 = jnp.split(mod[:, None, :], 6, axis=-1)
        u = rms_norm(h, norm_gain[i, 0]) * (1.0 + sc1) + sh1
        kind, j = i % N_MIXERS, i // N_MIXERS
        if kind == 0:
            y = fox_mixer(u, fox_w_in[j], fox_b_f[j], fox_q_gain[j], fox_k_gain[j], fox_w_out[j])
        elif kind == 1:
            y = nsa_mixer(u, cos, sin, nsa_w_in[j], nsa_q_gain[j], nsa_k_gain[j], nsa_cmp_pos[j],
                          nsa_cmp_w1[j], nsa_cmp_w2[j], nsa_w_out[j])
        elif kind == 2:
            y = dilated_mixer(u, cos, sin, dil_w_in[j], dil_q_gain[j], dil_k_gain[j], dil_w_out[j])
        else:
            y = diff_mixer(u, cos, sin, diff_w_in[j], diff_q_gain[j], diff_k_gain[j], diff_lambda[j],
                           diff_sub_gain[j], diff_w_out[j], i)
        h = h + g1 * y
        u = rms_norm(h, norm_gain[i, 1]) * (1.0 + sc2) + sh2
        h = h + g2 * moe_ffn(u, router_w, router_b, moe_w_gate[i], moe_w_up[i], moe_w_down[i])
    return h


_drawn_inputs = setup_inputs


def setup_inputs(seed=0):
    import zlib

    import numpy as np

    out = dict(_drawn_inputs(seed))
    spreads = {}
    factors = {}
    for name, (base, spread) in spreads.items():
        noise = np.random.default_rng([zlib.crc32(name.encode()), seed]).standard_normal(out[name].shape)
        drawn = base * np.exp(spread * noise) if base else spread * noise
        out[name] = jnp.asarray(drawn.astype(out[name].dtype))
    for name, factor in factors.items():
        out[name] = (out[name] * factor).astype(out[name].dtype)
    return out
```

```python
from contextlib import ExitStack

import concourse.bass as bass
from concourse import mybir

F32 = mybir.dt.float32
F16 = mybir.dt.float16
I32 = mybir.dt.int32
ACT = mybir.ActivationFunctionType
ALU = mybir.AluOpType
AX = mybir.AxisListType

P = 128
D = 1024
KT = D // P
S = 2048
TT = S // P
H = 16
HD = 64
PAIRS = H // 2
CH = 512
QC = S // CH
TPC = CH // P
E = 16
G = 4
FF = 512
FT = FF // P
R = S * 2 + E * P
NBK = R // P
EPS = 1e-6
WS = 32.0
CS = 16.0
ROWS = 5
BIG = 60000.0
FAR = 1e30


class Memory:

    def __init__(self, nc, ctx):
        self.nc, self.ctx = nc, ctx

    def sb(self, name, shape, dt=F32):
        return self.ctx.enter_context(self.nc.sbuf_tensor(name, shape, dt))

    def ps(self, name, shape, dt=F32):
        return self.ctx.enter_context(self.nc.psum_tensor(name, shape, dt))

    def sem(self, name):
        return self.ctx.enter_context(self.nc.semaphore(name))


def one(ap, i):
    return ap[:, bass.ds(i, 1), :].rearrange("p a n -> p (a n)")


def since(eng, sem, value):
    if not isinstance(value, int) or value > 0:
        eng.wait_ge(sem, value)


def tile_cols(ap, t):
    return ap[:, bass.ds(t * P, P)]


def staggered(eng, lead, follow):
    lead(0, 0)
    with eng.Fori(0, TT // 4 - 1) as g:
        for p in range(4):
            lead(g * 4 + (p + 1), (p + 1) % 4)
            follow(g * 4 + p, p)
    for p in range(4):
        t = TT - 4 + p
        if p < 3:
            lead(t + 1, p + 1)
        follow(t, p)


def modulate(nc, x, c, norm_gain, ada_w, ada_b, K):
    with ExitStack() as ctx:
        m = Memory(nc, ctx)
        mod1 = m.sb("mod1", [P, 2, D])
        mod2 = K["mod2"]
        u_hi, u_lo, ident = K["u_hi"], K["u_lo"], K["ident"]
        gains = m.sb("gains", [P, 2, D])
        stage = m.sb("ada_stage", [P, 2, KT, CH])
        c8 = m.sb("c8", [KT, P])
        cond8 = m.sb("cond8", [KT, P])
        cond = m.sb("cond", [P, KT])
        condb = m.sb("condb", [P, KT, P])
        xt = m.sb("xt", [P, 4, D])
        ut = m.sb("ut", [P, 2, D])
        dump = m.sb("dump", [P, D])
        ssq = m.sb("ssq", [P, TT])
        root = m.sb("root", [P, TT])
        rstd = m.sb("rstd", [P, TT])
        mps = [m.ps(f"mps{i}", [P, CH]) for i in range(2)]
        tps = [m.ps(f"tps{i}", [P, KT, P]) for i in range(2)]

        c_in, b_in, gain_in = m.sem("c_in"), m.sem("b_in"), m.sem("gain_in")
        ada_in = [m.sem(f"ada_in{i}") for i in range(2)]
        x_in = [m.sem(f"x_in{i}") for i in range(4)]
        const0, const1 = m.sem("const0"), m.sem("const1")
        silu_done, cond_turned, condb_ready = m.sem("silu_done"), m.sem("cond_turned"), m.sem("condb_ready")
        mod_ps, mod_ready, mod_scaled = m.sem("mod_ps"), m.sem("mod_ready"), m.sem("mod_scaled")
        gain_ready = m.sem("gain_ready")
        root_ready = m.sem("root_ready")
        square_done, rstd_ready, u_scaled, u_ready = (m.sem(n) for n in ("square_done", "rstd_ready", "u_scaled", "u_ready"))
        u_turned, hi_ready, lo_ready = m.sem("u_turned"), m.sem("hi_ready"), m.sem("lo_ready")
        NADA = 6 * D // CH
        av = ada_w[0].rearrange("(k p) n -> p k n", p=P)

        def mod_chunk(i):
            n, half = divmod(i, 2)
            return (mod1[:, n] if n < 2 else mod2[:, n - 2])[:, half * CH:(half + 1) * CH]

        with nc.Block() as block:

            @block.sync
            def _(sp):
                sp.dma_start(c8[:, :], c.rearrange("a (k p) -> (a k) p", p=P)).then_inc(c_in, 16)
                for i in range(2):
                    sp.dma_start(stage[:, i], av[:, :, i * CH:(i + 1) * CH]).then_inc(ada_in[i], 16)
                sp.dma_start(mod1[:, :, :].rearrange("p a n -> p (a n)"), ada_b[0, 0:2 * D].partition_broadcast(P)).then_inc(b_in, 16)
                sp.dma_start(mod2[:, :, :].rearrange("p a n -> p (a n)"), ada_b[0, 2 * D:].partition_broadcast(P)).then_inc(b_in, 16)
                sp.dma_start(gains[:, :, :], norm_gain[0].partition_broadcast(P)).then_inc(gain_in, 16)
                for i in range(2, NADA):
                    sp.wait_ge(mod_ps, i - 1)
                    sp.dma_start(stage[:, i % 2], av[:, :, i * CH:(i + 1) * CH]).then_inc(ada_in[i % 2], 16)

            @block.gpsimd
            def _(pool):
                nc.gpsimd.memset(K["ident"][:, :], 0.0).then_inc(const0, 1)
                nc.gpsimd.memset(K["ones"][:, :], 1.0).then_inc(const0, 1)
                nc.gpsimd.memset(K["upto"][:, :], 0.0).then_inc(const0, 1)
                nc.gpsimd.memset(K["before"][:, :], 0.0).then_inc(const0, 1)
                nc.gpsimd.memset(K["mask_rows"][:, :], 0.0).then_inc(const0, 1)
                nc.gpsimd.memset(K["big_ident"][:, :], 0.0).then_inc(const0, 1)
                nc.gpsimd.memset(K["eps"][:, 0:1], D * EPS).then_inc(const0, 1)
                nc.gpsimd.memset(K["eps"][:, 1:2], HD * WS * WS * EPS).then_inc(const0, 1)
                pool.wait_ge(const0, 8)

                def fill(buf, compare, value, base=0):
                    return nc.gpsimd.affine_select(out=buf[:, :], in_=buf[:, :], compare_op=compare, fill=value,
                                                   base=base, pattern=[[-1, P]], channel_multiplier=1).then_inc(const1, 1)

                fill(K["ident"], ALU.not_equal, 1.0)
                fill(K["upto"], ALU.is_gt, 1.0)
                fill(K["before"], ALU.is_ge, 1.0)
                fill(K["mask_rows"], ALU.is_ge, -BIG)
                fill(K["big_ident"], ALU.not_equal, BIG)
                pool.wait_ge(const1, 5)

            @block.scalar
            def _(act):
                act.wait_ge(c_in, 16)
                act.wait_ge(const0, 8)
                nc.scalar.activation(cond8[:, :], c8[:, :], ACT.Silu).then_inc(silu_done, 1)
                with act.Fori(0, TT // 4) as g:
                    for p in range(4):
                        act.wait_ge(u_scaled, g * 4)
                        act.dma_start(xt[:, p], x[0, bass.ds(g * 4 * P + p * P, P), :]).then_inc(x_in[p], 16)
                    for p in range(4):
                        act.wait_ge(x_in[p], g * 16 + 16)
                        act.wait_ge(square_done, g * 4 + p)
                        nc.scalar.activation(dump[:, :], xt[:, p], ACT.Square,
                                             accum_out=ssq[:, bass.ds(g * 4 + p, 1)]).then_inc(square_done, 1)
                        act.wait_ge(square_done, g * 4 + p + 1)
                        nc.scalar.activation(root[:, bass.ds(g * 4 + p, 1)], ssq[:, bass.ds(g * 4 + p, 1)], ACT.Sqrt, bias=K["eps"][:, 0:1]).then_inc(root_ready, 1)
                    for p in range(4):
                        t = g * 4 + p
                        act.wait_ge(u_turned, t + 1)
                        nc.scalar.activation(u_hi[:, :, bass.ds(t * P, P)], tps[p % 2][:, :, :], ACT.Copy).then_inc(hi_ready, 1)

            @block.tensor
            def _(pe):
                def mod(i, n):
                    since(pe, mod_ready, i - 1)
                    for k in range(KT):
                        mm = nc.tensor.matmul(mps[n][:, :], condb[:, k], stage[:, n, k], start=(k == 0), stop=(k == KT - 1))
                    mm.then_inc(mod_ps, 1)

                pe.wait_ge(const1, 5)
                pe.wait_ge(silu_done, 1)
                nc.tensor.transpose(mps[0][:, 0:KT], cond8[:, :], ident[0:KT, 0:KT]).then_inc(cond_turned, 1)
                pe.wait_ge(condb_ready, KT + 2)
                for i in range(4):
                    pe.wait_ge(ada_in[i % 2], 16 * (i // 2 + 1))
                    mod(i, i % 2)
                with pe.Fori(0, TT // 4) as g:
                    for p in range(4):
                        t = g * 4 + p
                        pe.wait_ge(u_ready, t + 1)
                        if p < 2:
                            pe.wait_ge(lo_ready, g * 4)
                        else:
                            pe.wait_ge(lo_ready, t - 1)
                        for k in range(KT):
                            mm = nc.tensor.transpose(tps[p % 2][:, k], ut[:, p % 2, k * P:(k + 1) * P], ident[:, :])
                        mm.then_inc(u_turned, 1)
                        if p % 2:
                            n = p // 2
                            pe.wait_ge(ada_in[n], g * 16 + 48)
                            mod(g * 2 + 4 + n, n)

            @block.vector
            def _(dve):
                nc.vector.memset(condb[:, :, :], 1.0).then_inc(condb_ready, 1)
                dve.wait_ge(condb_ready, 1)
                dve.wait_ge(cond_turned, 1)
                nc.vector.tensor_copy(cond[:, :], mps[0][:, 0:KT]).then_inc(condb_ready, 1)
                dve.wait_ge(condb_ready, 2)
                for k in range(KT):
                    nc.vector.tensor_scalar(condb[:, k], condb[:, k], cond[:, k:k + 1], None, ALU.mult).then_inc(condb_ready, 1)
                dve.wait_ge(gain_in, 16)
                nc.vector.tensor_scalar(gains[:, :, :], gains[:, :, :], float(D) ** 0.5, None, ALU.mult).then_inc(gain_ready, 1)
                dve.wait_ge(b_in, 32)

                def add_mod(i, n, out):
                    dve.wait_ge(mod_ps, i + 1)
                    nc.vector.tensor_tensor(out, out, mps[n][:, :], ALU.add).then_inc(mod_ready, 1)

                for i in range(4):
                    add_mod(i, i % 2, mod_chunk(i))
                dve.wait_ge(mod_ready, 4)
                dve.wait_ge(gain_ready, 1)
                nc.vector.scalar_tensor_tensor(out=mod1[:, 1], in0=mod1[:, 1], scalar=1.0, in1=gains[:, 0],
                                               op0=ALU.add, op1=ALU.mult).then_inc(mod_scaled, 1)
                dve.wait_ge(mod_scaled, 1)

                def lo(t, p):
                    dve.wait_ge(hi_ready, t + 1)
                    cols = bass.ds(t * P, P)
                    nc.vector.tensor_tensor(u_lo[:, :, cols], tps[p % 2][:, :, :], u_hi[:, :, cols], ALU.subtract).then_inc(lo_ready, 1)

                with dve.Fori(0, TT // 4) as g:
                    for p in range(4):
                        t = g * 4 + p
                        dve.wait_ge(root_ready, t + 1)
                        nc.vector.reciprocal(rstd[:, bass.ds(t, 1)], root[:, bass.ds(t, 1)]).then_inc(rstd_ready, 1)
                        dve.wait_ge(rstd_ready, t + 1)
                        if p < 2:
                            dve.wait_ge(u_turned, g * 4)
                        else:
                            dve.wait_ge(u_turned, t - 1)
                        nc.vector.scalar_tensor_tensor(out=ut[:, p % 2], in0=xt[:, p], scalar=rstd[:, bass.ds(t, 1)],
                                                       in1=mod1[:, 1], op0=ALU.mult, op1=ALU.mult).then_inc(u_scaled, 1)
                        dve.wait_ge(u_scaled, t + 1)
                        nc.vector.tensor_tensor(ut[:, p % 2], ut[:, p % 2], mod1[:, 0], ALU.add).then_inc(u_ready, 1)
                        if p:
                            lo(t - 1, p - 1)
                    lo(g * 4 + 3, 3)
                    m2 = mod2[:, :, :].rearrange("p a n -> p (a n)")
                    for n in range(2):
                        add_mod(g * 2 + 4 + n, n, m2[:, bass.ds(g * 2 * CH + n * CH, CH)])
                dve.wait_ge(mod_ready, NADA)
                nc.vector.scalar_tensor_tensor(out=mod2[:, 2], in0=mod2[:, 2], scalar=1.0, in1=gains[:, 1],
                                               op0=ALU.add, op1=ALU.mult).then_inc(mod_scaled, 1)
                nc.vector.tensor_scalar(mod2[:, 0], mod2[:, 0], 1.0 / WS, None, ALU.mult).then_inc(mod_scaled, 1)
                dve.wait_ge(mod_scaled, 3)


def project(nc, w_in, b_f, q_gain, k_gain, K, dram):
    with ExitStack() as ctx:
        m = Memory(nc, ctx)
        u_hi, u_lo, ident = K["u_hi"], K["u_lo"], K["ident"]
        HK = KT // 2
        stage = m.sb("w_stage", [P, 2, HK, CH])
        w_hi = m.sb("w_hi", [P, 2, KT, CH], F16)
        w_lo = m.sb("w_lo", [P, 2, KT, CH], F16)
        t_hi = m.sb("t_hi", [P, 4, S], F16)
        t_lo = m.sb("t_lo", [P, 4, S], F16)
        vt = m.sb("vt", [P, 4, CH])
        sq = m.sb("sq", [P, 2, CH])
        qn = m.sb("qn", [P, 2, CH])
        hss = m.sb("hss", [P, 2, 8])
        hrt = m.sb("hrt", [P, 2, 8])
        hrs = m.sb("hrs", [P, 2, 8])
        wf = m.sb("wf", [P, KT, H])
        wf_hi = m.sb("wf_hi", [P, KT, H], F16)
        wf_lo = m.sb("wf_lo", [P, KT, H], F16)
        bfb = m.sb("bfb", [P, H])
        z = m.sb("z", [P, TT, H])
        za = m.sb("za", [P, TT, H])
        cum = m.sb("cum", [P, TT, H])
        gqk = m.sb("gqk", [P, 2])
        grow = m.sb("grow", [H, 2, HD])
        bound = m.sb("bound", [H, 2])
        cumT = m.sb("cumT", [H, S])
        rem = m.sb("rem", [H, 2, CH])
        krow = m.sb("krow", [H, ROWS, CH], F16)
        qrow = m.sb("qrow", [H, ROWS, CH], F16)
        acc = [m.ps(f"acc{i}", [P, CH]) for i in range(2)]
        qps = [m.ps(f"qps{i}", [P, 4, P]) for i in range(2)]
        cps = [m.ps(f"cps{i}", [P, CH]) for i in range(4)]

        def sems(*names):
            return [m.sem(n) for n in names]

        w_in_sem = sems("w_in0", "w_in1")
        wf_in, gain_in, wf_parts, f_ps, z_ready, f_act = sems("wf_in", "gain_in", "wf_parts", "f_ps", "z_ready", "f_act")
        w_hi_ready, w_lo_ready = sems("w_hi_ready", "w_lo_ready")
        acc_ready, sq_ready, hss_ready, hrs_ready, qn_ready = sems("acc_ready", "sq_ready", "hss_ready", "hrs_ready", "qn_ready")
        turned, th_ready, tl_ready, t_out = sems("turned", "th_ready", "tl_ready", "t_out")
        v_ready, hrt_ready = sems("v_ready", "hrt_ready")
        v_out = sems(*[f"v_out{i}" for i in range(4)])
        cum_ps, cum_ready, cumT_ps, cumT_ready = sems("cum_ps", "cum_ready", "cumT_ps", "cumT_ready")
        gains_ready, row_step, row_out = sems("gains_ready", "row_step", "row_out")
        NQK, NCH = 4, 6
        wv = w_in[0].rearrange("(k p) n -> p k n", p=P)

        with nc.Block() as block:

            @block.sync
            def _(sp):
                def load(j):
                    for h in range(2):
                        if j:
                            sp.wait_ge(w_hi_ready, 2 * j - 1 + h)
                            sp.wait_ge(w_lo_ready, 2 * j - 1 + h)
                        sp.dma_start(stage[:, h], wv[:, h * HK:(h + 1) * HK, j * CH:(j + 1) * CH]).then_inc(w_in_sem[h], 16)

                load(0)
                load(1)
                for j in range(NQK):
                    to = (dram["q_hi"], dram["q_lo"]) if j < 2 else (dram["k_hi"], dram["k_lo"])
                    first = 4 * (j % 2)
                    for g in range(QC):
                        cols = slice(g * CH, (g + 1) * CH)
                        sp.wait_ge(th_ready, j * TT + 4 * g + 4)
                        sp.dma_start(to[0][first:first + 4, :, cols].rearrange("a p n -> p a n"), t_hi[:, :, cols]).then_inc(t_out, 16)
                        sp.wait_ge(tl_ready, j * TT + 4 * g + 4)
                        sp.dma_start(to[1][first:first + 4, :, cols].rearrange("a p n -> p a n"), t_lo[:, :, cols]).then_inc(t_out, 16)
                    if j + 2 < NCH:
                        load(j + 2)
                sp.wait_ge(t_out, 16 * 2 * QC * NQK)

            @block.gpsimd
            def _(pool):
                pool.dma_start(grow[:, 0], q_gain[0].partition_broadcast(H)).then_inc(gain_in, 16)
                pool.dma_start(grow[:, 1], k_gain[0].partition_broadcast(H)).then_inc(gain_in, 16)
                for half in range(2):
                    rows = slice(half * HD, (half + 1) * HD)
                    pool.dma_start(gqk[rows, 0:1], q_gain[0].rearrange("(p a) -> p a", a=1)).then_inc(gain_in, 16)
                    pool.dma_start(gqk[rows, 1:2], k_gain[0].rearrange("(p a) -> p a", a=1)).then_inc(gain_in, 16)
                nc.gpsimd.memset(krow[:, :, :], CS).then_inc(row_step, 1)
                nc.gpsimd.memset(qrow[:, :, :], CS).then_inc(row_step, 1)
                pool.wait_ge(gains_ready, 4)
                pool.wait_ge(row_step, 2)
                n = 2
                for g in range(QC):
                    cs = cumT[:, g * CH:(g + 1) * CH]
                    pool.wait_ge(cumT_ready, g + 1)
                    since(pool, row_out, 32 * g)
                    nc.gpsimd.tensor_scalar(krow[:, 2], cs, -1.0 / CS, None, ALU.mult).then_inc(row_step, 1)
                    nc.gpsimd.tensor_scalar(rem[:, 0], cs, -1.0 / CS, None, ALU.mult).then_inc(row_step, 1)
                    pool.wait_ge(row_step, n + 2)
                    nc.gpsimd.tensor_tensor(rem[:, 0], rem[:, 0], krow[:, 2], ALU.subtract).then_inc(row_step, 1)
                    pool.wait_ge(row_step, n + 3)
                    nc.gpsimd.tensor_copy(krow[:, 3], rem[:, 0]).then_inc(row_step, 1)
                    pool.wait_ge(row_step, n + 4)
                    nc.gpsimd.tensor_tensor(krow[:, 4], rem[:, 0], krow[:, 3], ALU.subtract).then_inc(row_step, 1)
                    nc.gpsimd.tensor_scalar(rem[:, 1], cs, bound[:, 1:2], 1.0 / CS, ALU.subtract, ALU.mult).then_inc(row_step, 1)
                    pool.wait_ge(row_step, n + 6)
                    nc.gpsimd.tensor_copy(qrow[:, 0], rem[:, 1]).then_inc(row_step, 1)
                    pool.wait_ge(row_step, n + 7)
                    nc.gpsimd.tensor_tensor(qrow[:, 1], rem[:, 1], qrow[:, 0], ALU.subtract).then_inc(row_step, 1)
                    n += 8
                    pool.wait_ge(row_step, n)
                    pool.dma_start(dram["k_rows"][:, :, g * CH:(g + 1) * CH], krow[:, :, :]).then_inc(row_out, 16)
                    pool.dma_start(dram["q_rows"][:, :, g * CH:(g + 1) * CH], qrow[:, :, :]).then_inc(row_out, 16)
                pool.wait_ge(row_out, 32 * QC)

            @block.scalar
            def _(act):
                act.dma_start(wf[:, :, :], wv[:, :, 3 * D:3 * D + H]).then_inc(wf_in, 16)
                act.dma_start(bfb[:, :], b_f[0].partition_broadcast(P)).then_inc(wf_in, 16)
                act.wait_ge(wf_in, 32)
                nc.scalar.activation(wf_hi[:, :, :], wf[:, :, :], ACT.Copy, scale=WS).then_inc(wf_parts, 1)

                def hi(j):
                    if j >= 2:
                        act.wait_ge(acc_ready, (j - 1) * TT)
                    for h in range(2):
                        act.wait_ge(w_in_sem[h], 16 * (j + 1))
                        nc.scalar.activation(w_hi[:, j % 2, h * HK:(h + 1) * HK], stage[:, h], ACT.Copy, scale=WS).then_inc(w_hi_ready, 1)

                hi(0)
                act.wait_ge(z_ready, 2)
                nc.scalar.activation(za[:, :, :], za[:, :, :], ACT.Exp, scale=-1.0).then_inc(f_act, 1)
                act.wait_ge(f_act, 1)
                nc.scalar.activation(za[:, :, :], za[:, :, :], ACT.Ln, bias=1.0).then_inc(f_act, 1)
                hi(1)
                act.wait_ge(gains_ready, 1)
                for j in range(NQK):
                    base = j * TT

                    def square(t, p):
                        act.wait_ge(acc_ready, t + (base + 1))
                        since(act, hss_ready, t + (base - 1))
                        nc.scalar.activation(sq[:, p % 2], acc[p % 2][:, :], ACT.Square).then_inc(sq_ready, 1)
                        act.wait_ge(hss_ready, t + (base + 1))
                        nc.scalar.activation(hrt[:, p % 2], hss[:, p % 2], ACT.Sqrt, bias=K["eps"][:, 1:2]).then_inc(hrt_ready, 1)

                    def turn_hi(t, p):
                        act.wait_ge(turned, t + (base + 1))
                        scale = gqk[:, 0:1] if j < 2 else 8.0
                        nc.scalar.activation(t_hi[:, :, bass.ds(t * P, P)], qps[p % 2][:, :, :], ACT.Copy, scale=scale).then_inc(th_ready, 1)

                    since(act, t_out, 32 * QC * j)
                    staggered(act, square, turn_hi)
                    if j + 2 < NCH:
                        hi(j + 2)
                for j in range(NCH - NQK):
                    with act.Fori(0, TT // 4) as g:
                        for p in range(4):
                            act.wait_ge(acc_ready, g * 4 + ((NQK + j) * TT + p + 1))
                            act.wait_ge(v_out[p], g * 16 + 64 * j)
                            nc.scalar.activation(vt[:, p], acc[p % 2][:, :], ACT.Copy, scale=1.0 / WS).then_inc(v_ready, 1)
                            act.wait_ge(v_ready, g * 4 + (j * TT + p + 1))
                            act.dma_start(dram["v"][bass.ds(g * 4 * P + p * P, P), j * CH:(j + 1) * CH], vt[:, p]).then_inc(v_out[p], 16)
                for p in range(4):
                    act.wait_ge(v_out[p], 128)

            @block.tensor
            def _(pe):
                pe.wait_ge(wf_parts, 2)
                fz = cps[0][:, 0:TT * H].rearrange("p (t h) -> p t h", h=H)
                with pe.Fori(0, TT) as t:
                    n = 0
                    for a, b in ((u_hi, wf_hi), (u_hi, wf_lo), (u_lo, wf_hi)):
                        for k in range(KT):
                            mm = nc.tensor.matmul(one(fz, t), tile_cols(a[:, k], t), b[:, k], start=(n == 0), stop=(n == 3 * KT - 1))
                            n += 1
                    mm.then_inc(f_ps, 1)

                for j in range(NCH):
                    base = j * TT
                    pe.wait_ge(w_hi_ready, 2 * j + 2)
                    pe.wait_ge(w_lo_ready, 2 * j + 2)

                    def product(t, p):
                        since(pe, qn_ready, t + (base - 1))
                        n = 0
                        for a, b in ((u_hi, w_hi), (u_hi, w_lo), (u_lo, w_hi)):
                            for k in range(KT):
                                mm = nc.tensor.matmul(acc[p % 2][:, :], tile_cols(a[:, k], t), b[:, j % 2, k],
                                                      start=(n == 0), stop=(n == 3 * KT - 1))
                                n += 1
                        mm.then_inc(acc_ready, 1)

                    def turn(t, p):
                        pe.wait_ge(qn_ready, t + (base + 1))
                        since(pe, tl_ready, t + base)
                        for a in range(4):
                            mm = nc.tensor.transpose(qps[p % 2][:, a], qn[:, p % 2, a * P:(a + 1) * P], ident[:, :])
                        mm.then_inc(turned, 1)

                    if j < NQK:
                        staggered(pe, product, turn)
                    else:
                        jv = j - NQK
                        with pe.Fori(0, TT // 4) as g:
                            for p in range(4):
                                if p < 2 and jv == 0:
                                    pe.wait_ge(qn_ready, NQK * TT)
                                    pe.wait_ge(v_ready, g * 4)
                                else:
                                    pe.wait_ge(v_ready, g * 4 + (jv * TT + p - 1))
                                n = 0
                                for a, b in ((u_hi, w_hi), (u_hi, w_lo), (u_lo, w_hi)):
                                    for k in range(KT):
                                        mm = nc.tensor.matmul(acc[p % 2][:, :], tile_cols(a[:, k], g * 4 + p), b[:, j % 2, k],
                                                              start=(n == 0), stop=(n == 3 * KT - 1))
                                        n += 1
                                mm.then_inc(acc_ready, 1)
                    if j == 0:
                        pe.wait_ge(z_ready, 4)
                        cz = cps[1][:, 0:TT * H].rearrange("p (t h) -> p t h", h=H)
                        for t in range(TT - 1):
                            rest = TT - 1 - t
                            nc.tensor.matmul(cz[:, t + 1:TT], K["ones"][:, :], z[:, t:t + 1].broadcast_to([P, rest, H]),
                                             start=(t == 0), stop=False, skip_group_check=True)
                        nc.tensor.matmul(cz, K["upto"][:, :], z[:, :, :], start=False, stop=True,
                                         skip_group_check=True).then_inc(cum_ps, 1)
                    if j == 1:
                        pe.wait_ge(cum_ready, 1)
                        for g in range(QC):
                            for i in range(TPC):
                                mm = nc.tensor.transpose(cps[g][0:H, i * P:(i + 1) * P], cum[:, g * TPC + i], ident[:, :])
                            mm.then_inc(cumT_ps, 1)

            @block.vector
            def _(dve):
                dve.wait_ge(wf_parts, 1)
                nc.vector.scalar_tensor_tensor(out=wf_lo[:, :, :], in0=wf[:, :, :], scalar=WS, in1=wf_hi[:, :, :],
                                               op0=ALU.mult, op1=ALU.subtract).then_inc(wf_parts, 1)
                dve.wait_ge(gain_in, 96)
                nc.vector.tensor_tensor(gqk[:, 0:1], gqk[:, 0:1], gqk[:, 1:2], ALU.mult).then_inc(gains_ready, 1)
                nc.vector.tensor_tensor(grow[:, 0], grow[:, 0], grow[:, 1], ALU.mult).then_inc(gains_ready, 1)
                dve.wait_ge(gains_ready, 2)
                nc.vector.tensor_reduce(bound[:, 0:1], grow[:, 0], AX.X, ALU.max, apply_absolute_value=True).then_inc(gains_ready, 1)
                dve.wait_ge(gains_ready, 3)
                nc.vector.tensor_scalar(bound[:, 1:2], bound[:, 0:1], float(HD) ** 0.5, None, ALU.mult).then_inc(gains_ready, 1)

                def lo(j):
                    for h in range(2):
                        dve.wait_ge(w_hi_ready, 2 * j + h + 1)
                        ks = slice(h * HK, (h + 1) * HK)
                        nc.vector.scalar_tensor_tensor(out=w_lo[:, j % 2, ks], in0=stage[:, h], scalar=WS, in1=w_hi[:, j % 2, ks],
                                                       op0=ALU.mult, op1=ALU.subtract).then_inc(w_lo_ready, 1)

                lo(0)
                dve.wait_ge(f_ps, TT)
                dve.wait_ge(wf_in, 32)
                fz = cps[0][:, 0:TT * H].rearrange("p (t h) -> p t h", h=H)
                bias = bfb[:, :].rearrange("p (a h) -> p a h", a=1).broadcast_to([P, TT, H])
                nc.vector.scalar_tensor_tensor(out=z[:, :, :], in0=fz, scalar=1.0 / WS, in1=bias,
                                               op0=ALU.mult, op1=ALU.add).then_inc(z_ready, 1)
                dve.wait_ge(z_ready, 1)
                nc.vector.scalar_tensor_tensor(out=za[:, :, :], in0=z[:, :, :], scalar=-1.0, in1=z[:, :, :],
                                               op0=ALU.mult, op1=ALU.max).then_inc(z_ready, 1)
                dve.wait_ge(z_ready, 2)
                nc.vector.tensor_scalar(z[:, :, :], z[:, :, :], 0.0, None, ALU.min).then_inc(z_ready, 1)
                dve.wait_ge(z_ready, 3)
                dve.wait_ge(f_act, 2)
                nc.vector.tensor_tensor(z[:, :, :], z[:, :, :], za[:, :, :], ALU.subtract).then_inc(z_ready, 1)
                lo(1)
                for j in range(NQK):
                    base = j * TT

                    def norm(t, p):
                        i = p % 2
                        dve.wait_ge(sq_ready, t + (base + 1))
                        nc.vector.tensor_reduce(hss[:, i], sq[:, i].rearrange("p (h d) -> p h d", d=HD), AX.X, ALU.add).then_inc(hss_ready, 1)
                        dve.wait_ge(hrt_ready, t + (base + 1))
                        nc.vector.reciprocal(hrs[:, i], hrt[:, i]).then_inc(hrs_ready, 1)
                        dve.wait_ge(hrs_ready, t + (base + 1))
                        since(dve, turned, t + (base - 1))
                        r = hrs[:, i].rearrange("p (h a) -> p h a", a=1).broadcast_to([P, 8, HD])
                        nc.vector.tensor_tensor(qn[:, i].rearrange("p (h d) -> p h d", d=HD),
                                                acc[i][:, :].rearrange("p (h d) -> p h d", d=HD), r, ALU.mult).then_inc(qn_ready, 1)

                    def turn_lo(t, p):
                        dve.wait_ge(th_ready, t + (base + 1))
                        scale = gqk[:, 0:1] if j < 2 else 8.0
                        cols = bass.ds(t * P, P)
                        nc.vector.scalar_tensor_tensor(out=t_lo[:, :, cols], in0=qps[p % 2][:, :, :], scalar=scale, in1=t_hi[:, :, cols],
                                                       op0=ALU.mult, op1=ALU.subtract).then_inc(tl_ready, 1)

                    staggered(dve, norm, turn_lo)
                    if j + 2 < NCH:
                        lo(j + 2)
                    if j == 0:
                        dve.wait_ge(cum_ps, 1)
                        nc.vector.tensor_copy(cum[:, :, :], cps[1][:, 0:TT * H].rearrange("p (t h) -> p t h", h=H)).then_inc(cum_ready, 1)
                    if j == 1:
                        for g in range(QC):
                            dve.wait_ge(cumT_ps, g + 1)
                            nc.vector.tensor_copy(cumT[:, g * CH:(g + 1) * CH], cps[g][0:H, :]).then_inc(cumT_ready, 1)


def attend(nc, K, dram):
    with ExitStack() as ctx:
        m = Memory(nc, ctx)
        o_hi, o_lo = K["o_hi"], K["o_lo"]
        kA, kB, qA, qB = ([m.sb(f"{n}{i}", [P, 2, S], F16) for i in range(2)] for n in ("kA", "kB", "qA", "qB"))
        v = [m.sb(f"v{i}", [P, TT, P]) for i in range(2)]
        NPROB = 3
        prob = [m.sb(f"prob{i}", [P, 2, CH]) for i in range(NPROB)]
        den = [m.sb(f"den{i}", [P, 2, CH]) for i in range(2)]
        rden = m.sb("rden", [P, CH])
        o32 = m.sb("o32", [P, CH])
        sps = [m.ps(f"sps{i}", [P, 2, CH]) for i in range(2)]
        ops = [m.ps(f"ops{i}", [P, CH]) for i in range(2)]
        dps = m.ps("dps", [P, CH])
        heads_in = [m.sem(f"heads_in{i}") for i in range(2)]
        s_ready, p_ready, pv_done, den_step, den_bc = (m.sem(n) for n in ("s_ready", "p_ready", "pv_done", "den_step", "den_bc"))
        r_ready, o_ready, oh_ready, ol_ready = (m.sem(n) for n in ("r_ready", "o_ready", "oh_ready", "ol_ready"))
        steps = [(qc, j) for qc in range(QC) for j in range(TPC * (qc + 1))]
        NS = len(steps)
        last_of = {qc: max(i for i, st in enumerate(steps) if st[0] == qc) for qc in range(QC)}
        LOADS = 2 * 8 + 1
        ROWSL = slice(HD, HD + ROWS)
        CK = HD + ROWS

        def left(i):
            qc, j = steps[i]
            return max(0, j - TPC * qc) * P

        with nc.Block() as block:

            @block.sync
            def _(sp):
                def load(pair, sl):
                    for a in range(2):
                        rows = slice(a * HD, (a + 1) * HD)

                        def pair_rows(t):
                            return dram[t][bass.ds(pair, 1), rows, :].rearrange("a p n -> p (a n)")

                        def head_rows(t):
                            return dram[t][bass.ds(pair * 2 + a, 1), :, :].rearrange("a p n -> p (a n)")

                        for to, part in ((kA[sl][0:HD, a], pair_rows("k_hi")), (kA[sl][HD:P, a], pair_rows("k_lo")),
                                         (kB[sl][0:HD, a], pair_rows("k_hi")), (kB[sl][ROWSL, a], head_rows("k_rows")),
                                         (qA[sl][0:HD, a], pair_rows("q_hi")), (qA[sl][HD:P, a], pair_rows("q_hi")),
                                         (qB[sl][0:HD, a], pair_rows("q_lo")), (qB[sl][ROWSL, a], head_rows("q_rows"))):
                            sp.dma_start(to, part).then_inc(heads_in[sl], 16)
                    sp.dma_start(v[sl][:, :, :], dram["v"].rearrange("(t p) n -> p t n", p=P)[:, :, bass.ds(pair * P, P)]).then_inc(heads_in[sl], 16)

                load(0, 0)
                load(1, 1)
                with sp.Fori(1, PAIRS // 2) as g:
                    for sl in range(2):
                        pair = sp.snap(g * 2 + sl)
                        sp.wait_ge(pv_done, g * 2 * NS + (sl - 1) * NS)
                        load(pair, sl)

            @block.tensor
            def _(pe):
                with pe.Fori(0, PAIRS // 2) as g:
                    for sl in range(2):
                        step0 = g * 2 * NS + sl * NS
                        chunk0 = g * 2 * QC + sl * QC

                        def scores(i):
                            qc, j = steps[i]
                            w0 = left(i)
                            ks, qs = slice(j * P, (j + 1) * P), slice(qc * CH + w0, (qc + 1) * CH)
                            if i >= 2 or sl:
                                pe.wait_ge(p_ready, step0 + (i - 1))
                            elif i == 0:
                                pe.wait_ge(p_ready, step0)
                            for a in range(2):
                                out = sps[i % 2][:, a, w0:CH]
                                diag = j >= TPC * qc
                                nc.tensor.matmul(out, kA[sl][:, a, ks], qA[sl][:, a, qs], start=True, stop=False)
                                if diag:
                                    nc.tensor.matmul(sps[i % 2][:, a, w0:w0 + P], K["mask_rows"][:, :], K["big_ident"][:, :],
                                                     start=False, stop=False, skip_group_check=True)
                                mm = nc.tensor.matmul(out, kB[sl][0:CK, a, ks], qB[sl][0:CK, a, qs], start=False, stop=True)
                            mm.then_inc(s_ready, 1)

                        def weigh(i):
                            qc, j = steps[i]
                            w0 = left(i)
                            pe.wait_ge(p_ready, step0 + (i + 1))
                            if j == 0:
                                if qc >= 1 or sl:
                                    pe.wait_ge(o_ready, chunk0 + (qc - 1))
                                else:
                                    pe.wait_ge(o_ready, chunk0)
                            for a in range(2):
                                rows = slice(a * HD, (a + 1) * HD)
                                mm = nc.tensor.matmul(ops[qc % 2][rows, w0:CH], v[sl][:, j, rows], prob[(i + sl * NS) % NPROB][:, a, w0:CH],
                                                      start=(j == 0), stop=(i == last_of[qc]), skip_group_check=True)
                            mm.then_inc(pv_done, 1)

                        def denominators(qc):
                            pe.wait_ge(den_step, step0 + (last_of[qc] + 1))
                            pe.wait_ge(r_ready, chunk0 + qc)
                            for a in range(2):
                                rows = slice(a * HD, (a + 1) * HD)
                                mm = nc.tensor.matmul(dps[rows, :], K["ones"][:, 0:HD], den[qc % 2][:, a], start=True, stop=True, skip_group_check=True)
                            mm.then_inc(den_bc, 1)

                        pe.wait_ge(heads_in[sl], g * 16 * LOADS + 16 * LOADS)
                        scores(0)
                        for i in range(NS):
                            if i + 1 < NS:
                                scores(i + 1)
                            weigh(i)
                            qc, j = steps[i]
                            if j == 1 and qc:
                                denominators(qc - 1)
                        denominators(QC - 1)

            @block.scalar
            def _(act):
                with act.Fori(0, PAIRS // 2) as g:
                    for sl in range(2):
                        step0 = g * 2 * NS + sl * NS
                        for i in range(NS):
                            w0 = left(i)
                            act.wait_ge(s_ready, step0 + (i + 1))
                            back = i - NPROB + 1
                            if back >= 0 or sl:
                                act.wait_ge(pv_done, step0 + back)
                                act.wait_ge(den_step, step0 + back)
                            else:
                                act.wait_ge(pv_done, step0)
                                act.wait_ge(den_step, step0)
                            nc.scalar.activation(prob[(i + sl * NS) % NPROB][:, :, w0:CH], sps[i % 2][:, :, w0:CH], ACT.Exp).then_inc(p_ready, 1)

            @block.vector
            def _(dve):
                with dve.Fori(0, PAIRS // 2) as g:
                    for sl in range(2):
                        step0 = g * 2 * NS + sl * NS
                        chunk0 = g * 2 * QC + sl * QC

                        def divide(qc):
                            pair = g * 2 + sl
                            n = chunk0 + (qc + 1)
                            dve.wait_ge(den_bc, n)
                            nc.vector.reciprocal(rden[:, :], dps[:, :]).then_inc(r_ready, 1)
                            dve.wait_ge(r_ready, n)
                            dve.wait_ge(pv_done, step0 + (last_of[qc] + 1))
                            nc.vector.tensor_tensor(o32[:, :], ops[qc % 2][:, :], rden[:, :], ALU.mult).then_inc(o_ready, 1)
                            dve.wait_ge(o_ready, n)
                            oh = one(o_hi, pair)[:, qc * CH:(qc + 1) * CH]
                            ol = one(o_lo, pair)[:, qc * CH:(qc + 1) * CH]
                            nc.vector.tensor_copy(oh, o32[:, :]).then_inc(oh_ready, 1)
                            dve.wait_ge(oh_ready, n)
                            nc.vector.tensor_tensor(ol, o32[:, :], oh, ALU.subtract).then_inc(ol_ready, 1)

                        for i in range(NS):
                            qc, j = steps[i]
                            w0 = left(i)
                            d = den[qc % 2][:, :, w0:CH]
                            pr = prob[(i + sl * NS) % NPROB][:, :, w0:CH]
                            dve.wait_ge(p_ready, step0 + (i + 1))
                            if j == 0:
                                if qc >= 1 or sl:
                                    dve.wait_ge(den_bc, chunk0 + (qc - 1))
                                else:
                                    dve.wait_ge(den_bc, chunk0)
                                nc.vector.tensor_copy(d, pr).then_inc(den_step, 1)
                            else:
                                dve.wait_ge(den_step, step0 + i)
                                nc.vector.tensor_tensor(d, d, pr, ALU.add).then_inc(den_step, 1)
                            if j == 2 and qc:
                                divide(qc - 1)
                        divide(QC - 1)
                dve.wait_ge(ol_ready, PAIRS * QC)


def merge(nc, x, w_out, router_w, K, dram):
    with ExitStack() as ctx:
        m = Memory(nc, ctx)
        o_hi, o_lo, mod2, ident, score = K["o_hi"], K["o_lo"], K["mod2"], K["ident"], K["score"]
        stage = m.sb("wo_stage", [P, 4, D])
        w_hi = m.sb("wo_hi", [P, PAIRS, D], F16)
        w_lo = m.sb("wo_lo", [P, PAIRS, D], F16)
        rw = m.sb("rw", [P, KT, E])
        xt = m.sb("xt2", [P, 2, D])
        ht = m.sb("ht", [P, 2, D])
        ut = m.sb("ut2", [P, 2, D])
        uT = m.sb("uT", [P, KT, P])
        dump = m.sb("dump2", [P, D])
        ssq = m.sb("ssq2", [P, TT])
        root = m.sb("root2", [P, TT])
        rstd = m.sb("rstd2", [P, TT])
        yps = [m.ps(f"yps{i}", [P, D]) for i in range(2)]
        tps = m.ps("tps2", [P, KT, P])
        rps = m.ps("rps", [P, 2, E])
        wo_in, rw_in = m.sem("wo_in"), m.sem("rw_in")
        x_in = [m.sem(f"x_in{i}b") for i in range(2)]
        h_out = [m.sem(f"h_out{i}") for i in range(2)]
        u_out = [m.sem(f"u_out{i}") for i in range(2)]
        names = "wo_hi_ready wo_lo_ready y_ready y_scaled h_ready square_done root_ready rstd_ready u_scaled u_ready u_turned uT_ready r_ready score_ready"
        s = {n: m.sem(n + "2") for n in names.split()}
        wv = w_out[0].rearrange("(k p) n -> p k n", p=P)

        with nc.Block() as block:

            @block.sync
            def _(sp):
                for k in range(PAIRS):
                    if k >= 4:
                        sp.wait_ge(s["wo_lo_ready"], k - 3)
                    sp.dma_start(stage[:, k % 4], wv[:, k]).then_inc(wo_in, 16)
                    sp.wait_ge(wo_in, 16 * (k + 1))
                with sp.Fori(0, TT // 2) as g:
                    for p in range(2):
                        row = sp.snap(g * 2 * P + p * P)
                        sp.wait_ge(s["h_ready"], g * 2 + p + 1)
                        sp.dma_start(dram["h"][bass.ds(row, P), :], ht[:, p]).then_inc(h_out[p], 16)
                        sp.wait_ge(s["u_ready"], g * 2 + p + 1)
                        sp.dma_start(dram["u2"][bass.ds(row, P), :], ut[:, p]).then_inc(u_out[p], 16)
                for p in range(2):
                    sp.wait_ge(h_out[p], 16 * (TT // 2))
                    sp.wait_ge(u_out[p], 16 * (TT // 2))

            @block.gpsimd
            def _(pool):
                pool.dma_start(rw[:, :, :], router_w.rearrange("(k p) n -> p k n", p=P)).then_inc(rw_in, 16)
                with pool.Fori(0, TT // 2) as g:
                    for p in range(2):
                        pool.wait_ge(s["h_ready"], g * 2)
                        pool.dma_start(xt[:, p], x[0, bass.ds(g * 2 * P + p * P, P), :]).then_inc(x_in[p], 16)

            @block.scalar
            def _(act):
                for k in range(PAIRS):
                    act.wait_ge(wo_in, 16 * (k + 1))
                    nc.scalar.activation(w_hi[:, k], stage[:, k % 4], ACT.Copy, scale=WS).then_inc(s["wo_hi_ready"], 1)

                def square(t, p):
                    act.wait_ge(s["h_ready"], t + 1)
                    since(act, s["square_done"], t)
                    nc.scalar.activation(dump[:, :], ht[:, p % 2], ACT.Square, accum_out=ssq[:, bass.ds(t, 1)]).then_inc(s["square_done"], 1)
                    act.wait_ge(s["square_done"], t + 1)
                    nc.scalar.activation(root[:, bass.ds(t, 1)], ssq[:, bass.ds(t, 1)], ACT.Sqrt, bias=K["eps"][:, 0:1]).then_inc(s["root_ready"], 1)

                def router(t, p):
                    act.wait_ge(s["u_turned"], t + 1)
                    since(act, s["r_ready"], t)
                    nc.scalar.activation(uT[:, :, :], tps[:, :, :], ACT.Copy).then_inc(s["uT_ready"], 1)
                    act.wait_ge(s["r_ready"], t + 1)
                    nc.scalar.activation(one(score, t), rps[:, p % 2], ACT.Copy).then_inc(s["score_ready"], 1)

                staggered(act, square, router)
                act.wait_ge(s["score_ready"], TT)

            @block.tensor
            def _(pe):
                def project_out(t, p):
                    since(pe, s["y_scaled"], t - 1)
                    for half in range(2):
                        cols = slice(half * CH, (half + 1) * CH)
                        n = 0
                        for a, b in ((o_hi, w_hi), (o_hi, w_lo), (o_lo, w_hi)):
                            for k in range(PAIRS):
                                mm = nc.tensor.matmul(yps[p % 2][:, cols], tile_cols(a[:, k], t), b[:, k, cols],
                                                      start=(n == 0), stop=(n == 3 * PAIRS - 1))
                                n += 1
                    mm.then_inc(s["y_ready"], 1)

                def route(t, p):
                    pe.wait_ge(s["u_ready"], t + 1)
                    since(pe, s["uT_ready"], t)
                    for k in range(KT):
                        mm = nc.tensor.transpose(tps[:, k], ut[:, p % 2, k * P:(k + 1) * P], ident[:, :])
                    mm.then_inc(s["u_turned"], 1)
                    pe.wait_ge(s["uT_ready"], t + 1)
                    since(pe, s["score_ready"], t)
                    for k in range(KT):
                        mm = nc.tensor.matmul(rps[:, p % 2], uT[:, k], rw[:, k], start=(k == 0), stop=(k == KT - 1))
                    mm.then_inc(s["r_ready"], 1)

                pe.wait_ge(s["wo_hi_ready"], PAIRS)
                pe.wait_ge(s["wo_lo_ready"], PAIRS)
                pe.wait_ge(rw_in, 16)
                staggered(pe, project_out, route)

            @block.vector
            def _(dve):
                for k in range(PAIRS):
                    dve.wait_ge(s["wo_hi_ready"], k + 1)
                    nc.vector.scalar_tensor_tensor(out=w_lo[:, k], in0=stage[:, k % 4], scalar=WS, in1=w_hi[:, k],
                                                   op0=ALU.mult, op1=ALU.subtract).then_inc(s["wo_lo_ready"], 1)
                with dve.Fori(0, TT // 2) as g:
                    for p in range(2):
                        t = g * 2 + p
                        dve.wait_ge(s["y_ready"], t + 1)
                        dve.wait_ge(h_out[p], g * 16)
                        dve.wait_ge(u_out[p], g * 16)
                        nc.vector.tensor_tensor(ht[:, p], yps[p][:, :], mod2[:, 0], ALU.mult).then_inc(s["y_scaled"], 1)
                        dve.wait_ge(s["y_scaled"], t + 1)
                        dve.wait_ge(x_in[p], g * 16 + 16)
                        nc.vector.tensor_tensor(ht[:, p], ht[:, p], xt[:, p], ALU.add).then_inc(s["h_ready"], 1)
                        dve.wait_ge(s["root_ready"], t + 1)
                        nc.vector.reciprocal(rstd[:, bass.ds(t, 1)], root[:, bass.ds(t, 1)]).then_inc(s["rstd_ready"], 1)
                        dve.wait_ge(s["rstd_ready"], t + 1)
                        dve.wait_ge(s["u_turned"], g * 2)
                        nc.vector.scalar_tensor_tensor(out=ut[:, p], in0=ht[:, p], scalar=rstd[:, bass.ds(t, 1)], in1=mod2[:, 2],
                                                       op0=ALU.mult, op1=ALU.mult).then_inc(s["u_scaled"], 1)
                        dve.wait_ge(s["u_scaled"], t + 1)
                        nc.vector.tensor_tensor(ut[:, p], ut[:, p], mod2[:, 1], ALU.add).then_inc(s["u_ready"], 1)


def route(nc, router_b, K, dram):
    with ExitStack() as ctx:
        m = Memory(nc, ctx)
        score, slot, ends, table = K["score"], K["slot"], K["ends"], K["table"]
        TE = [P, TT, E]
        rb = m.sb("rb", [P, E])
        sel = m.sb("sel", TE)
        pairs = m.sb("pairs", [P, 4, TT * G])
        gscore = m.sb("gscore", [P, TT, G])
        gwin = m.sb("gwin", [P, TT, G])
        best = m.sb("best", [P, TT])
        pick = [m.sb(f"pick{i}", TE) for i in range(2)]
        tmp = m.sb("tmp", TE)
        rank = m.sb("rank", TE)
        sw = m.sb("sw", [P, 3, TT])
        rows = m.sb("rows", [P, 2, TT])
        info = m.sb("info", [P, 2, TT, 2])
        rev_e = m.sb("rev_e", [P, E])
        token = m.sb("token", [P, TT])
        blk = m.sb("blk", [P, NBK])
        cnt = m.sb("cnt", [P, E])
        cnt_i = m.sb("cnt_i", [P, E], I32)
        nblk = m.sb("nblk", [P, E])
        first = m.sb("first", [P, E])
        past = m.sb("past", [P, NBK, E])
        own = m.sb("own", [P, NBK])
        own_i = m.sb("own_i", [P, NBK], I32)
        zero = m.sb("zero", [P, NBK * 2])
        rps, nps = m.ps("rank_ps", [P, 512]), m.ps("cnt_ps", [P, 512])
        rb_in, scored, iotas, chain, picked, ranked, zeroed, info_ready, info_out = (
            m.sem(n) for n in ("rb_in", "scored", "iotas", "chain", "picked", "ranked", "zeroed", "info_ready", "info_out"))

        def spread(ap, n):
            return ap.rearrange("p (a b) -> p a b", b=1).broadcast_to([P, ap.shape[1], n])

        def over(ap, n):
            return ap.rearrange("p (b a) -> p b a", b=1).broadcast_to([P, n, ap.shape[1]])

        with nc.Block() as block:

            @block.sync
            def _(sp):
                sp.dma_start(rb[:, :], router_b.partition_broadcast(P)).then_inc(rb_in, 16)
                sp.wait_ge(iotas, 4)
                sp.dma_start(dram["info"].rearrange("(p a) b -> p (a b)", p=P), zero[:, :]).then_inc(zeroed, 16)

            @block.gpsimd
            def _(pool):
                nc.gpsimd.iota(rev_e[:, :], pattern=[[-1, E]], base=E, channel_multiplier=0, allow_small_or_imprecise_dtypes=True).then_inc(iotas, 1)
                nc.gpsimd.iota(token[:, :].bitcast(I32), pattern=[[P, TT]], base=0, channel_multiplier=1).then_inc(iotas, 1)
                nc.gpsimd.iota(blk[:, :], pattern=[[1, NBK]], base=0, channel_multiplier=0, allow_small_or_imprecise_dtypes=True).then_inc(iotas, 1)
                nc.gpsimd.memset(zero[:, :], 0.0).then_inc(iotas, 1)
                pool.wait_ge(info_ready, 1)
                pool.wait_ge(zeroed, 16)
                for i in range(2):
                    for t in range(TT):
                        pool.indirect_dma_start(out=dram["info"], out_offset=bass.IndirectOffsetOnAxis(ap=slot[:, i, t:t + 1], axis=0),
                                                in_=info[:, i, t], in_offset=None).then_inc(info_out, 16)
                pool.wait_ge(info_out, 16 * 2 * TT)

            @block.scalar
            def _(act):
                nc.scalar.activation(score[:, :, :], score[:, :, :], ACT.Sigmoid).then_inc(scored, 1)

            @block.tensor
            def _(pe):
                pe.wait_ge(picked, 1)
                rz = rps[:, 0:TT * E].rearrange("p (t e) -> p t e", e=E)
                for t in range(TT - 1):
                    nc.tensor.matmul(rz[:, t + 1:TT], K["ones"][:, :], tmp[:, t:t + 1].broadcast_to([P, TT - 1 - t, E]),
                                     start=(t == 0), stop=False, skip_group_check=True)
                nc.tensor.matmul(rz, K["before"][:, :], tmp[:, :, :], start=False, stop=True, skip_group_check=True)
                for t in range(TT):
                    mm = nc.tensor.matmul(nps[:, 0:E], K["ones"][:, :], tmp[:, t], start=(t == 0), stop=(t == TT - 1))
                mm.then_inc(ranked, 1)

            @block.vector
            def _(dve):
                made = [0]

                def then(ins):
                    made[0] += 1
                    ins.then_inc(chain, 1)
                    dve.wait_ge(chain, made[0])

                tt, ts, stt, red = nc.vector.tensor_tensor, nc.vector.tensor_scalar, nc.vector.scalar_tensor_tensor, nc.vector.tensor_reduce
                dve.wait_ge(rb_in, 16)
                dve.wait_ge(scored, 1)
                then(tt(sel[:, :, :], score[:, :, :], over(rb[:, :], TT), ALU.add))
                lane = sel[:, :, :].rearrange("p t (g i) -> p (t g) i", i=4)
                a0, a1, a2, a3 = (lane[:, :, i] for i in range(4))
                b0, b1, b2, b3 = (pairs[:, i] for i in range(4))
                then(tt(b0, a0, a1, ALU.max))
                then(tt(b1, a0, a1, ALU.min))
                then(tt(b2, a2, a3, ALU.max))
                then(tt(b3, a2, a3, ALU.min))
                then(tt(b1, b1, b3, ALU.max))
                then(tt(b3, b0, b2, ALU.min))
                then(tt(b1, b1, b3, ALU.max))
                then(tt(b0, b0, b2, ALU.max))
                gs = gscore[:, :, :]
                then(tt(gs.rearrange("p t g -> p (t g)"), b0, b1, ALU.add))
                dve.wait_ge(iotas, 4)
                rev_g = over(rev_e[:, E - G:E], TT)
                then(red(best[:, :], gs, AX.X, ALU.max))
                then(tt(gwin[:, :, :], gs, spread(best[:, :], G), ALU.is_equal))
                then(tt(gwin[:, :, :], gwin[:, :, :], rev_g, ALU.mult))
                then(red(best[:, :], gwin[:, :, :], AX.X, ALU.max))
                then(tt(gwin[:, :, :], gwin[:, :, :], spread(best[:, :], G), ALU.is_equal))
                wide = gwin[:, :, :].rearrange("p t g -> p (t g)")
                then(tt(sel[:, :, :].rearrange("p t (g i) -> p (t g) i", i=4), lane, spread(wide, 4), ALU.mult))
                then(ts(wide, wide, 1.0, FAR, ALU.subtract, ALU.mult))
                then(tt(sel[:, :, :].rearrange("p t (g i) -> p (t g) i", i=4), lane, spread(wide, 4), ALU.add))
                for i in range(2):
                    pk = pick[i][:, :, :]
                    then(red(best[:, :], sel[:, :, :], AX.X, ALU.max))
                    then(tt(pk, sel[:, :, :], spread(best[:, :], E), ALU.is_equal))
                    then(tt(pk, pk, over(rev_e[:, :], TT), ALU.mult))
                    then(red(best[:, :], pk, AX.X, ALU.max))
                    then(tt(pk, pk, spread(best[:, :], E), ALU.is_equal))
                    if i == 0:
                        then(stt(out=sel[:, :, :], in0=pk, scalar=-2 * FAR, in1=sel[:, :, :], op0=ALU.mult, op1=ALU.add))
                    then(tt(tmp[:, :, :], pk, score[:, :, :], ALU.mult))
                    then(red(sw[:, i], tmp[:, :, :], AX.X, ALU.add))
                tt(tmp[:, :, :], pick[0][:, :, :], pick[1][:, :, :], ALU.add).then_inc(picked, 1)
                then(tt(sw[:, 2], sw[:, 0], sw[:, 1], ALU.add))
                then(nc.vector.reciprocal(sw[:, 2], sw[:, 2]))
                for i in range(2):
                    then(tt(info[:, i, :, 1], sw[:, i], sw[:, 2], ALU.mult))
                    then(nc.vector.tensor_copy(info[:, i, :, 0].bitcast(I32), token[:, :].bitcast(I32)))
                dve.wait_ge(ranked, 1)
                then(ts(cnt_i[:, :], nps[:, 0:E], float(P - 1), None, ALU.add))
                then(ts(cnt_i[:, :], cnt_i[:, :], 7, None, ALU.arith_shift_right))
                then(nc.vector.tensor_copy(nblk[:, :], cnt_i[:, :]))
                then(nc.vector.tensor_tensor_scan(ends[:, :], K["ones"][:, 0:E], nblk[:, :], 0.0, ALU.mult, ALU.add))
                then(tt(first[:, :], ends[:, :], nblk[:, :], ALU.subtract))
                then(ts(first[:, :], first[:, :], float(P), None, ALU.mult))
                then(tt(rank[:, :, :], rps[:, 0:TT * E].rearrange("p (t e) -> p t e", e=E), over(first[:, :], TT), ALU.add))
                for i in range(2):
                    then(tt(tmp[:, :, :], rank[:, :, :], pick[i][:, :, :], ALU.mult))
                    then(red(rows[:, i], tmp[:, :, :], AX.X, ALU.add))
                then(nc.vector.tensor_copy(slot[:, :, :], rows[:, :, :]))
                nc.vector.tensor_copy(cnt[:, :], nblk[:, :]).then_inc(info_ready, 1)
                then(tt(past[:, :, :], over(ends[:, :], NBK), spread(blk[:, :], E), ALU.is_le))
                then(red(own[:, :], past[:, :, :], AX.X, ALU.add))
                then(ts(own[:, :], own[:, :], float(E - 1), None, ALU.min))
                then(ts(table[:, 0], own[:, :], 1.0, None, ALU.add))
                then(nc.vector.tensor_copy(own_i[:, :], own[:, :]))
                then(ts(table[:, 1], own_i[:, :], 1, None, ALU.bitwise_and))
                then(nc.vector.memset(own[:, 0:E], 0.0))
                then(nc.vector.tensor_copy(own[:, 2:E], ends[:, 0:E - 2]))
                then(nc.vector.tensor_copy(table[:, 2, 0:E], own[:, 0:E]))


def experts(nc, w_gate, w_up, w_down, K, dram):
    with ExitStack() as ctx:
        m = Memory(nc, ctx)
        ident, table, mod2 = K["ident"], K["table"], K["mod2"]
        wg = m.sb("wg", [P, 2 * KT, FF])
        wu = m.sb("wu", [P, 2 * KT, FF])
        wd = m.sb("wd", [P, 2 * FT, D])
        info = m.sb("info_all", [P, NBK, 2])
        idx = m.sb("idx", [P, 2], I32)
        xg = m.sb("xg", [P, 2, D])
        xT = m.sb("xT", [P, 2, KT, P])
        act_g = m.sb("act_g", [P, FF])
        hid = m.sb("hid", [P, 2, FF])
        hT = m.sb("hT", [P, FT, P])
        ys = m.sb("ys", [P, 2, D])
        tps = m.ps("tps3", [P, KT, P])
        gps, ups = m.ps("gps", [P, FF]), m.ps("ups", [P, FF])
        hps = m.ps("hps", [P, FT, P])
        yps = m.ps("yps3", [P, D])
        info_in, w_in = m.sem("info_in"), m.sem("w_in_e")
        x_in = [m.sem(f"xg_in{i}") for i in range(2)]
        y_out = [m.sem(f"y_out{i}") for i in range(2)]
        names = "idx_ready idx_seen x_turned xT_ready g_ready silu_ready hid_ready h_turned hT_ready y_ready ys_ready up_ready"
        s = {n: m.sem(n + "3") for n in names.split()}
        W_LOADS = 16 * 3

        with nc.Block() as block:

            @block.sync
            def _(sp):
                with sp.Fori(0, E // 2) as g:
                    for n in range(2):
                        e = sp.snap(g * 2 + n)
                        until = sp.value_load(table[0:1, 2, bass.ds(e, 1)], min_val=0, max_val=NBK)
                        sp.wait_ge(w_in, e * W_LOADS)
                        sp.wait_ge(s["y_ready"], until)
                        sp.dma_start(wg[:, n * KT:(n + 1) * KT], w_gate[0, bass.ds(e, 1)].rearrange("a (k p) n -> p (a k) n", p=P)).then_inc(w_in, 16)
                        sp.dma_start(wu[:, n * KT:(n + 1) * KT], w_up[0, bass.ds(e, 1)].rearrange("a (k p) n -> p (a k) n", p=P)).then_inc(w_in, 16)
                        sp.dma_start(wd[:, n * FT:(n + 1) * FT], w_down[0, bass.ds(e, 1)].rearrange("a (k p) n -> p (a k) n", p=P)).then_inc(w_in, 16)

            @block.gpsimd
            def _(pool):
                pool.dma_start(info[:, :, :], dram["info"].rearrange("(b p) n -> p b n", p=P)).then_inc(info_in, 16)
                pool.wait_ge(info_in, 16)
                with pool.Fori(0, NBK // 2) as g:
                    for p in range(2):
                        pool.wait_ge(s["x_turned"], g * 2)
                        nc.gpsimd.tensor_copy(idx[:, p:p + 1], info[:, bass.ds(g * 2 + p, 1), 0].bitcast(I32)).then_inc(s["idx_ready"], 1)
                        pool.wait_ge(s["idx_ready"], g * 2 + p + 1)
                        pool.sem_inc(s["idx_seen"], 1)
                        pool.indirect_dma_start(out=xg[:, p], out_offset=None, in_=dram["u2"],
                                                in_offset=bass.IndirectOffsetOnAxis(ap=idx[:, p:p + 1], axis=0)).then_inc(x_in[p], 16)

            def blocks(body):
                def run(eng):
                    body(0, 0)
                    body(1, 1)
                    with eng.Fori(1, NBK // 2 - 1) as g:
                        for p in range(2):
                            body(g * 2 + p, p)
                    body(NBK - 2, 0)
                    body(NBK - 1, 1)
                return run

            def is_first(b):
                return isinstance(b, int) and b == 0

            def is_last(b):
                return isinstance(b, int) and b == NBK - 1

            def uses(b, p):
                return b * 8 - 8 * p

            @block.tensor
            def _(pe):
                def turn(b, p):
                    pe.wait_ge(x_in[p], uses(b, p) + 16)
                    since(pe, s["xT_ready"], b)
                    for k in range(KT):
                        mm = nc.tensor.transpose(tps[:, k], xg[:, p, k * P:(k + 1) * P], ident[:, :])
                    mm.then_inc(s["x_turned"], 1)

                def turn_hidden(b, p):
                    pe.wait_ge(s["hid_ready"], b + 1)
                    since(pe, s["hT_ready"], b)
                    for k in range(FT):
                        mm = nc.tensor.transpose(hps[:, k], hid[:, p, k * P:(k + 1) * P], ident[:, :])
                    mm.then_inc(s["h_turned"], 1)

                def down(b):
                    half = pe.value_load(table[0:1, 1, bass.ds(b, 1)], min_val=0, max_val=1)
                    pe.wait_ge(s["hT_ready"], b + 1)
                    since(pe, s["ys_ready"], b)
                    for c in range(2):
                        cols = slice(c * CH, (c + 1) * CH)
                        for k in range(FT):
                            mm = nc.tensor.matmul(yps[:, cols], hT[:, k], one(wd, half * FT + k)[:, cols], start=(k == 0), stop=(k == FT - 1))
                    mm.then_inc(s["y_ready"], 1)

                def body(b, p):
                    need = pe.value_load(table[0:1, 0, bass.ds(b, 1)], min_val=1, max_val=E)
                    half = pe.value_load(table[0:1, 1, bass.ds(b, 1)], min_val=0, max_val=1)
                    if is_first(b):
                        turn(b, p)
                    if not is_last(b):
                        turn(b + 1, 1 - p)
                    pe.wait_ge(s["xT_ready"], b + 1)
                    pe.wait_ge(w_in, need * W_LOADS)
                    since(pe, s["silu_ready"], b)
                    for k in range(KT):
                        mm = nc.tensor.matmul(gps[:, :], xT[:, p, k], one(wg, half * KT + k), start=(k == 0), stop=(k == KT - 1))
                    mm.then_inc(s["g_ready"], 1)
                    if not is_first(b):
                        turn_hidden(b - 1, 1 - p)
                    since(pe, s["hid_ready"], b)
                    for k in range(KT):
                        mm = nc.tensor.matmul(ups[:, :], xT[:, p, k], one(wu, half * KT + k), start=(k == 0), stop=(k == KT - 1))
                    mm.then_inc(s["up_ready"], 1)
                    if not is_first(b):
                        down(b - 1)

                blocks(body)(pe)
                turn_hidden(NBK - 1, 1)
                down(NBK - 1)

            @block.scalar
            def _(act):
                def turn(b, p):
                    act.wait_ge(s["x_turned"], b + 1)
                    since(act, s["up_ready"], b - 1)
                    nc.scalar.activation(xT[:, p], tps[:, :, :], ACT.Copy).then_inc(s["xT_ready"], 1)

                def store(b, p):
                    act.wait_ge(s["ys_ready"], b + 1)
                    act.dma_start(dram["ys"][bass.ds(b * P, P), :], ys[:, p]).then_inc(y_out[p], 16)

                def body(b, p):
                    if is_first(b):
                        turn(b, p)
                    if not is_last(b):
                        turn(b + 1, 1 - p)
                    act.wait_ge(s["g_ready"], b + 1)
                    since(act, s["hid_ready"], b)
                    nc.scalar.activation(act_g[:, :], gps[:, :], ACT.Silu).then_inc(s["silu_ready"], 1)
                    if not isinstance(b, int) or b >= 2:
                        store(b - 2, p)

                blocks(body)(act)
                for p in range(2):
                    store(NBK - 2 + p, p)
                for p in range(2):
                    act.wait_ge(y_out[p], 16 * (NBK // 2))

            @block.vector
            def _(dve):
                dve.wait_ge(info_in, 16)

                def take_hidden(b, p):
                    dve.wait_ge(s["h_turned"], b + 1)
                    since(dve, s["y_ready"], b)
                    nc.vector.tensor_copy(hT[:, :, :], hps[:, :, :]).then_inc(s["hT_ready"], 1)

                def weigh(b, p):
                    dve.wait_ge(s["y_ready"], b + 1)
                    since(dve, y_out[p], uses(b, p))
                    nc.vector.scalar_tensor_tensor(out=ys[:, p], in0=yps[:, :], scalar=info[:, bass.ds(b, 1), 1], in1=mod2[:, 3],
                                                   op0=ALU.mult, op1=ALU.mult).then_inc(s["ys_ready"], 1)

                def body(b, p):
                    if not is_first(b):
                        take_hidden(b - 1, 1 - p)
                    dve.wait_ge(s["up_ready"], b + 1)
                    dve.wait_ge(s["silu_ready"], b + 1)
                    since(dve, s["h_turned"], b - 1)
                    nc.vector.tensor_tensor(hid[:, p], ups[:, :], act_g[:, :], ALU.mult).then_inc(s["hid_ready"], 1)
                    if not is_first(b):
                        weigh(b - 1, 1 - p)

                blocks(body)(dve)
                take_hidden(NBK - 1, 1)
                weigh(NBK - 1, 1)


def combine(nc, K, dram, out):
    with ExitStack() as ctx:
        m = Memory(nc, ctx)
        slot = K["slot"]
        N = 4
        y = [m.sb(f"y{i}", [P, N, D]) for i in range(2)]
        h = m.sb("h_in", [P, N, D])
        y_in = [[m.sem(f"y_in{i}{n}") for n in range(N)] for i in range(2)]
        h_in = [m.sem(f"h_in{n}") for n in range(N)]
        o_out = [m.sem(f"o_out{n}") for n in range(N)]
        summed, added = m.sem("summed"), m.sem("added")
        with nc.Block() as block:

            @block.gpsimd
            def _(pool):
                for t in range(TT):
                    n = t % N
                    if t >= N:
                        pool.wait_ge(added, t - N + 1)
                    for i in range(2):
                        pool.indirect_dma_start(out=y[i][:, n], out_offset=None, in_=dram["ys"],
                                                in_offset=bass.IndirectOffsetOnAxis(ap=slot[:, i, t:t + 1], axis=0)).then_inc(y_in[i][n], 16)

            @block.scalar
            def _(act):
                for t in range(TT):
                    n = t % N
                    if t >= N:
                        act.wait_ge(o_out[n], 16 * (t // N))
                    act.dma_start(h[:, n], dram["h"][t * P:(t + 1) * P, :]).then_inc(h_in[n], 16)

            @block.vector
            def _(dve):
                for t in range(TT):
                    n = t % N
                    for i in range(2):
                        dve.wait_ge(y_in[i][n], 16 * (t // N + 1))
                    nc.vector.tensor_tensor(y[0][:, n], y[0][:, n], y[1][:, n], ALU.add).then_inc(summed, 1)
                    dve.wait_ge(summed, t + 1)
                    dve.wait_ge(h_in[n], 16 * (t // N + 1))
                    nc.vector.tensor_tensor(h[:, n], h[:, n], y[0][:, n], ALU.add).then_inc(added, 1)

            @block.sync
            def _(sp):
                for t in range(TT):
                    n = t % N
                    sp.wait_ge(added, t + 1)
                    sp.dma_start(out[0, t * P:(t + 1) * P, :], h[:, n]).then_inc(o_out[n], 16)
                for n in range(N):
                    sp.wait_ge(o_out[n], 16 * (TT // N))


def decoder_layer(nc, x, c, fox_w_in, fox_b_f, fox_q_gain, fox_k_gain, fox_w_out, norm_gain, ada_w, ada_b,
                  router_w, router_b, moe_w_gate, moe_w_up, moe_w_down, out):
    def scratch(name, shape, dt=F32):
        return nc.dram_tensor(name, shape, dt).ap()

    dram = {n: scratch("s_" + n, (PAIRS, P, S), F16) for n in ("q_hi", "q_lo", "k_hi", "k_lo")}
    dram |= {n: scratch("s_" + n, (H, ROWS, S), F16) for n in ("q_rows", "k_rows")}
    dram |= {n: scratch("s_" + n, (S, D)) for n in ("v", "h", "u2")}
    dram["ys"] = scratch("s_ys", (R, D))
    dram["info"] = scratch("s_info", (R, 2))
    with ExitStack() as ctx:
        m = Memory(nc, ctx)
        K = {n: m.sb(n, [P, P]) for n in ("ident", "ones", "upto", "before")}
        K |= {n: m.sb(n, [P, P], F16) for n in ("mask_rows", "big_ident")}
        K["eps"] = m.sb("eps", [P, 2])
        K["mod2"] = m.sb("mod2", [P, 4, D])
        with ExitStack() as inner:
            mi = Memory(nc, inner)
            K["u_hi"], K["u_lo"] = mi.sb("u_hi", [P, KT, S], F16), mi.sb("u_lo", [P, KT, S], F16)
            modulate(nc, x, c, norm_gain, ada_w, ada_b, K)
            project(nc, fox_w_in, fox_b_f, fox_q_gain, fox_k_gain, K, dram)
        K["score"] = m.sb("score", [P, TT, E])
        K["slot"] = m.sb("slot", [P, 2, TT], I32)
        K["ends"] = m.sb("ends", [P, E])
        K["table"] = m.sb("table", [P, 3, NBK], I32)
        with ExitStack() as inner:
            mi = Memory(nc, inner)
            K["o_hi"], K["o_lo"] = mi.sb("o_hi", [P, PAIRS, S], F16), mi.sb("o_lo", [P, PAIRS, S], F16)
            attend(nc, K, dram)
            merge(nc, x, fox_w_out, router_w, K, dram)
        route(nc, router_b, K, dram)
        experts(nc, moe_w_gate, moe_w_up, moe_w_down, K, dram)
        combine(nc, K, dram, out)


_INS = ['x', 'c', 'fox_w_in', 'fox_b_f', 'fox_q_gain', 'fox_k_gain', 'fox_w_out', 'norm_gain', 'ada_w', 'ada_b',
        'router_w', 'router_b', 'moe_w_gate', 'moe_w_up', 'moe_w_down']


def kernel(**inputs):
    import numpy as _np
    import concourse.bacc as _bacc
    from concourse import mybir as _mybir
    from concourse.bass_utils import run_bass_kernel_spmd as _run

    nc = _bacc.Bacc("TRN2", target_bir_lowering=False, num_devices=1)
    arrays, args = {}, []
    for name in _INS:
        a = _np.ascontiguousarray(inputs[name])
        arrays[f"in_{name}_dram"] = a
        args.append(nc.dram_tensor(f"in_{name}_dram", a.shape, _mybir.dt.from_np(a.dtype), kind="ExternalInput").ap())
    out = nc.dram_tensor("out_0_dram", (1, S, D), _mybir.dt.float32, kind="ExternalOutput").ap()
    decoder_layer(nc, *args, out)
    r = _run(nc, [arrays], core_ids=[0])
    return r.results[0]["out_0_dram"]
```

```python
from contextlib import ExitStack

import concourse.bass as bass
from concourse import mybir

F32 = mybir.dt.float32
F16 = mybir.dt.float16
I32 = mybir.dt.int32
ACT = mybir.ActivationFunctionType
ALU = mybir.AluOpType
AX = mybir.AxisListType

P = 128
D = 1024
KT = D // P
S = 2048
TT = S // P
H = 16
HD = 64
PAIRS = H // 2
CH = 512
QC = S // CH
TPC = CH // P
E = 16
G = 4
FF = 512
FT = FF // P
R = S * 2 + E * P
NBK = R // P
NBT = NBK + 3
EPS = 1e-6
WS = 32.0
CS = 16.0
ROWS = 5
BIG = 60000.0
FAR = 1e30
FROM = 1


class Memory:

    def __init__(self, nc, ctx):
        self.nc, self.ctx, self.sems = nc, ctx, []

    def sb(self, name, shape, dt=F32):
        return self.ctx.enter_context(self.nc.sbuf_tensor(name, shape, dt))

    def ps(self, name, shape, dt=F32):
        return self.ctx.enter_context(self.nc.psum_tensor(name, shape, dt))

    def sem(self, name, soft=False):
        if soft:
            return self.ctx.enter_context(self.nc.semaphore(name))
        self.sems.append(self.ctx.enter_context(self.nc.semaphore(name)))
        return self.sems[-1]

    def start_counts(self):
        with self.nc.Block(no_gpsimd_drain=True) as raising:
            @raising.sync
            def _(sp):
                for sem in self.sems:
                    sp.sem_inc(sem, FROM)


def one(ap, i):
    return ap[:, bass.ds(i, 1), :].rearrange("p a n -> p (a n)")


def since(eng, sem, value):
    if not isinstance(value, int) or value > 0:
        eng.wait_ge(sem, FROM + value)


def tile_cols(ap, t):
    return ap[:, bass.ds(t * P, P)]


def staggered(eng, lead, follow):
    lead(0, 0)
    with eng.Fori(0, TT // 4 - 1) as g:
        for p in range(4):
            lead(g * 4 + (p + 1), (p + 1) % 4)
            follow(g * 4 + p, p)
    for p in range(4):
        t = TT - 4 + p
        if p < 3:
            lead(t + 1, p + 1)
        follow(t, p)


def modulate(nc, x, c, norm_gain, ada_w, ada_b, K):
    with ExitStack() as ctx:
        m = Memory(nc, ctx)
        mod1 = m.sb("mod1", [P, 2, D])
        mod2 = K["mod2"]
        u_hi, u_lo, ident = K["u_hi"], K["u_lo"], K["ident"]
        gains = m.sb("gains", [P, 2, D])
        stage = m.sb("ada_stage", [P, 2, KT, CH])
        c8 = m.sb("c8", [KT, P])
        cond8 = m.sb("cond8", [KT, P])
        cond = m.sb("cond", [P, KT])
        condb = m.sb("condb", [P, KT, P])
        xt = m.sb("xt", [P, 4, D])
        ut = m.sb("ut", [P, 2, D])
        dump = m.sb("dump", [P, D])
        ssq = m.sb("ssq", [P, TT])
        root = m.sb("root", [P, TT])
        rstd = m.sb("rstd", [P, TT])
        mps = [m.ps(f"mps{i}", [P, CH]) for i in range(2)]
        tps = [m.ps(f"tps{i}", [P, KT, P]) for i in range(2)]

        c_in, b_in, gain_in = m.sem("c_in"), m.sem("b_in"), m.sem("gain_in")
        ada_in = [m.sem(f"ada_in{i}") for i in range(2)]
        x_in = [m.sem(f"x_in{i}") for i in range(4)]
        const0, const1 = m.sem("const0"), m.sem("const1")
        silu_done, cond_turned, condb_ready = m.sem("silu_done"), m.sem("cond_turned"), m.sem("condb_ready")
        mod_ps, mod_ready, mod_scaled = m.sem("mod_ps"), m.sem("mod_ready"), m.sem("mod_scaled")
        gain_ready = m.sem("gain_ready")
        root_ready = m.sem("root_ready")
        square_done, rstd_ready, u_scaled, u_ready = (m.sem(n) for n in ("square_done", "rstd_ready", "u_scaled", "u_ready"))
        u_turned, hi_ready, lo_ready = m.sem("u_turned"), m.sem("hi_ready"), m.sem("lo_ready")
        NADA = 6 * D // CH
        av = ada_w[0].rearrange("(k p) n -> p k n", p=P)

        def mod_chunk(i):
            n, half = divmod(i, 2)
            return (mod1[:, n] if n < 2 else mod2[:, n - 2])[:, half * CH:(half + 1) * CH]

        m.start_counts()
        with nc.Block() as block:

            @block.sync
            def _(sp):
                sp.dma_start(c8[:, :], c.rearrange("a (k p) -> (a k) p", p=P)).then_inc(c_in, 16)
                for i in range(2):
                    sp.dma_start(stage[:, i], av[:, :, i * CH:(i + 1) * CH]).then_inc(ada_in[i], 16)
                sp.dma_start(mod1[:, :, :].rearrange("p a n -> p (a n)"), ada_b[0, 0:2 * D].partition_broadcast(P)).then_inc(b_in, 16)
                sp.dma_start(mod2[:, :, :].rearrange("p a n -> p (a n)"), ada_b[0, 2 * D:].partition_broadcast(P)).then_inc(b_in, 16)
                sp.dma_start(gains[:, :, :], norm_gain[0].partition_broadcast(P)).then_inc(gain_in, 16)
                for i in range(2, NADA):
                    sp.wait_ge(mod_ps, FROM + i - 1)
                    sp.dma_start(stage[:, i % 2], av[:, :, i * CH:(i + 1) * CH]).then_inc(ada_in[i % 2], 16)

            @block.gpsimd
            def _(pool):
                nc.gpsimd.memset(K["ident"][:, :], 0.0).then_inc(const0, 1)
                nc.gpsimd.memset(K["ones"][:, :], 1.0).then_inc(const0, 1)
                nc.gpsimd.memset(K["upto"][:, :], 0.0).then_inc(const0, 1)
                nc.gpsimd.memset(K["before"][:, :], 0.0).then_inc(const0, 1)
                nc.gpsimd.memset(K["mask_rows"][:, :], 0.0).then_inc(const0, 1)
                nc.gpsimd.memset(K["big_ident"][:, :], 0.0).then_inc(const0, 1)
                nc.gpsimd.memset(K["eps"][:, 0:1], D * EPS).then_inc(const0, 1)
                nc.gpsimd.memset(K["eps"][:, 1:2], HD * WS * WS * EPS).then_inc(const0, 1)
                pool.wait_ge(const0, FROM + 8)

                def fill(buf, compare, value, base=0):
                    return nc.gpsimd.affine_select(out=buf[:, :], in_=buf[:, :], compare_op=compare, fill=value,
                                                   base=base, pattern=[[-1, P]], channel_multiplier=1).then_inc(const1, 1)

                fill(K["ident"], ALU.not_equal, 1.0)
                fill(K["upto"], ALU.is_gt, 1.0)
                fill(K["before"], ALU.is_ge, 1.0)
                fill(K["mask_rows"], ALU.is_ge, -BIG)
                fill(K["big_ident"], ALU.not_equal, BIG)
                pool.wait_ge(const1, FROM + 5)

            @block.scalar
            def _(act):
                act.wait_ge(c_in, FROM + 16)
                act.wait_ge(const0, FROM + 8)
                nc.scalar.activation(cond8[:, :], c8[:, :], ACT.Silu).then_inc(silu_done, 1)
                with act.Fori(0, TT // 4) as g:
                    for p in range(4):
                        act.wait_ge(u_scaled, FROM + g * 4)
                        act.dma_start(xt[:, p], x[0, bass.ds(g * 4 * P + p * P, P), :]).then_inc(x_in[p], 16)
                    for p in range(4):
                        act.wait_ge(x_in[p], FROM + g * 16 + 16)
                        act.wait_ge(square_done, FROM + g * 4 + p)
                        nc.scalar.activation(dump[:, :], xt[:, p], ACT.Square,
                                             accum_out=ssq[:, bass.ds(g * 4 + p, 1)]).then_inc(square_done, 1)
                        act.wait_ge(square_done, FROM + g * 4 + p + 1)
                        nc.scalar.activation(root[:, bass.ds(g * 4 + p, 1)], ssq[:, bass.ds(g * 4 + p, 1)], ACT.Sqrt, bias=K["eps"][:, 0:1]).then_inc(root_ready, 1)
                    for p in range(4):
                        t = g * 4 + p
                        act.wait_ge(u_turned, FROM + t + 1)
                        nc.scalar.activation(u_hi[:, :, bass.ds(t * P, P)], tps[p % 2][:, :, :], ACT.Copy).then_inc(hi_ready, 1)

            @block.tensor
            def _(pe):
                def mod(i, n):
                    since(pe, mod_ready, i - 1)
                    for k in range(KT):
                        mm = nc.tensor.matmul(mps[n][:, :], condb[:, k], stage[:, n, k], start=(k == 0), stop=(k == KT - 1))
                    mm.then_inc(mod_ps, 1)

                pe.wait_ge(const1, FROM + 5)
                pe.wait_ge(silu_done, FROM + 1)
                nc.tensor.transpose(mps[0][:, 0:KT], cond8[:, :], ident[0:KT, 0:KT]).then_inc(cond_turned, 1)
                pe.wait_ge(condb_ready, FROM + KT + 2)
                for i in range(4):
                    pe.wait_ge(ada_in[i % 2], FROM + 16 * (i // 2 + 1))
                    mod(i, i % 2)
                with pe.Fori(0, TT // 4) as g:
                    for p in range(4):
                        t = g * 4 + p
                        pe.wait_ge(u_ready, FROM + t + 1)
                        if p < 2:
                            pe.wait_ge(lo_ready, FROM + g * 4)
                        else:
                            pe.wait_ge(lo_ready, FROM + t - 1)
                        for k in range(KT):
                            mm = nc.tensor.transpose(tps[p % 2][:, k], ut[:, p % 2, k * P:(k + 1) * P], ident[:, :])
                        mm.then_inc(u_turned, 1)
                        if p % 2:
                            n = p // 2
                            pe.wait_ge(ada_in[n], FROM + g * 16 + 48)
                            mod(g * 2 + 4 + n, n)

            @block.vector
            def _(dve):
                nc.vector.memset(condb[:, :, :], 1.0).then_inc(condb_ready, 1)
                dve.wait_ge(condb_ready, FROM + 1)
                dve.wait_ge(cond_turned, FROM + 1)
                nc.vector.tensor_copy(cond[:, :], mps[0][:, 0:KT]).then_inc(condb_ready, 1)
                dve.wait_ge(condb_ready, FROM + 2)
                for k in range(KT):
                    nc.vector.tensor_scalar(condb[:, k], condb[:, k], cond[:, k:k + 1], None, ALU.mult).then_inc(condb_ready, 1)
                dve.wait_ge(gain_in, FROM + 16)
                nc.vector.tensor_scalar(gains[:, :, :], gains[:, :, :], float(D) ** 0.5, None, ALU.mult).then_inc(gain_ready, 1)
                dve.wait_ge(b_in, FROM + 32)

                def add_mod(i, n, out):
                    dve.wait_ge(mod_ps, FROM + i + 1)
                    nc.vector.tensor_tensor(out, out, mps[n][:, :], ALU.add).then_inc(mod_ready, 1)

                for i in range(4):
                    add_mod(i, i % 2, mod_chunk(i))
                dve.wait_ge(mod_ready, FROM + 4)
                dve.wait_ge(gain_ready, FROM + 1)
                nc.vector.scalar_tensor_tensor(out=mod1[:, 1], in0=mod1[:, 1], scalar=1.0, in1=gains[:, 0],
                                               op0=ALU.add, op1=ALU.mult).then_inc(mod_scaled, 1)
                dve.wait_ge(mod_scaled, FROM + 1)

                def lo(t, p):
                    dve.wait_ge(hi_ready, FROM + t + 1)
                    cols = bass.ds(t * P, P)
                    nc.vector.tensor_tensor(u_lo[:, :, cols], tps[p % 2][:, :, :], u_hi[:, :, cols], ALU.subtract).then_inc(lo_ready, 1)

                with dve.Fori(0, TT // 4) as g:
                    for p in range(4):
                        t = g * 4 + p
                        dve.wait_ge(root_ready, FROM + t + 1)
                        nc.vector.reciprocal(rstd[:, bass.ds(t, 1)], root[:, bass.ds(t, 1)]).then_inc(rstd_ready, 1)
                        dve.wait_ge(rstd_ready, FROM + t + 1)
                        if p < 2:
                            dve.wait_ge(u_turned, FROM + g * 4)
                        else:
                            dve.wait_ge(u_turned, FROM + t - 1)
                        nc.vector.scalar_tensor_tensor(out=ut[:, p % 2], in0=xt[:, p], scalar=rstd[:, bass.ds(t, 1)],
                                                       in1=mod1[:, 1], op0=ALU.mult, op1=ALU.mult).then_inc(u_scaled, 1)
                        dve.wait_ge(u_scaled, FROM + t + 1)
                        nc.vector.tensor_tensor(ut[:, p % 2], ut[:, p % 2], mod1[:, 0], ALU.add).then_inc(u_ready, 1)
                        if p:
                            lo(t - 1, p - 1)
                    lo(g * 4 + 3, 3)
                    m2 = mod2[:, :, :].rearrange("p a n -> p (a n)")
                    for n in range(2):
                        add_mod(g * 2 + 4 + n, n, m2[:, bass.ds(g * 2 * CH + n * CH, CH)])
                dve.wait_ge(mod_ready, FROM + NADA)
                nc.vector.scalar_tensor_tensor(out=mod2[:, 2], in0=mod2[:, 2], scalar=1.0, in1=gains[:, 1],
                                               op0=ALU.add, op1=ALU.mult).then_inc(mod_scaled, 1)
                nc.vector.tensor_scalar(mod2[:, 0], mod2[:, 0], 1.0 / WS, None, ALU.mult).then_inc(mod_scaled, 1)
                nc.vector.tensor_scalar(mod2[:, 3], mod2[:, 3], 1.0 / WS, None, ALU.mult).then_inc(mod_scaled, 1)
                dve.wait_ge(mod_scaled, FROM + 4)


def project(nc, w_in, b_f, q_gain, k_gain, K, dram):
    with ExitStack() as ctx:
        m = Memory(nc, ctx)
        u_hi, u_lo, ident = K["u_hi"], K["u_lo"], K["ident"]
        HK = KT // 2
        stage = m.sb("w_stage", [P, 2, HK, CH])
        w_hi = m.sb("w_hi", [P, 2, KT, CH], F16)
        w_lo = m.sb("w_lo", [P, 2, KT, CH], F16)
        t_hi = m.sb("t_hi", [P, 4, S], F16)
        t_lo = m.sb("t_lo", [P, 4, S], F16)
        vt = m.sb("vt", [P, 4, CH])
        sq = m.sb("sq", [P, 2, CH])
        qn = m.sb("qn", [P, 2, CH])
        hss = m.sb("hss", [P, 2, 8])
        hrt = m.sb("hrt", [P, 2, 8])
        hrs = m.sb("hrs", [P, 2, 8])
        wf = m.sb("wf", [P, KT, H])
        wf_hi = m.sb("wf_hi", [P, KT, H], F16)
        wf_lo = m.sb("wf_lo", [P, KT, H], F16)
        bfb = m.sb("bfb", [P, H])
        z = m.sb("z", [P, TT, H])
        za = m.sb("za", [P, TT, H])
        cum = m.sb("cum", [P, TT, H])
        gqk = m.sb("gqk", [P, 2])
        grow = m.sb("grow", [H, 2, HD])
        bound = m.sb("bound", [H, 2])
        cumT = m.sb("cumT", [H, S])
        rem = m.sb("rem", [H, 2, CH])
        krow = m.sb("krow", [H, ROWS, CH], F16)
        qrow = m.sb("qrow", [H, ROWS, CH], F16)
        acc = [m.ps(f"acc{i}", [P, CH]) for i in range(2)]
        qps = [m.ps(f"qps{i}", [P, 4, P]) for i in range(2)]
        cps = [m.ps(f"cps{i}", [P, CH]) for i in range(4)]

        def sems(*names):
            return [m.sem(n) for n in names]

        w_in_sem = sems("w_in0", "w_in1")
        wf_in, gain_in, wf_parts, f_ps, z_ready, f_act = sems("wf_in", "gain_in", "wf_parts", "f_ps", "z_ready", "f_act")
        w_hi_ready, w_lo_ready = sems("w_hi_ready", "w_lo_ready")
        acc_ready, sq_ready, hss_ready, hrs_ready, qn_ready = sems("acc_ready", "sq_ready", "hss_ready", "hrs_ready", "qn_ready")
        turned, th_ready, tl_ready, t_out = sems("turned", "th_ready", "tl_ready", "t_out")
        v_ready, hrt_ready = sems("v_ready", "hrt_ready")
        v_out = sems(*[f"v_out{i}" for i in range(4)])
        cum_ps, cum_ready, cumT_ps, cumT_ready = sems("cum_ps", "cum_ready", "cumT_ps", "cumT_ready")
        gains_ready, row_step = sems("gains_ready", "row_step")
        row_out = m.sem("row_out", soft=True)
        NQK, NCH = 4, 6
        wv = w_in[0].rearrange("(k p) n -> p k n", p=P)

        m.start_counts()
        with nc.Block() as block:

            @block.sync
            def _(sp):
                def load(j):
                    for h in range(2):
                        if j:
                            sp.wait_ge(w_hi_ready, FROM + 2 * j - 1 + h)
                            sp.wait_ge(w_lo_ready, FROM + 2 * j - 1 + h)
                        sp.dma_start(stage[:, h], wv[:, h * HK:(h + 1) * HK, j * CH:(j + 1) * CH]).then_inc(w_in_sem[h], 16)

                load(0)
                load(1)
                for j in range(NQK):
                    to = (dram["q_hi"], dram["q_lo"]) if j < 2 else (dram["k_hi"], dram["k_lo"])
                    first = 4 * (j % 2)
                    for g in range(QC):
                        cols = slice(g * CH, (g + 1) * CH)
                        sp.wait_ge(th_ready, FROM + j * TT + 4 * g + 4)
                        sp.dma_start(to[0][first:first + 4, :, cols].rearrange("a p n -> p a n"), t_hi[:, :, cols]).then_inc(t_out, 16)
                        sp.wait_ge(tl_ready, FROM + j * TT + 4 * g + 4)
                        sp.dma_start(to[1][first:first + 4, :, cols].rearrange("a p n -> p a n"), t_lo[:, :, cols]).then_inc(t_out, 16)
                    if j + 2 < NCH:
                        load(j + 2)
                sp.wait_ge(t_out, FROM + 16 * 2 * QC * NQK)

            @block.gpsimd
            def _(pool):
                nc.gpsimd.memset(krow[:, :, :], CS).then_inc(row_step, 1)
                nc.gpsimd.memset(qrow[:, :, :], CS).then_inc(row_step, 1)
                pool.wait_ge(gains_ready, FROM + 4)
                pool.wait_ge(row_step, FROM + 2)
                n = 2
                for g in range(QC):
                    cs = cumT[:, g * CH:(g + 1) * CH]
                    pool.wait_ge(cumT_ready, FROM + g + 1)
                    if g:
                        pool.wait_ge(row_out, 32 * g)
                    nc.gpsimd.tensor_scalar(krow[:, 2], cs, -1.0 / CS, None, ALU.mult).then_inc(row_step, 1)
                    nc.gpsimd.tensor_scalar(rem[:, 0], cs, -1.0 / CS, None, ALU.mult).then_inc(row_step, 1)
                    pool.wait_ge(row_step, FROM + n + 2)
                    nc.gpsimd.tensor_tensor(rem[:, 0], rem[:, 0], krow[:, 2], ALU.subtract).then_inc(row_step, 1)
                    pool.wait_ge(row_step, FROM + n + 3)
                    nc.gpsimd.tensor_copy(krow[:, 3], rem[:, 0]).then_inc(row_step, 1)
                    pool.wait_ge(row_step, FROM + n + 4)
                    nc.gpsimd.tensor_tensor(krow[:, 4], rem[:, 0], krow[:, 3], ALU.subtract).then_inc(row_step, 1)
                    nc.gpsimd.tensor_scalar(rem[:, 1], cs, bound[:, 1:2], 1.0 / CS, ALU.subtract, ALU.mult).then_inc(row_step, 1)
                    pool.wait_ge(row_step, FROM + n + 6)
                    nc.gpsimd.tensor_copy(qrow[:, 0], rem[:, 1]).then_inc(row_step, 1)
                    pool.wait_ge(row_step, FROM + n + 7)
                    nc.gpsimd.tensor_tensor(qrow[:, 1], rem[:, 1], qrow[:, 0], ALU.subtract).then_inc(row_step, 1)
                    n += 8
                    pool.wait_ge(row_step, FROM + n)
                    pool.dma_start(dram["k_rows"][:, :, g * CH:(g + 1) * CH], krow[:, :, :]).then_inc(row_out, 16)
                    pool.dma_start(dram["q_rows"][:, :, g * CH:(g + 1) * CH], qrow[:, :, :]).then_inc(row_out, 16)
                pool.wait_ge(row_out, 32 * QC)

            @block.scalar
            def _(act):
                act.dma_start(grow[:, 0], q_gain[0].partition_broadcast(H)).then_inc(gain_in, 16)
                act.dma_start(grow[:, 1], k_gain[0].partition_broadcast(H)).then_inc(gain_in, 16)
                for half in range(2):
                    rows = slice(half * HD, (half + 1) * HD)
                    act.dma_start(gqk[rows, 0:1], q_gain[0].rearrange("(p a) -> p a", a=1)).then_inc(gain_in, 16)
                    act.dma_start(gqk[rows, 1:2], k_gain[0].rearrange("(p a) -> p a", a=1)).then_inc(gain_in, 16)
                act.dma_start(wf[:, :, :], wv[:, :, 3 * D:3 * D + H]).then_inc(wf_in, 16)
                act.dma_start(bfb[:, :], b_f[0].partition_broadcast(P)).then_inc(wf_in, 16)
                act.wait_ge(wf_in, FROM + 32)
                nc.scalar.activation(wf_hi[:, :, :], wf[:, :, :], ACT.Copy, scale=WS).then_inc(wf_parts, 1)

                def hi(j):
                    if j >= 2:
                        act.wait_ge(acc_ready, FROM + (j - 1) * TT)
                    for h in range(2):
                        act.wait_ge(w_in_sem[h], FROM + 16 * (j + 1))
                        nc.scalar.activation(w_hi[:, j % 2, h * HK:(h + 1) * HK], stage[:, h], ACT.Copy, scale=WS).then_inc(w_hi_ready, 1)

                hi(0)
                act.wait_ge(z_ready, FROM + 2)
                nc.scalar.activation(za[:, :, :], za[:, :, :], ACT.Exp, scale=-1.0).then_inc(f_act, 1)
                act.wait_ge(f_act, FROM + 1)
                nc.scalar.activation(za[:, :, :], za[:, :, :], ACT.Ln, bias=1.0).then_inc(f_act, 1)
                hi(1)
                act.wait_ge(gains_ready, FROM + 1)
                for j in range(NQK):
                    base = j * TT

                    def square(t, p):
                        act.wait_ge(acc_ready, FROM + t + (base + 1))
                        since(act, hss_ready, t + (base - 1))
                        nc.scalar.activation(sq[:, p % 2], acc[p % 2][:, :], ACT.Square).then_inc(sq_ready, 1)
                        act.wait_ge(hss_ready, FROM + t + (base + 1))
                        nc.scalar.activation(hrt[:, p % 2], hss[:, p % 2], ACT.Sqrt, bias=K["eps"][:, 1:2]).then_inc(hrt_ready, 1)

                    def turn_hi(t, p):
                        act.wait_ge(turned, FROM + t + (base + 1))
                        scale = gqk[:, 0:1] if j < 2 else 8.0
                        nc.scalar.activation(t_hi[:, :, bass.ds(t * P, P)], qps[p % 2][:, :, :], ACT.Copy, scale=scale).then_inc(th_ready, 1)

                    since(act, t_out, 32 * QC * j)
                    staggered(act, square, turn_hi)
                    if j + 2 < NCH:
                        hi(j + 2)
                for j in range(NCH - NQK):
                    with act.Fori(0, TT // 4) as g:
                        for p in range(4):
                            act.wait_ge(acc_ready, FROM + g * 4 + ((NQK + j) * TT + p + 1))
                            act.wait_ge(v_out[p], FROM + g * 16 + 64 * j)
                            nc.scalar.activation(vt[:, p], acc[p % 2][:, :], ACT.Copy, scale=1.0 / WS).then_inc(v_ready, 1)
                            act.wait_ge(v_ready, FROM + g * 4 + (j * TT + p + 1))
                            act.dma_start(dram["v"][bass.ds(g * 4 * P + p * P, P), j * CH:(j + 1) * CH], vt[:, p]).then_inc(v_out[p], 16)
                for p in range(4):
                    act.wait_ge(v_out[p], FROM + 128)

            @block.tensor
            def _(pe):
                pe.wait_ge(wf_parts, FROM + 2)
                fz = cps[0][:, 0:TT * H].rearrange("p (t h) -> p t h", h=H)
                with pe.Fori(0, TT) as t:
                    n = 0
                    for a, b in ((u_hi, wf_hi), (u_hi, wf_lo), (u_lo, wf_hi)):
                        for k in range(KT):
                            mm = nc.tensor.matmul(one(fz, t), tile_cols(a[:, k], t), b[:, k], start=(n == 0), stop=(n == 3 * KT - 1))
                            n += 1
                    mm.then_inc(f_ps, 1)

                for j in range(NCH):
                    base = j * TT
                    pe.wait_ge(w_hi_ready, FROM + 2 * j + 2)
                    pe.wait_ge(w_lo_ready, FROM + 2 * j + 2)

                    def product(t, p):
                        since(pe, qn_ready, t + (base - 1))
                        n = 0
                        for a, b in ((u_hi, w_hi), (u_hi, w_lo), (u_lo, w_hi)):
                            for k in range(KT):
                                mm = nc.tensor.matmul(acc[p % 2][:, :], tile_cols(a[:, k], t), b[:, j % 2, k],
                                                      start=(n == 0), stop=(n == 3 * KT - 1))
                                n += 1
                        mm.then_inc(acc_ready, 1)

                    def turn(t, p):
                        pe.wait_ge(qn_ready, FROM + t + (base + 1))
                        since(pe, tl_ready, t + base)
                        for a in range(4):
                            mm = nc.tensor.transpose(qps[p % 2][:, a], qn[:, p % 2, a * P:(a + 1) * P], ident[:, :])
                        mm.then_inc(turned, 1)

                    if j < NQK:
                        staggered(pe, product, turn)
                    else:
                        jv = j - NQK
                        with pe.Fori(0, TT // 4) as g:
                            for p in range(4):
                                if p < 2 and jv == 0:
                                    pe.wait_ge(qn_ready, FROM + NQK * TT)
                                    pe.wait_ge(v_ready, FROM + g * 4)
                                else:
                                    pe.wait_ge(v_ready, FROM + g * 4 + (jv * TT + p - 1))
                                n = 0
                                for a, b in ((u_hi, w_hi), (u_hi, w_lo), (u_lo, w_hi)):
                                    for k in range(KT):
                                        mm = nc.tensor.matmul(acc[p % 2][:, :], tile_cols(a[:, k], g * 4 + p), b[:, j % 2, k],
                                                              start=(n == 0), stop=(n == 3 * KT - 1))
                                        n += 1
                                mm.then_inc(acc_ready, 1)
                    if j == 0:
                        pe.wait_ge(z_ready, FROM + 4)
                        cz = cps[1][:, 0:TT * H].rearrange("p (t h) -> p t h", h=H)
                        for t in range(TT - 1):
                            rest = TT - 1 - t
                            nc.tensor.matmul(cz[:, t + 1:TT], K["ones"][:, :], z[:, t:t + 1].broadcast_to([P, rest, H]),
                                             start=(t == 0), stop=False, skip_group_check=True)
                        nc.tensor.matmul(cz, K["upto"][:, :], z[:, :, :], start=False, stop=True,
                                         skip_group_check=True).then_inc(cum_ps, 1)
                    if j == 1:
                        pe.wait_ge(cum_ready, FROM + 1)
                        for g in range(QC):
                            for i in range(TPC):
                                mm = nc.tensor.transpose(cps[g][0:H, i * P:(i + 1) * P], cum[:, g * TPC + i], ident[:, :])
                            mm.then_inc(cumT_ps, 1)

            @block.vector
            def _(dve):
                dve.wait_ge(wf_parts, FROM + 1)
                nc.vector.scalar_tensor_tensor(out=wf_lo[:, :, :], in0=wf[:, :, :], scalar=WS, in1=wf_hi[:, :, :],
                                               op0=ALU.mult, op1=ALU.subtract).then_inc(wf_parts, 1)
                dve.wait_ge(gain_in, FROM + 96)
                nc.vector.tensor_tensor(gqk[:, 0:1], gqk[:, 0:1], gqk[:, 1:2], ALU.mult).then_inc(gains_ready, 1)
                nc.vector.tensor_tensor(grow[:, 0], grow[:, 0], grow[:, 1], ALU.mult).then_inc(gains_ready, 1)
                dve.wait_ge(gains_ready, FROM + 2)
                nc.vector.tensor_reduce(bound[:, 0:1], grow[:, 0], AX.X, ALU.max, apply_absolute_value=True).then_inc(gains_ready, 1)
                dve.wait_ge(gains_ready, FROM + 3)
                nc.vector.tensor_scalar(bound[:, 1:2], bound[:, 0:1], float(HD) ** 0.5, None, ALU.mult).then_inc(gains_ready, 1)

                def lo(j):
                    for h in range(2):
                        dve.wait_ge(w_hi_ready, FROM + 2 * j + h + 1)
                        ks = slice(h * HK, (h + 1) * HK)
                        nc.vector.scalar_tensor_tensor(out=w_lo[:, j % 2, ks], in0=stage[:, h], scalar=WS, in1=w_hi[:, j % 2, ks],
                                                       op0=ALU.mult, op1=ALU.subtract).then_inc(w_lo_ready, 1)

                lo(0)
                dve.wait_ge(f_ps, FROM + TT)
                dve.wait_ge(wf_in, FROM + 32)
                fz = cps[0][:, 0:TT * H].rearrange("p (t h) -> p t h", h=H)
                bias = bfb[:, :].rearrange("p (a h) -> p a h", a=1).broadcast_to([P, TT, H])
                nc.vector.scalar_tensor_tensor(out=z[:, :, :], in0=fz, scalar=1.0 / WS, in1=bias,
                                               op0=ALU.mult, op1=ALU.add).then_inc(z_ready, 1)
                dve.wait_ge(z_ready, FROM + 1)
                nc.vector.scalar_tensor_tensor(out=za[:, :, :], in0=z[:, :, :], scalar=-1.0, in1=z[:, :, :],
                                               op0=ALU.mult, op1=ALU.max).then_inc(z_ready, 1)
                dve.wait_ge(z_ready, FROM + 2)
                nc.vector.tensor_scalar(z[:, :, :], z[:, :, :], 0.0, None, ALU.min).then_inc(z_ready, 1)
                dve.wait_ge(z_ready, FROM + 3)
                dve.wait_ge(f_act, FROM + 2)
                nc.vector.tensor_tensor(z[:, :, :], z[:, :, :], za[:, :, :], ALU.subtract).then_inc(z_ready, 1)
                lo(1)
                for j in range(NQK):
                    base = j * TT

                    def norm(t, p):
                        i = p % 2
                        dve.wait_ge(sq_ready, FROM + t + (base + 1))
                        nc.vector.tensor_reduce(hss[:, i], sq[:, i].rearrange("p (h d) -> p h d", d=HD), AX.X, ALU.add).then_inc(hss_ready, 1)
                        dve.wait_ge(hrt_ready, FROM + t + (base + 1))
                        nc.vector.reciprocal(hrs[:, i], hrt[:, i]).then_inc(hrs_ready, 1)
                        dve.wait_ge(hrs_ready, FROM + t + (base + 1))
                        since(dve, turned, t + (base - 1))
                        r = hrs[:, i].rearrange("p (h a) -> p h a", a=1).broadcast_to([P, 8, HD])
                        nc.vector.tensor_tensor(qn[:, i].rearrange("p (h d) -> p h d", d=HD),
                                                acc[i][:, :].rearrange("p (h d) -> p h d", d=HD), r, ALU.mult).then_inc(qn_ready, 1)

                    def turn_lo(t, p):
                        dve.wait_ge(th_ready, FROM + t + (base + 1))
                        scale = gqk[:, 0:1] if j < 2 else 8.0
                        cols = bass.ds(t * P, P)
                        nc.vector.scalar_tensor_tensor(out=t_lo[:, :, cols], in0=qps[p % 2][:, :, :], scalar=scale, in1=t_hi[:, :, cols],
                                                       op0=ALU.mult, op1=ALU.subtract).then_inc(tl_ready, 1)

                    staggered(dve, norm, turn_lo)
                    if j + 2 < NCH:
                        lo(j + 2)
                    if j == 0:
                        dve.wait_ge(cum_ps, FROM + 1)
                        nc.vector.tensor_copy(cum[:, :, :], cps[1][:, 0:TT * H].rearrange("p (t h) -> p t h", h=H)).then_inc(cum_ready, 1)
                    if j == 1:
                        for g in range(QC):
                            dve.wait_ge(cumT_ps, FROM + g + 1)
                            nc.vector.tensor_copy(cumT[:, g * CH:(g + 1) * CH], cps[g][0:H, :]).then_inc(cumT_ready, 1)


def attend(nc, K, dram):
    with ExitStack() as ctx:
        m = Memory(nc, ctx)
        o_hi, o_lo = K["o_hi"], K["o_lo"]
        kA, kB, qA, qB = ([m.sb(f"{n}{i}", [P, 2, S], F16) for i in range(2)] for n in ("kA", "kB", "qA", "qB"))
        v = [m.sb(f"v{i}", [P, TT, P]) for i in range(2)]
        NPROB = 3
        prob = [m.sb(f"prob{i}", [P, 2, CH]) for i in range(NPROB)]
        den = [m.sb(f"den{i}", [P, 2, CH]) for i in range(2)]
        rden = m.sb("rden", [P, CH])
        o32 = m.sb("o32", [P, CH])
        sps = [m.ps(f"sps{i}", [P, 2, CH]) for i in range(2)]
        ops = [m.ps(f"ops{i}", [P, CH]) for i in range(2)]
        dps = m.ps("dps", [P, CH])
        heads_in = [m.sem(f"heads_in{i}") for i in range(2)]
        s_ready, p_ready, pv_done, den_step, den_bc = (m.sem(n) for n in ("s_ready", "p_ready", "pv_done", "den_step", "den_bc"))
        r_ready, o_ready, oh_ready, ol_ready = (m.sem(n) for n in ("r_ready", "o_ready", "oh_ready", "ol_ready"))
        steps = [(qc, j) for qc in range(QC) for j in range(TPC * (qc + 1))]
        NS = len(steps)
        last_of = {qc: max(i for i, st in enumerate(steps) if st[0] == qc) for qc in range(QC)}
        LOADS = 2 * 8 + 1
        ROWSL = slice(HD, HD + ROWS)
        CK = HD + ROWS

        def left(i):
            qc, j = steps[i]
            return max(0, j - TPC * qc) * P

        m.start_counts()
        with nc.Block() as block:

            @block.sync
            def _(sp):
                def load(pair, sl):
                    for a in range(2):
                        rows = slice(a * HD, (a + 1) * HD)

                        def pair_rows(t):
                            return dram[t][bass.ds(pair, 1), rows, :].rearrange("a p n -> p (a n)")

                        def head_rows(t):
                            return dram[t][bass.ds(pair * 2 + a, 1), :, :].rearrange("a p n -> p (a n)")

                        for to, part in ((kA[sl][0:HD, a], pair_rows("k_hi")), (kA[sl][HD:P, a], pair_rows("k_lo")),
                                         (kB[sl][0:HD, a], pair_rows("k_hi")), (kB[sl][ROWSL, a], head_rows("k_rows")),
                                         (qA[sl][0:HD, a], pair_rows("q_hi")), (qA[sl][HD:P, a], pair_rows("q_hi")),
                                         (qB[sl][0:HD, a], pair_rows("q_lo")), (qB[sl][ROWSL, a], head_rows("q_rows"))):
                            sp.dma_start(to, part).then_inc(heads_in[sl], 16)
                    sp.dma_start(v[sl][:, :, :], dram["v"].rearrange("(t p) n -> p t n", p=P)[:, :, bass.ds(pair * P, P)]).then_inc(heads_in[sl], 16)

                load(0, 0)
                load(1, 1)
                with sp.Fori(1, PAIRS // 2) as g:
                    for sl in range(2):
                        pair = sp.snap(g * 2 + sl)
                        sp.wait_ge(pv_done, FROM + g * 2 * NS + (sl - 1) * NS)
                        load(pair, sl)

            @block.tensor
            def _(pe):
                with pe.Fori(0, PAIRS // 2) as g:
                    for sl in range(2):
                        step0 = g * 2 * NS + sl * NS
                        chunk0 = g * 2 * QC + sl * QC

                        def scores(i):
                            qc, j = steps[i]
                            w0 = left(i)
                            ks, qs = slice(j * P, (j + 1) * P), slice(qc * CH + w0, (qc + 1) * CH)
                            if i >= 2 or sl:
                                pe.wait_ge(p_ready, FROM + step0 + (i - 1))
                            elif i == 0:
                                pe.wait_ge(p_ready, FROM + step0)
                            for a in range(2):
                                out = sps[i % 2][:, a, w0:CH]
                                diag = j >= TPC * qc
                                nc.tensor.matmul(out, kA[sl][:, a, ks], qA[sl][:, a, qs], start=True, stop=False)
                                if diag:
                                    nc.tensor.matmul(sps[i % 2][:, a, w0:w0 + P], K["mask_rows"][:, :], K["big_ident"][:, :],
                                                     start=False, stop=False, skip_group_check=True)
                                mm = nc.tensor.matmul(out, kB[sl][0:CK, a, ks], qB[sl][0:CK, a, qs], start=False, stop=True)
                            mm.then_inc(s_ready, 1)

                        def weigh(i):
                            qc, j = steps[i]
                            w0 = left(i)
                            pe.wait_ge(p_ready, FROM + step0 + (i + 1))
                            if j == 0:
                                if qc >= 1 or sl:
                                    pe.wait_ge(o_ready, FROM + chunk0 + (qc - 1))
                                else:
                                    pe.wait_ge(o_ready, FROM + chunk0)
                            for a in range(2):
                                rows = slice(a * HD, (a + 1) * HD)
                                mm = nc.tensor.matmul(ops[qc % 2][rows, w0:CH], v[sl][:, j, rows], prob[(i + sl * NS) % NPROB][:, a, w0:CH],
                                                      start=(j == 0), stop=(i == last_of[qc]), skip_group_check=True)
                            mm.then_inc(pv_done, 1)

                        def denominators(qc):
                            pe.wait_ge(den_step, FROM + step0 + (last_of[qc] + 1))
                            pe.wait_ge(r_ready, FROM + chunk0 + qc)
                            for a in range(2):
                                rows = slice(a * HD, (a + 1) * HD)
                                mm = nc.tensor.matmul(dps[rows, :], K["ones"][:, 0:HD], den[qc % 2][:, a], start=True, stop=True, skip_group_check=True)
                            mm.then_inc(den_bc, 1)

                        pe.wait_ge(heads_in[sl], FROM + g * 16 * LOADS + 16 * LOADS)
                        scores(0)
                        for i in range(NS):
                            if i + 1 < NS:
                                scores(i + 1)
                            weigh(i)
                            qc, j = steps[i]
                            if j == 1 and qc:
                                denominators(qc - 1)
                        denominators(QC - 1)

            @block.scalar
            def _(act):
                with act.Fori(0, PAIRS // 2) as g:
                    for sl in range(2):
                        step0 = g * 2 * NS + sl * NS
                        for i in range(NS):
                            w0 = left(i)
                            act.wait_ge(s_ready, FROM + step0 + (i + 1))
                            back = i - NPROB + 1
                            if back >= 0 or sl:
                                act.wait_ge(pv_done, FROM + step0 + back)
                                act.wait_ge(den_step, FROM + step0 + back)
                            else:
                                act.wait_ge(pv_done, FROM + step0)
                                act.wait_ge(den_step, FROM + step0)
                            nc.scalar.activation(prob[(i + sl * NS) % NPROB][:, :, w0:CH], sps[i % 2][:, :, w0:CH], ACT.Exp).then_inc(p_ready, 1)

            @block.vector
            def _(dve):
                with dve.Fori(0, PAIRS // 2) as g:
                    for sl in range(2):
                        step0 = g * 2 * NS + sl * NS
                        chunk0 = g * 2 * QC + sl * QC

                        def divide(qc):
                            pair = g * 2 + sl
                            n = chunk0 + (qc + 1)
                            dve.wait_ge(den_bc, FROM + n)
                            nc.vector.reciprocal(rden[:, :], dps[:, :]).then_inc(r_ready, 1)
                            dve.wait_ge(r_ready, FROM + n)
                            dve.wait_ge(pv_done, FROM + step0 + (last_of[qc] + 1))
                            nc.vector.tensor_tensor(o32[:, :], ops[qc % 2][:, :], rden[:, :], ALU.mult).then_inc(o_ready, 1)
                            dve.wait_ge(o_ready, FROM + n)
                            oh = one(o_hi, pair)[:, qc * CH:(qc + 1) * CH]
                            ol = one(o_lo, pair)[:, qc * CH:(qc + 1) * CH]
                            nc.vector.tensor_copy(oh, o32[:, :]).then_inc(oh_ready, 1)
                            dve.wait_ge(oh_ready, FROM + n)
                            nc.vector.tensor_tensor(ol, o32[:, :], oh, ALU.subtract).then_inc(ol_ready, 1)

                        for i in range(NS):
                            qc, j = steps[i]
                            w0 = left(i)
                            d = den[qc % 2][:, :, w0:CH]
                            pr = prob[(i + sl * NS) % NPROB][:, :, w0:CH]
                            dve.wait_ge(p_ready, FROM + step0 + (i + 1))
                            if j == 0:
                                if qc >= 1 or sl:
                                    dve.wait_ge(den_bc, FROM + chunk0 + (qc - 1))
                                else:
                                    dve.wait_ge(den_bc, FROM + chunk0)
                                nc.vector.tensor_copy(d, pr).then_inc(den_step, 1)
                            else:
                                dve.wait_ge(den_step, FROM + step0 + i)
                                nc.vector.tensor_tensor(d, d, pr, ALU.add).then_inc(den_step, 1)
                            if j == 2 and qc:
                                divide(qc - 1)
                        divide(QC - 1)
                dve.wait_ge(ol_ready, FROM + PAIRS * QC)


def merge(nc, x, w_out, router_w, K, dram):
    with ExitStack() as ctx:
        m = Memory(nc, ctx)
        o_hi, o_lo, mod2, ident, score = K["o_hi"], K["o_lo"], K["mod2"], K["ident"], K["score"]
        stage = m.sb("wo_stage", [P, 4, D])
        w_hi = m.sb("wo_hi", [P, PAIRS, D], F16)
        w_lo = m.sb("wo_lo", [P, PAIRS, D], F16)
        rw = m.sb("rw", [P, KT, E])
        xt = m.sb("xt2", [P, 2, D])
        ht = m.sb("ht", [P, 2, D])
        ut = m.sb("ut2", [P, 2, D])
        uT = m.sb("uT", [P, KT, P])
        dump = m.sb("dump2", [P, D])
        ssq = m.sb("ssq2", [P, TT])
        root = m.sb("root2", [P, TT])
        rstd = m.sb("rstd2", [P, TT])
        yps = [m.ps(f"yps{i}", [P, D]) for i in range(2)]
        tps = m.ps("tps2", [P, KT, P])
        rps = m.ps("rps", [P, 2, E])
        wo_in, rw_in = m.sem("wo_in"), m.sem("rw_in")
        x_in = [m.sem(f"x_in{i}b") for i in range(2)]
        h_out = [m.sem(f"h_out{i}") for i in range(2)]
        u_out = [m.sem(f"u_out{i}") for i in range(2)]
        names = "wo_hi_ready wo_lo_ready y_ready y_scaled h_ready square_done root_ready rstd_ready u_scaled u_ready u_turned uT_ready r_ready score_ready"
        s = {n: m.sem(n + "2") for n in names.split()}
        wv = w_out[0].rearrange("(k p) n -> p k n", p=P)

        m.start_counts()
        with nc.Block() as block:

            @block.sync
            def _(sp):
                for k in range(PAIRS):
                    if k >= 4:
                        sp.wait_ge(s["wo_lo_ready"], FROM + k - 3)
                    sp.dma_start(stage[:, k % 4], wv[:, k]).then_inc(wo_in, 16)
                    sp.wait_ge(wo_in, FROM + 16 * (k + 1))
                with sp.Fori(0, TT // 2) as g:
                    for p in range(2):
                        row = sp.snap(g * 2 * P + p * P)
                        sp.dma_start(xt[:, p], x[0, bass.ds(row, P), :]).then_inc(x_in[p], 16)
                    for p in range(2):
                        row = sp.snap(g * 2 * P + p * P)
                        sp.wait_ge(s["h_ready"], FROM + g * 2 + p + 1)
                        sp.dma_start(dram["h"][bass.ds(row, P), :], ht[:, p]).then_inc(h_out[p], 16)
                        sp.wait_ge(s["u_ready"], FROM + g * 2 + p + 1)
                        sp.dma_start(dram["u2"][bass.ds(row, P), :], ut[:, p]).then_inc(u_out[p], 16)
                for p in range(2):
                    sp.wait_ge(h_out[p], FROM + 16 * (TT // 2))
                    sp.wait_ge(u_out[p], FROM + 16 * (TT // 2))

            @block.scalar
            def _(act):
                act.dma_start(rw[:, :, :], router_w.rearrange("(k p) n -> p k n", p=P)).then_inc(rw_in, 16)
                for k in range(PAIRS):
                    act.wait_ge(wo_in, FROM + 16 * (k + 1))
                    nc.scalar.activation(w_hi[:, k], stage[:, k % 4], ACT.Copy, scale=WS).then_inc(s["wo_hi_ready"], 1)

                def square(t, p):
                    act.wait_ge(s["h_ready"], FROM + t + 1)
                    since(act, s["square_done"], t)
                    nc.scalar.activation(dump[:, :], ht[:, p % 2], ACT.Square, accum_out=ssq[:, bass.ds(t, 1)]).then_inc(s["square_done"], 1)
                    act.wait_ge(s["square_done"], FROM + t + 1)
                    nc.scalar.activation(root[:, bass.ds(t, 1)], ssq[:, bass.ds(t, 1)], ACT.Sqrt, bias=K["eps"][:, 0:1]).then_inc(s["root_ready"], 1)

                def router(t, p):
                    act.wait_ge(s["u_turned"], FROM + t + 1)
                    since(act, s["r_ready"], t)
                    nc.scalar.activation(uT[:, :, :], tps[:, :, :], ACT.Copy).then_inc(s["uT_ready"], 1)
                    act.wait_ge(s["r_ready"], FROM + t + 1)
                    nc.scalar.activation(one(score, t), rps[:, p % 2], ACT.Copy).then_inc(s["score_ready"], 1)

                with act.Fori(0, TT // 2) as g:
                    for p in range(2):
                        square(g * 2 + p, p)
                        router(g * 2 + p, p)
                act.wait_ge(s["score_ready"], FROM + TT)

            @block.tensor
            def _(pe):
                def turn(t, p):
                    pe.wait_ge(s["u_ready"], FROM + t + 1)
                    since(pe, s["uT_ready"], t)
                    for k in range(KT):
                        mm = nc.tensor.transpose(tps[:, k], ut[:, p % 2, k * P:(k + 1) * P], ident[:, :])
                    mm.then_inc(s["u_turned"], 1)

                def project_out(t, p, between=None):
                    since(pe, s["y_scaled"], t - 1)
                    for half in range(2):
                        cols = slice(half * CH, (half + 1) * CH)
                        n = 0
                        for a, b in ((o_hi, w_hi), (o_hi, w_lo), (o_lo, w_hi)):
                            if half and a is o_lo and between:
                                between()
                            for k in range(PAIRS):
                                mm = nc.tensor.matmul(yps[p % 2][:, cols], tile_cols(a[:, k], t), b[:, k, cols],
                                                      start=(n == 0), stop=(n == 3 * PAIRS - 1))
                                n += 1
                    mm.then_inc(s["y_ready"], 1)

                def router(t, p):
                    pe.wait_ge(s["uT_ready"], FROM + t + 1)
                    since(pe, s["score_ready"], t)
                    for k in range(KT):
                        mm = nc.tensor.matmul(rps[:, p % 2], uT[:, k], rw[:, k], start=(k == 0), stop=(k == KT - 1))
                    mm.then_inc(s["r_ready"], 1)

                def pair(t, p):
                    project_out(t + 1, (p + 1) % 2, between=lambda: turn(t, p))
                    router(t, p)

                pe.wait_ge(s["wo_hi_ready"], FROM + PAIRS)
                pe.wait_ge(s["wo_lo_ready"], FROM + PAIRS)
                pe.wait_ge(rw_in, FROM + 16)
                project_out(0, 0)
                pair(0, 0)
                with pe.Fori(0, (TT - 2) // 2) as g:
                    for p in range(2):
                        pair(g * 2 + (1 + p), (1 + p) % 2)
                turn(TT - 1, 1)
                router(TT - 1, 1)

            @block.vector
            def _(dve):
                for k in range(PAIRS):
                    dve.wait_ge(s["wo_hi_ready"], FROM + k + 1)
                    nc.vector.scalar_tensor_tensor(out=w_lo[:, k], in0=stage[:, k % 4], scalar=WS, in1=w_hi[:, k],
                                                   op0=ALU.mult, op1=ALU.subtract).then_inc(s["wo_lo_ready"], 1)
                with dve.Fori(0, TT // 2) as g:
                    for p in range(2):
                        t = g * 2 + p
                        dve.wait_ge(s["y_ready"], FROM + t + 1)
                        dve.wait_ge(h_out[p], FROM + g * 16)
                        dve.wait_ge(u_out[p], FROM + g * 16)
                        nc.vector.tensor_tensor(ht[:, p], yps[p][:, :], mod2[:, 0], ALU.mult).then_inc(s["y_scaled"], 1)
                        dve.wait_ge(s["y_scaled"], FROM + t + 1)
                        dve.wait_ge(x_in[p], FROM + g * 16 + 16)
                        nc.vector.tensor_tensor(ht[:, p], ht[:, p], xt[:, p], ALU.add).then_inc(s["h_ready"], 1)
                        dve.wait_ge(s["root_ready"], FROM + t + 1)
                        nc.vector.reciprocal(rstd[:, bass.ds(t, 1)], root[:, bass.ds(t, 1)]).then_inc(s["rstd_ready"], 1)
                        dve.wait_ge(s["rstd_ready"], FROM + t + 1)
                        dve.wait_ge(s["u_turned"], FROM + g * 2)
                        nc.vector.scalar_tensor_tensor(out=ut[:, p], in0=ht[:, p], scalar=rstd[:, bass.ds(t, 1)], in1=mod2[:, 2],
                                                       op0=ALU.mult, op1=ALU.mult).then_inc(s["u_scaled"], 1)
                        dve.wait_ge(s["u_scaled"], FROM + t + 1)
                        nc.vector.tensor_tensor(ut[:, p], ut[:, p], mod2[:, 1], ALU.add).then_inc(s["u_ready"], 1)


def route(nc, router_b, K, dram):
    with ExitStack() as ctx:
        m = Memory(nc, ctx)
        score, slot, ends, table = K["score"], K["slot"], K["ends"], K["table"]
        TE = [P, TT, E]
        rb = m.sb("rb", [P, E])
        sel = m.sb("sel", TE)
        pairs = m.sb("pairs", [P, 4, TT * G])
        gscore = m.sb("gscore", [P, TT, G])
        gwin = m.sb("gwin", [P, TT, G])
        best = m.sb("best", [P, TT])
        pick = [m.sb(f"pick{i}", TE) for i in range(2)]
        tmp = m.sb("tmp", TE)
        rank = m.sb("rank", TE)
        sw = m.sb("sw", [P, 3, TT])
        rows = m.sb("rows", [P, 2, TT])
        info = m.sb("info", [P, 2, TT, 2])
        rev_e = m.sb("rev_e", [P, E])
        token = m.sb("token", [P, TT])
        blk = m.sb("blk", [P, NBT])
        cnt_i = m.sb("cnt_i", [P, E], I32)
        nblk = m.sb("nblk", [P, E])
        first = m.sb("first", [P, E])
        past = m.sb("past", [P, NBT, E])
        own = m.sb("own", [P, NBT])
        own_i = m.sb("own_i", [P, NBT], I32)
        zero = m.sb("zero", [P, NBT * 2])
        rps, nps = m.ps("rank_ps", [P, 512]), m.ps("cnt_ps", [P, 512])
        rb_in, scored, iotas, chain, picked, ranked, zeroed, info_ready = (
            m.sem(n) for n in ("rb_in", "scored", "iotas", "chain", "picked", "ranked", "zeroed", "info_ready"))
        info_out = m.sem("info_out", soft=True)

        def spread(ap, n):
            return ap.rearrange("p (a b) -> p a b", b=1).broadcast_to([P, ap.shape[1], n])

        def over(ap, n):
            return ap.rearrange("p (b a) -> p b a", b=1).broadcast_to([P, n, ap.shape[1]])

        m.start_counts()
        with nc.Block() as block:

            @block.sync
            def _(sp):
                sp.dma_start(rb[:, :], router_b.partition_broadcast(P)).then_inc(rb_in, 16)
                sp.wait_ge(iotas, FROM + 4)
                sp.dma_start(dram["info"].rearrange("(p a) b -> p (a b)", p=P), zero[:, :]).then_inc(zeroed, 16)

            @block.gpsimd
            def _(pool):
                nc.gpsimd.iota(rev_e[:, :], pattern=[[-1, E]], base=E, channel_multiplier=0, allow_small_or_imprecise_dtypes=True).then_inc(iotas, 1)
                nc.gpsimd.iota(token[:, :], pattern=[[P, TT]], base=0, channel_multiplier=1, allow_small_or_imprecise_dtypes=True).then_inc(iotas, 1)
                nc.gpsimd.iota(blk[:, :], pattern=[[1, NBT]], base=0, channel_multiplier=0, allow_small_or_imprecise_dtypes=True).then_inc(iotas, 1)
                nc.gpsimd.memset(zero[:, :], 0.0).then_inc(iotas, 1)
                pool.wait_ge(info_ready, FROM + 1)
                pool.wait_ge(zeroed, FROM + 16)
                for i in range(2):
                    for t in range(TT):
                        pool.indirect_dma_start(out=dram["info"], out_offset=bass.IndirectOffsetOnAxis(ap=slot[:, i, t:t + 1], axis=0),
                                                in_=info[:, i, t], in_offset=None).then_inc(info_out, 16)
                pool.wait_ge(info_out, 16 * 2 * TT)

            @block.scalar
            def _(act):
                nc.scalar.activation(score[:, :, :], score[:, :, :], ACT.Sigmoid).then_inc(scored, 1)

            @block.tensor
            def _(pe):
                pe.wait_ge(picked, FROM + 1)
                rz = rps[:, 0:TT * E].rearrange("p (t e) -> p t e", e=E)
                for t in range(TT - 1):
                    nc.tensor.matmul(rz[:, t + 1:TT], K["ones"][:, :], tmp[:, t:t + 1].broadcast_to([P, TT - 1 - t, E]),
                                     start=(t == 0), stop=False, skip_group_check=True)
                nc.tensor.matmul(rz, K["before"][:, :], tmp[:, :, :], start=False, stop=True, skip_group_check=True)
                for t in range(TT):
                    mm = nc.tensor.matmul(nps[:, 0:E], K["ones"][:, :], tmp[:, t], start=(t == 0), stop=(t == TT - 1))
                mm.then_inc(ranked, 1)

            @block.vector
            def _(dve):
                made = [0]

                def then(ins):
                    made[0] += 1
                    ins.then_inc(chain, 1)
                    dve.wait_ge(chain, FROM + made[0])

                tt, ts, stt, red = nc.vector.tensor_tensor, nc.vector.tensor_scalar, nc.vector.scalar_tensor_tensor, nc.vector.tensor_reduce
                dve.wait_ge(rb_in, FROM + 16)
                dve.wait_ge(scored, FROM + 1)
                then(tt(sel[:, :, :], score[:, :, :], over(rb[:, :], TT), ALU.add))
                lane = sel[:, :, :].rearrange("p t (g i) -> p (t g) i", i=4)
                a0, a1, a2, a3 = (lane[:, :, i] for i in range(4))
                b0, b1, b2, b3 = (pairs[:, i] for i in range(4))
                then(tt(b0, a0, a1, ALU.max))
                then(tt(b1, a0, a1, ALU.min))
                then(tt(b2, a2, a3, ALU.max))
                then(tt(b3, a2, a3, ALU.min))
                then(tt(b1, b1, b3, ALU.max))
                then(tt(b3, b0, b2, ALU.min))
                then(tt(b1, b1, b3, ALU.max))
                then(tt(b0, b0, b2, ALU.max))
                gs = gscore[:, :, :]
                then(tt(gs.rearrange("p t g -> p (t g)"), b0, b1, ALU.add))
                dve.wait_ge(iotas, FROM + 4)
                rev_g = over(rev_e[:, E - G:E], TT)
                then(red(best[:, :], gs, AX.X, ALU.max))
                then(tt(gwin[:, :, :], gs, spread(best[:, :], G), ALU.is_equal))
                then(tt(gwin[:, :, :], gwin[:, :, :], rev_g, ALU.mult))
                then(red(best[:, :], gwin[:, :, :], AX.X, ALU.max))
                then(tt(gwin[:, :, :], gwin[:, :, :], spread(best[:, :], G), ALU.is_equal))
                wide = gwin[:, :, :].rearrange("p t g -> p (t g)")
                then(tt(sel[:, :, :].rearrange("p t (g i) -> p (t g) i", i=4), lane, spread(wide, 4), ALU.mult))
                then(ts(wide, wide, 1.0, FAR, ALU.subtract, ALU.mult))
                then(tt(sel[:, :, :].rearrange("p t (g i) -> p (t g) i", i=4), lane, spread(wide, 4), ALU.add))
                for i in range(2):
                    pk = pick[i][:, :, :]
                    then(red(best[:, :], sel[:, :, :], AX.X, ALU.max))
                    then(tt(pk, sel[:, :, :], spread(best[:, :], E), ALU.is_equal))
                    then(tt(pk, pk, over(rev_e[:, :], TT), ALU.mult))
                    then(red(best[:, :], pk, AX.X, ALU.max))
                    then(tt(pk, pk, spread(best[:, :], E), ALU.is_equal))
                    if i == 0:
                        then(stt(out=sel[:, :, :], in0=pk, scalar=-2 * FAR, in1=sel[:, :, :], op0=ALU.mult, op1=ALU.add))
                    then(tt(tmp[:, :, :], pk, score[:, :, :], ALU.mult))
                    then(red(sw[:, i], tmp[:, :, :], AX.X, ALU.add))
                tt(tmp[:, :, :], pick[0][:, :, :], pick[1][:, :, :], ALU.add).then_inc(picked, 1)
                then(tt(sw[:, 2], sw[:, 0], sw[:, 1], ALU.add))
                then(nc.vector.reciprocal(sw[:, 2], sw[:, 2]))
                for i in range(2):
                    then(tt(info[:, i, :, 1], sw[:, i], sw[:, 2], ALU.mult))
                    then(nc.vector.tensor_copy(info[:, i, :, 0], token[:, :]))
                dve.wait_ge(ranked, FROM + 1)
                then(ts(cnt_i[:, :], nps[:, 0:E], float(P - 1), float(P), ALU.add, ALU.max))
                then(ts(cnt_i[:, :], cnt_i[:, :], 7, None, ALU.arith_shift_right))
                then(nc.vector.tensor_copy(nblk[:, :], cnt_i[:, :]))
                then(nc.vector.tensor_tensor_scan(ends[:, :], K["ones"][:, 0:E], nblk[:, :], 0.0, ALU.mult, ALU.add))
                then(tt(first[:, :], ends[:, :], nblk[:, :], ALU.subtract))
                then(ts(first[:, :], first[:, :], float(P), None, ALU.mult))
                then(tt(rank[:, :, :], rps[:, 0:TT * E].rearrange("p (t e) -> p t e", e=E), over(first[:, :], TT), ALU.add))
                for i in range(2):
                    then(tt(tmp[:, :, :], rank[:, :, :], pick[i][:, :, :], ALU.mult))
                    then(red(rows[:, i], tmp[:, :, :], AX.X, ALU.add))
                then(nc.vector.tensor_copy(slot[:, :, :], rows[:, :, :]))
                nc.vector.memset(own_i[:, :], 0).then_inc(info_ready, 1)
                then(tt(past[:, :, :], over(ends[:, :], NBT), spread(blk[:, :], E), ALU.is_le))
                then(red(own[:, :], past[:, :, :], AX.X, ALU.add))
                then(ts(table[:, 0], own[:, :], float(E - 1), None, ALU.min))
                then(ts(table[:, 2], table[:, 0], 1, None, ALU.bitwise_and))
                then(ts(first[:, :], first[:, :], 1.0 / P, None, ALU.mult))
                then(tt(past[:, :, :], over(first[:, :], NBT), spread(blk[:, :], E), ALU.is_equal))
                then(red(own[:, :], past[:, :, :], AX.X, ALU.add))
                then(nc.vector.tensor_copy(table[:, 1], own[:, :]))
                then(nc.vector.tensor_copy(table[:, 3, 0:1], ends[:, E - 1:E]))
                then(ts(table[:, 3, 3:4], table[:, 3, 0:1], -16, 16 * NBT + FROM, ALU.mult, ALU.add))
                then(ts(table[:, 3, 1:2], table[:, 3, 0:1], 1, None, ALU.add))
                then(nc.vector.tensor_copy(table[:, 3, 2:3], table[:, 3, 0:1]))
                then(ts(table[:, 3, 1:3], table[:, 3, 1:3], 1, None, ALU.arith_shift_right))
                then(ts(table[:, 3, 1:3], table[:, 3, 1:3], 16, None, ALU.mult))


def experts(nc, w_gate, w_up, w_down, K, dram):
    with ExitStack() as ctx:
        m = Memory(nc, ctx)
        ident, table, mod2 = K["ident"], K["table"], K["mod2"]
        kinds = ("gate", "up", "down")
        source = {"gate": w_gate, "up": w_up, "down": w_down}
        tiles = {"gate": KT, "up": KT, "down": FT}
        width = {"gate": FF, "up": FF, "down": D}
        stage = {n: m.sb(f"{n}_stage", [P, tiles[n], width[n]]) for n in kinds}
        w_hi = {n: m.sb(f"{n}_hi", [P, 2 * tiles[n], width[n]], F16) for n in kinds}
        w_lo = {n: m.sb(f"{n}_lo", [P, 2 * tiles[n], width[n]], F16) for n in kinds}
        info = m.sb("info_rows", [NBT, P, 2])
        token = m.sb("token_of", [P, NBT], I32)
        weight = m.sb("weight_of", [P, NBT])
        idx = m.sb("idx", [P, 2], I32)
        xg = m.sb("xg", [P, 2, D])
        x_hi = m.sb("x_hi", [P, 2, KT, P], F16)
        x_lo = m.sb("x_lo", [P, 2, KT, P], F16)
        act_g = m.sb("act_g", [P, FF])
        hid = m.sb("hid", [P, 2, FF])
        h_hi = m.sb("h_hi", [P, FT, P], F16)
        h_lo = m.sb("h_lo", [P, FT, P], F16)
        ys = m.sb("ys", [P, 2, D])
        tps = m.ps("tps3", [P, KT, P])
        gps, ups = m.ps("gps", [P, FF]), m.ps("ups", [P, FF])
        hps = m.ps("hps", [P, FT, P])
        yps = m.ps("yps3", [P, D])
        info_in, filled = m.sem("info_in"), m.sem("filled")
        w_in = {n: m.sem(f"{n}_in") for n in kinds}
        hi_made = {n: m.sem(f"{n}_hi_made") for n in kinds}
        lo_made = {n: m.sem(f"{n}_lo_made") for n in kinds}
        x_in = [m.sem(f"xg_in{i}", soft=True) for i in range(2)]
        y_out = [m.sem(f"y_out{i}", soft=True) for i in range(2)]
        names = """all_filled info_turned info_ready idx_ready idx_seen x_turned x_hi_ready x_lo_ready g_ready silu_ready up_ready
            hid_ready h_turned h_hi_ready h_lo_ready y_ready ys_ready"""
        s = {n: m.sem(n + "3") for n in names.split()}

        def blocks(eng, body):
            count = eng.snap(eng.value_load(table[0:1, 3, 0:1], min_val=E, max_val=NBK) + 1)
            for b in range(4):
                body(b, b % 2)
            with eng.Fori(2, NBK // 2) as g:
                for p in range(2):
                    with eng.If(g * 2 + p < count):
                        body(g * 2 + p, p)
            with eng.If(count > NBK):
                body(NBK, 0)

        def is_first(b):
            return isinstance(b, int) and b == 0

        def uses(b, p):
            return b * 8 - 8 * p

        def entry(eng, row, b, top):
            return eng.value_load(table[0:1, row, bass.ds(b, 1)], min_val=0, max_val=top)

        m.start_counts()
        with nc.Block() as block:

            @block.sync
            def _(sp):
                sp.dma_start(info[:, :, :], dram["info"].rearrange("(b p) n -> b p n", p=P)).then_inc(info_in, 16)

                def load(n, e):
                    sp.dma_start(stage[n][:, :, :], source[n][0, bass.ds(e, 1)].rearrange("a (k p) n -> p (a k) n", p=P)).then_inc(w_in[n], 16)

                for n in kinds:
                    load(n, 0)
                with sp.Fori(1, E) as e_:
                    e = sp.snap(e_)
                    for n in kinds:
                        sp.wait_ge(lo_made[n], FROM + e)
                        load(n, e)
                count = sp.value_load(table[0:1, 3, 0:1], min_val=E, max_val=NBK)
                with sp.Fori(E, NBT) as b_:
                    b = sp.snap(b_)
                    with sp.If(count <= b):
                        sp.dma_start(dram["ys"][bass.ds(b * P, P), :], mod2[:, 0]).then_inc(filled, 16)
                sp.wait_ge(filled, sp.value_load(table[0:1, 3, 3:4], min_val=FROM, max_val=FROM + 16 * NBT))
                sp.sem_inc(s["all_filled"], 1)

            @block.gpsimd
            def _(pool):
                def gather(b, p):
                    since(pool, s["x_turned"], b - 1)
                    nc.gpsimd.tensor_copy(idx[:, p:p + 1], token[:, bass.ds(b, 1)]).then_inc(s["idx_ready"], 1)
                    pool.wait_ge(s["idx_ready"], FROM + b + 1)
                    pool.sem_inc(s["idx_seen"], 1)
                    pool.indirect_dma_start(out=xg[:, p], out_offset=None, in_=dram["u2"],
                                            in_offset=bass.IndirectOffsetOnAxis(ap=idx[:, p:p + 1], axis=0)).then_inc(x_in[p], 16)

                def body(b, p):
                    gather(b + 2, p)
                    if not is_first(b):
                        pool.wait_ge(s["ys_ready"], FROM + b)
                        pool.dma_start(dram["ys"][bass.ds(b * P - P, P), :], ys[:, 1 - p]).then_inc(y_out[1 - p], 16)

                pool.wait_ge(s["info_ready"], FROM + 2)
                gather(0, 0)
                gather(1, 1)
                blocks(pool, body)
                stored = [pool.value_load(table[0:1, 3, 1 + p:2 + p], min_val=16, max_val=16 * NBK) for p in range(2)]
                for p in range(2):
                    pool.wait_ge(y_out[p], stored[p])

            @block.tensor
            def _(pe):
                def turn(b, p):
                    pe.wait_ge(x_in[p], uses(b, p) + 16)
                    since(pe, s["x_lo_ready"], b)
                    for k in range(KT):
                        mm = nc.tensor.transpose(tps[:, k], xg[:, p, k * P:(k + 1) * P], ident[:, :])
                    mm.then_inc(s["x_turned"], 1)

                def turn_hidden(b, p):
                    pe.wait_ge(s["hid_ready"], FROM + b + 1)
                    for k in range(FT):
                        mm = nc.tensor.transpose(hps[:, k], hid[:, p, k * P:(k + 1) * P], ident[:, :])
                    mm.then_inc(s["h_turned"], 1)

                def product(out, x, w, kind, half, cols=slice(None)):
                    n = 0
                    K_ = tiles[kind]
                    for a, b in ((0, 0), (1, 0), (0, 1)):
                        for k in range(K_):
                            mm = nc.tensor.matmul(out, x[a][:, k], one(w[b], half * K_ + k)[:, cols], start=(n == 0), stop=(n == 3 * K_ - 1))
                            n += 1
                    return mm

                def body(b, p):
                    e = entry(pe, 0, b, E - 1)
                    half = entry(pe, 2, b, 1)
                    pe.wait_ge(s["x_lo_ready"], FROM + b + 1)
                    pe.wait_ge(lo_made["gate"], FROM + e + 1)
                    since(pe, s["silu_ready"], b)
                    x = (x_hi[:, p], x_lo[:, p])
                    product(gps[:, :], x, (w_hi["gate"], w_lo["gate"]), "gate", half).then_inc(s["g_ready"], 1)
                    if not is_first(b):
                        turn_hidden(b - 1, 1 - p)
                    turn(b + 1, 1 - p)
                    pe.wait_ge(lo_made["up"], FROM + e + 1)
                    product(ups[:, :], x, (w_hi["up"], w_lo["up"]), "up", half).then_inc(s["up_ready"], 1)
                    if not is_first(b):
                        e = entry(pe, 0, b - 1, E - 1)
                        half = entry(pe, 2, b - 1, 1)
                        pe.wait_ge(lo_made["down"], FROM + e + 1)
                        pe.wait_ge(s["h_lo_ready"], FROM + b)
                        since(pe, s["ys_ready"], b - 1)
                        for c in range(2):
                            cols = slice(c * CH, (c + 1) * CH)
                            mm = product(yps[:, cols], (h_hi[:, :, :], h_lo[:, :, :]), (w_hi["down"], w_lo["down"]), "down", half, cols)
                        mm.then_inc(s["y_ready"], 1)

                pe.wait_ge(info_in, FROM + 16)
                for j in range(2):
                    mm = nc.tensor.transpose(hps[:, j, 0:NBT], info[:, :, j], ident[0:NBT, 0:NBT])
                mm.then_inc(s["info_turned"], 1)
                pe.wait_ge(s["info_ready"], FROM + 2)
                turn(0, 0)
                blocks(pe, body)

            @block.scalar
            def _(act):
                def part(n, number, row):
                    act.wait_ge(w_in[n], FROM + number * 16 + 16)
                    out = w_hi[n][:, bass.ds(row, tiles[n]), :]
                    nc.scalar.activation(out, stage[n][:, :, :], ACT.Copy, scale=WS).then_inc(hi_made[n], 1)

                def take_x(b, p):
                    act.wait_ge(s["x_turned"], FROM + b + 1)
                    since(act, s["up_ready"], b - 1)
                    nc.scalar.activation(x_hi[:, p], tps[:, :, :], ACT.Copy).then_inc(s["x_hi_ready"], 1)

                def body(b, p):
                    e = entry(act, 0, b, E - 1)
                    half = entry(act, 2, b, 1)
                    begins = entry(act, 1, b, 1)
                    rows = {n: (act.snap(half * tiles[n]), act.snap(tiles[n] - half * tiles[n])) for n in kinds}
                    act.wait_ge(s["g_ready"], FROM + b + 1)
                    since(act, s["hid_ready"], b)
                    nc.scalar.activation(act_g[:, :], gps[:, :], ACT.Silu, scale=1.0 / WS).then_inc(s["silu_ready"], 1)
                    if not is_first(b):
                        act.wait_ge(s["h_turned"], FROM + b)
                        since(act, s["y_ready"], b - 1)
                        nc.scalar.activation(h_hi[:, :, :], hps[:, :, :], ACT.Copy).then_inc(s["h_hi_ready"], 1)
                    take_x(b + 1, 1 - p)
                    with act.If(begins > 0):
                        since(act, s["y_ready"], b - 1)
                        part("down", e, rows["down"][0])
                        with act.If(e < E - 1):
                            since(act, s["up_ready"], b)
                            part("gate", e + 1, rows["gate"][1])
                            part("up", e + 1, rows["up"][1])

                part("gate", 0, 0)
                part("up", 0, 0)
                take_x(0, 0)
                blocks(act, body)

            @block.vector
            def _(dve):
                def part(n, number, row):
                    dve.wait_ge(hi_made[n], FROM + number + 1)
                    rows = bass.ds(row, tiles[n])
                    nc.vector.scalar_tensor_tensor(out=w_lo[n][:, rows, :], in0=stage[n][:, :, :], scalar=WS, in1=w_hi[n][:, rows, :],
                                                   op0=ALU.mult, op1=ALU.subtract).then_inc(lo_made[n], 1)

                def take_x(b, p):
                    dve.wait_ge(s["x_hi_ready"], FROM + b + 1)
                    nc.vector.tensor_tensor(x_lo[:, p], tps[:, :, :], x_hi[:, p], ALU.subtract).then_inc(s["x_lo_ready"], 1)

                def body(b, p):
                    e = entry(dve, 0, b, E - 1)
                    half = entry(dve, 2, b, 1)
                    begins = entry(dve, 1, b, 1)
                    rows = {n: (dve.snap(half * tiles[n]), dve.snap(tiles[n] - half * tiles[n])) for n in kinds}
                    if not is_first(b):
                        dve.wait_ge(s["h_hi_ready"], FROM + b)
                        nc.vector.tensor_tensor(h_lo[:, :, :], hps[:, :, :], h_hi[:, :, :], ALU.subtract).then_inc(s["h_lo_ready"], 1)
                    take_x(b + 1, 1 - p)
                    with dve.If(begins > 0):
                        part("down", e, rows["down"][0])
                    dve.wait_ge(s["up_ready"], FROM + b + 1)
                    dve.wait_ge(s["silu_ready"], FROM + b + 1)
                    since(dve, s["h_turned"], b - 1)
                    nc.vector.scalar_tensor_tensor(out=hid[:, p], in0=ups[:, :], scalar=1.0 / WS, in1=act_g[:, :],
                                                   op0=ALU.mult, op1=ALU.mult).then_inc(s["hid_ready"], 1)
                    with dve.If(begins > 0):
                        with dve.If(e < E - 1):
                            part("gate", e + 1, rows["gate"][1])
                            part("up", e + 1, rows["up"][1])
                    if not is_first(b):
                        dve.wait_ge(s["y_ready"], FROM + b)
                        if not isinstance(b, int) or b > 2:
                            dve.wait_ge(y_out[1 - p], uses(b - 1, 1 - p))
                        nc.vector.scalar_tensor_tensor(out=ys[:, 1 - p], in0=yps[:, :], scalar=weight[:, bass.ds(b - 1, 1)], in1=mod2[:, 3],
                                                       op0=ALU.mult, op1=ALU.mult).then_inc(s["ys_ready"], 1)

                dve.wait_ge(s["info_turned"], FROM + 1)
                nc.vector.tensor_copy(token[:, :], hps[:, 0, 0:NBT]).then_inc(s["info_ready"], 1)
                nc.vector.tensor_copy(weight[:, :], hps[:, 1, 0:NBT]).then_inc(s["info_ready"], 1)
                dve.wait_ge(s["info_ready"], FROM + 2)
                part("gate", 0, 0)
                part("up", 0, 0)
                take_x(0, 0)
                blocks(dve, body)


def combine(nc, K, dram, out):
    with ExitStack() as ctx:
        m = Memory(nc, ctx)
        slot = K["slot"]
        N = 4
        y = [m.sb(f"y{i}", [P, N, D]) for i in range(2)]
        h = m.sb("h_in", [P, N, D])
        y_in = [[m.sem(f"y_in{i}{n}", soft=True) for n in range(N)] for i in range(2)]
        h_in = [m.sem(f"h_in{n}") for n in range(N)]
        o_out = [m.sem(f"o_out{n}") for n in range(N)]
        summed, added = m.sem("summed"), m.sem("added")
        m.start_counts()
        with nc.Block() as block:

            @block.gpsimd
            def _(pool):
                for t in range(TT):
                    n = t % N
                    if t >= N:
                        pool.wait_ge(added, FROM + t - N + 1)
                    for i in range(2):
                        pool.indirect_dma_start(out=y[i][:, n], out_offset=None, in_=dram["ys"],
                                                in_offset=bass.IndirectOffsetOnAxis(ap=slot[:, i, t:t + 1], axis=0)).then_inc(y_in[i][n], 16)

            @block.scalar
            def _(act):
                for t in range(TT):
                    n = t % N
                    if t >= N:
                        act.wait_ge(o_out[n], FROM + 16 * (t // N))
                    act.dma_start(h[:, n], dram["h"][t * P:(t + 1) * P, :]).then_inc(h_in[n], 16)

            @block.vector
            def _(dve):
                for t in range(TT):
                    n = t % N
                    for i in range(2):
                        dve.wait_ge(y_in[i][n], 16 * (t // N + 1))
                    nc.vector.tensor_tensor(y[0][:, n], y[0][:, n], y[1][:, n], ALU.add).then_inc(summed, 1)
                    dve.wait_ge(summed, FROM + t + 1)
                    dve.wait_ge(h_in[n], FROM + 16 * (t // N + 1))
                    nc.vector.tensor_tensor(h[:, n], h[:, n], y[0][:, n], ALU.add).then_inc(added, 1)

            @block.sync
            def _(sp):
                for t in range(TT):
                    n = t % N
                    sp.wait_ge(added, FROM + t + 1)
                    sp.dma_start(out[0, t * P:(t + 1) * P, :], h[:, n]).then_inc(o_out[n], 16)
                for n in range(N):
                    sp.wait_ge(o_out[n], FROM + 16 * (TT // N))


def decoder_layer(nc, x, c, fox_w_in, fox_b_f, fox_q_gain, fox_k_gain, fox_w_out, norm_gain, ada_w, ada_b,
                  router_w, router_b, moe_w_gate, moe_w_up, moe_w_down, out):
    def scratch(name, shape, dt=F32):
        return nc.dram_tensor(name, shape, dt).ap()

    dram = {n: scratch("s_" + n, (PAIRS, P, S), F16) for n in ("q_hi", "q_lo", "k_hi", "k_lo")}
    dram |= {n: scratch("s_" + n, (H, ROWS, S), F16) for n in ("q_rows", "k_rows")}
    dram |= {n: scratch("s_" + n, (S, D)) for n in ("v", "h", "u2")}
    dram["ys"] = scratch("s_ys", (NBT * P, D))
    dram["info"] = scratch("s_info", (NBT * P, 2))
    with ExitStack() as ctx:
        m = Memory(nc, ctx)
        K = {n: m.sb(n, [P, P]) for n in ("ident", "ones", "upto", "before")}
        K |= {n: m.sb(n, [P, P], F16) for n in ("mask_rows", "big_ident")}
        K["eps"] = m.sb("eps", [P, 2])
        K["mod2"] = m.sb("mod2", [P, 4, D])
        with ExitStack() as inner:
            mi = Memory(nc, inner)
            K["u_hi"], K["u_lo"] = mi.sb("u_hi", [P, KT, S], F16), mi.sb("u_lo", [P, KT, S], F16)
            modulate(nc, x, c, norm_gain, ada_w, ada_b, K)
            project(nc, fox_w_in, fox_b_f, fox_q_gain, fox_k_gain, K, dram)
        K["score"] = m.sb("score", [P, TT, E])
        K["slot"] = m.sb("slot", [P, 2, TT], I32)
        K["ends"] = m.sb("ends", [P, E])
        K["table"] = m.sb("table", [P, 4, NBT], I32)
        with ExitStack() as inner:
            mi = Memory(nc, inner)
            K["o_hi"], K["o_lo"] = mi.sb("o_hi", [P, PAIRS, S], F16), mi.sb("o_lo", [P, PAIRS, S], F16)
            attend(nc, K, dram)
            merge(nc, x, fox_w_out, router_w, K, dram)
        route(nc, router_b, K, dram)
        experts(nc, moe_w_gate, moe_w_up, moe_w_down, K, dram)
        combine(nc, K, dram, out)


_INS = ['x', 'c', 'fox_w_in', 'fox_b_f', 'fox_q_gain', 'fox_k_gain', 'fox_w_out', 'norm_gain', 'ada_w', 'ada_b',
        'router_w', 'router_b', 'moe_w_gate', 'moe_w_up', 'moe_w_down']


def kernel(**inputs):
    import numpy as _np
    import concourse.bacc as _bacc
    from concourse import mybir as _mybir
    from concourse.bass_utils import run_bass_kernel_spmd as _run

    nc = _bacc.Bacc("TRN2", target_bir_lowering=False, num_devices=1)
    arrays, args = {}, []
    for name in _INS:
        a = _np.ascontiguousarray(inputs[name])
        arrays[f"in_{name}_dram"] = a
        args.append(nc.dram_tensor(f"in_{name}_dram", a.shape, _mybir.dt.from_np(a.dtype), kind="ExternalInput").ap())
    out = nc.dram_tensor("out_0_dram", (1, S, D), _mybir.dt.float32, kind="ExternalOutput").ap()
    decoder_layer(nc, *args, out)
    r = _run(nc, [arrays], core_ids=[0])
    return r.results[0]["out_0_dram"]
```

```python
from contextlib import ExitStack

import concourse.bass as bass
from concourse import mybir

F32 = mybir.dt.float32
F16 = mybir.dt.float16
I32 = mybir.dt.int32
ACT = mybir.ActivationFunctionType
ALU = mybir.AluOpType
AX = mybir.AxisListType

P = 128
D = 1024
KT = D // P
S = 2048
TT = S // P
H = 16
HD = 64
PAIRS = H // 2
CH = 512
QC = S // CH
TPC = CH // P
E = 16
G = 4
FF = 512
FT = FF // P
R = S * 2 + E * P
NBK = R // P
NBT = NBK + 3
KINDS = ("gate", "up", "down")
TILES = {"gate": KT, "up": KT, "down": FT}
WIDTH = {"gate": FF, "up": FF, "down": D}
EPS = 1e-6
WS = 32.0
CS = 16.0
ROWS = 6
WIDE = 24
BIG = 60000.0
FAR = 1e30
FROM = 8


class Memory:

    def __init__(self, nc, ctx):
        self.nc, self.ctx, self.sems = nc, ctx, []

    def sb(self, name, shape, dt=F32):
        return self.ctx.enter_context(self.nc.sbuf_tensor(name, shape, dt))

    def ps(self, name, shape, dt=F32):
        return self.ctx.enter_context(self.nc.psum_tensor(name, shape, dt))

    def sem(self, name, soft=False):
        if soft:
            return self.ctx.enter_context(self.nc.semaphore(name))
        self.sems.append(self.ctx.enter_context(self.nc.semaphore(name)))
        return self.sems[-1]

    def start_counts(self):
        with self.nc.Block(no_gpsimd_drain=True) as raising:
            @raising.sync
            def _(sp):
                for sem in self.sems:
                    sp.sem_inc(sem, FROM)


def one(ap, i):
    return ap[:, bass.ds(i, 1), :].rearrange("p a n -> p (a n)")


def since(eng, sem, value):
    if not isinstance(value, int) or value > 0:
        eng.wait_ge(sem, FROM + value)


def tile_cols(ap, t):
    return ap[:, bass.ds(t * P, P)]


def staggered(eng, lead, follow, ahead=1, aside=None):
    for t in range(ahead):
        lead(t, t)
    with eng.Fori(0, TT // 4 - 1) as g:
        for p in range(4):
            lead(g * 4 + (p + ahead), (p + ahead) % 4)
            follow(g * 4 + p, p)
    for p in range(4):
        t = TT - 4 + p
        if p + ahead < 4:
            lead(t + ahead, p + ahead)
        follow(t, p)
        if aside and p < 2:
            aside(p)


def modulate(nc, x, c, norm_gain, ada_w, ada_b, w_in, K):
    with ExitStack() as ctx:
        m = Memory(nc, ctx)
        NADA = 2 * D // CH
        shift1 = m.sb("shift1", [P, D])
        scale1 = m.sb("scale1", [P, D])
        u_hi, u_lo, ident, cond = K["u_hi"], K["u_lo"], K["ident"], K["cond"]
        gain = m.sb("gain", [P, D])
        stage = [K["w_stage"][:, :, :, :].rearrange("p a k n -> p (a k) n")] + [
            whole.rearrange("p a (b n) -> p (a b) n", n=CH)
            for whole in (K["mod2"][:, :, :], K["t_hi"][:, :, :].bitcast(F32), K["t_lo"][:, :, :].bitcast(F32))]
        c8 = m.sb("c8", [KT, P])
        cond8 = m.sb("cond8", [KT, P])
        condb = m.sb("condb", [P, KT, P])
        xt = m.sb("xt", [P, 4, D])
        ut = m.sb("ut", [P, 4, D])
        dump = m.sb("dump", [P, D], F16)
        ssq = m.sb("ssq", [P, TT])
        root = m.sb("root", [P, TT])
        rstd = m.sb("rstd", [P, TT])
        mps = [m.ps(f"mps{i}", [P, CH]) for i in range(NADA)]
        tps = [m.ps(f"tps{i}", [P, KT, P]) for i in range(2)]

        c_in, rows_in, w_first = m.sem("c_in"), m.sem("rows_in"), m.sem("w_first")
        ada_in = [m.sem(f"ada_in{i}") for i in range(NADA)]
        x_in = [m.sem(f"x_in{i}") for i in range(4)]
        const = m.sem("const")
        silu_done, cond_turned, condb_ready = m.sem("silu_done"), m.sem("cond_turned"), m.sem("condb_ready")
        mod_ps, mod_ready, scale_ready, gain_ready = (m.sem(n) for n in ("mod_ps", "mod_ready", "scale_ready", "gain_ready"))
        square_done, root_ready, rstd_ready, u_scaled, u_ready = (
            m.sem(n) for n in ("square_done", "root_ready", "rstd_ready", "u_scaled", "u_ready"))
        u_turned, hi_ready, lo_ready = m.sem("u_turned"), m.sem("hi_ready"), m.sem("lo_ready")
        av = ada_w[0].rearrange("(k p) n -> p k n", p=P)
        order = [2, 3, 0, 1]
        home = [scale1[:, 0:CH], scale1[:, CH:D], shift1[:, 0:CH], shift1[:, CH:D]]

        m.start_counts()
        with nc.Block() as block:

            @block.sync
            def _(sp):
                sp.dma_start(c8[:, :], c.rearrange("a (k p) -> (a k) p", p=P)).then_inc(c_in, 16)
                for i in range(2):
                    sp.dma_start(stage[i], av[:, :, order[i] * CH:(order[i] + 1) * CH]).then_inc(ada_in[i], 16)
                sp.dma_start(scale1[:, :], ada_b[0, D:2 * D].partition_broadcast(P)).then_inc(rows_in, 16)
                sp.dma_start(shift1[:, :], ada_b[0, 0:D].partition_broadcast(P)).then_inc(rows_in, 16)
                sp.dma_start(gain[:, :], norm_gain[0, 0].partition_broadcast(P)).then_inc(rows_in, 16)
                sp.dma_start(stage[2], av[:, :, order[2] * CH:(order[2] + 1) * CH]).then_inc(ada_in[2], 16)
                for p in range(4):
                    sp.dma_start(xt[:, p], x[0, p * P:(p + 1) * P, :]).then_inc(x_in[p], 16)
                    if p == 0:
                        sp.dma_start(stage[3], av[:, :, order[3] * CH:(order[3] + 1) * CH]).then_inc(ada_in[3], 16)
                wv = w_in[0].rearrange("(k p) n -> p k n", p=P)
                sp.wait_ge(mod_ps, FROM + 1)
                sp.dma_start(stage[0], wv[:, :, 0:CH]).then_inc(w_first, 16)
                sp.dma_start(K["wf"][:, :, :], wv[:, :, 3 * D:3 * D + H]).then_inc(w_first, 16)
                with sp.Fori(1, TT // 4) as g:
                    for p in range(4):
                        row = sp.snap(g * 4 * P + p * P)
                        sp.wait_ge(u_scaled, FROM + g * 4 + (p - 3))
                        sp.dma_start(xt[:, p], x[0, bass.ds(row, P), :]).then_inc(x_in[p], 16)
                sp.wait_ge(w_first, FROM + 32)

            @block.gpsimd
            def _(pool):
                nc.gpsimd.memset(K["ident"][:, :], 0.0).then_inc(const, 1)
                nc.gpsimd.memset(K["ones"][:, :], 1.0).then_inc(const, 1)
                nc.gpsimd.memset(K["before"][:, :], 0.0).then_inc(const, 1)
                nc.gpsimd.memset(K["mask_rows"][:, :], 0.0).then_inc(const, 1)
                nc.gpsimd.memset(K["big_ident"][:, :], 0.0).then_inc(const, 1)
                nc.gpsimd.memset(K["eps"][:, 0:1], D * EPS).then_inc(const, 1)
                nc.gpsimd.memset(K["eps"][:, 1:2], HD * WS * WS * EPS).then_inc(const, 1)
                pool.wait_ge(const, FROM + 7)

                def fill(buf, compare, value, base=0):
                    return nc.gpsimd.affine_select(out=buf[:, :], in_=buf[:, :], compare_op=compare, fill=value,
                                                   base=base, pattern=[[-1, P]], channel_multiplier=1).then_inc(const, 1)

                fill(K["ident"], ALU.not_equal, 1.0)
                fill(K["before"], ALU.is_ge, 1.0)
                fill(K["mask_rows"], ALU.is_ge, -BIG)
                fill(K["big_ident"], ALU.not_equal, BIG)
                pool.wait_ge(const, FROM + 11)
                pool.wait_ge(mod_ready, FROM + NADA)
                with pool.Fori(0, TT // 4) as g:
                    for p in range(4):
                        pool.wait_ge(u_scaled, FROM + g * 4 + (p + 1))
                        nc.gpsimd.tensor_tensor(ut[:, p], ut[:, p], shift1[:, :], ALU.add).then_inc(u_ready, 1)

            @block.scalar
            def _(act):
                act.wait_ge(c_in, FROM + 16)
                act.wait_ge(const, FROM + 7)
                nc.scalar.activation(cond8[:, :], c8[:, :], ACT.Silu).then_inc(silu_done, 1)

                def square(t, p):
                    act.wait_ge(x_in[p], FROM + 16 + (t - p) * 4)
                    act.wait_ge(square_done, FROM + t)
                    nc.scalar.activation(dump[:, :], xt[:, p], ACT.Square, accum_out=ssq[:, bass.ds(t, 1)]).then_inc(square_done, 1)
                    act.wait_ge(square_done, FROM + t + 1)
                    nc.scalar.activation(root[:, bass.ds(t, 1)], ssq[:, bass.ds(t, 1)], ACT.Sqrt, bias=K["eps"][:, 0:1]).then_inc(root_ready, 1)

                def hi(t, p):
                    act.wait_ge(u_turned, FROM + t + 1)
                    nc.scalar.activation(u_hi[:, :, bass.ds(t * P, P)], tps[p % 2][:, :, :], ACT.Copy).then_inc(hi_ready, 1)

                staggered(act, square, hi, ahead=3)

            @block.tensor
            def _(pe):
                pe.wait_ge(const, FROM + 11)
                pe.wait_ge(silu_done, FROM + 1)
                nc.tensor.transpose(tps[0][:, 0, 0:KT], cond8[:, :], ident[0:KT, 0:KT]).then_inc(cond_turned, 1)
                pe.wait_ge(condb_ready, FROM + KT + 2)
                for i in range(NADA):
                    pe.wait_ge(ada_in[i], FROM + 16)
                    for k in range(KT):
                        mm = nc.tensor.matmul(mps[i][:, :], condb[:, k], stage[i][:, k], start=(k == 0), stop=(k == KT - 1))
                    mm.then_inc(mod_ps, 1)
                with pe.Fori(0, TT // 4) as g:
                    for p in range(4):
                        t = g * 4 + p
                        pe.wait_ge(u_ready, FROM + t + 1)
                        if p < 2:
                            pe.wait_ge(lo_ready, FROM + g * 4)
                        else:
                            pe.wait_ge(lo_ready, FROM + t - 1)
                        for k in range(KT):
                            mm = nc.tensor.transpose(tps[p % 2][:, k], ut[:, p, k * P:(k + 1) * P], ident[:, :])
                        mm.then_inc(u_turned, 1)

            @block.vector
            def _(dve):
                nc.vector.memset(condb[:, :, :], 1.0).then_inc(condb_ready, 1)
                dve.wait_ge(condb_ready, FROM + 1)
                dve.wait_ge(cond_turned, FROM + 1)
                nc.vector.tensor_copy(cond[:, :], tps[0][:, 0, 0:KT]).then_inc(condb_ready, 1)
                dve.wait_ge(condb_ready, FROM + 2)
                for k in range(KT):
                    nc.vector.tensor_scalar(condb[:, k], condb[:, k], cond[:, k:k + 1], None, ALU.mult).then_inc(condb_ready, 1)
                dve.wait_ge(rows_in, FROM + 48)
                nc.vector.tensor_scalar(gain[:, :], gain[:, :], float(D) ** 0.5, None, ALU.mult).then_inc(gain_ready, 1)

                def add_mod(i):
                    dve.wait_ge(mod_ps, FROM + i + 1)
                    nc.vector.tensor_tensor(home[i], home[i], mps[i][:, :], ALU.add).then_inc(mod_ready, 1)

                add_mod(0)
                add_mod(1)
                dve.wait_ge(mod_ready, FROM + 2)
                dve.wait_ge(gain_ready, FROM + 1)
                nc.vector.scalar_tensor_tensor(out=scale1[:, :], in0=scale1[:, :], scalar=1.0, in1=gain[:, :],
                                               op0=ALU.add, op1=ALU.mult).then_inc(scale_ready, 1)
                dve.wait_ge(scale_ready, FROM + 1)

                def scale(t, p):
                    dve.wait_ge(root_ready, FROM + t + 1)
                    nc.vector.reciprocal(rstd[:, bass.ds(t, 1)], root[:, bass.ds(t, 1)]).then_inc(rstd_ready, 1)
                    dve.wait_ge(rstd_ready, FROM + t + 1)
                    since(dve, u_turned, t - 3)
                    nc.vector.scalar_tensor_tensor(out=ut[:, p], in0=xt[:, p], scalar=rstd[:, bass.ds(t, 1)],
                                                   in1=scale1[:, :], op0=ALU.mult, op1=ALU.mult).then_inc(u_scaled, 1)
                    if isinstance(t, int) and t == 1:
                        add_mod(2)
                        add_mod(3)

                def lo(t, p):
                    dve.wait_ge(hi_ready, FROM + t + 1)
                    cols = bass.ds(t * P, P)
                    nc.vector.tensor_tensor(u_lo[:, :, cols], tps[p % 2][:, :, :], u_hi[:, :, cols], ALU.subtract).then_inc(lo_ready, 1)

                staggered(dve, scale, lo, ahead=3)


def project(nc, w_in, b_f, q_gain, k_gain, K, dram):
    with ExitStack() as ctx:
        m = Memory(nc, ctx)
        u_hi, u_lo, ident = K["u_hi"], K["u_lo"], K["ident"]
        HK = KT // 2
        stage = K["w_stage"]
        w_hi = m.sb("w_hi", [P, 2, KT, CH], F16)
        w_lo = m.sb("w_lo", [P, 2, KT, CH], F16)
        t_hi, t_lo = K["t_hi"], K["t_lo"]
        vt = m.sb("vt", [P, 4, CH])
        sq = m.sb("sq", [P, 2, CH])
        qn = m.sb("qn", [P, 2, CH])
        hss = m.sb("hss", [P, 2, 8])
        hrt = m.sb("hrt", [P, 2, 8])
        hrs = m.sb("hrs", [P, 2, 8])
        wf = K["wf"]
        GR = P // QC
        wf_hi = m.sb("wf_hi", [P, KT, GR], F16)
        wf_lo = m.sb("wf_lo", [P, KT, GR], F16)
        bf = m.sb("bf", [P, 1])
        z = m.sb("z", [P, CH])
        za = m.sb("za", [P, CH])
        upto_tile = m.sb("upto_tile", [P, TPC])
        start_sum = m.sb("start_sum", [P, TPC])
        chunk_before = m.sb("chunk_before", [P, P])
        cum = m.sb("cum", [P, CH])
        gqk = m.sb("gqk", [P, 2])
        grow = m.sb("grow", [P, 2, HD])
        bound = m.sb("bound", [P, 2])
        rem = m.sb("rem", [P, 2, CH])
        krow = m.sb("krow", [P, ROWS, CH], F16)
        qrow = m.sb("qrow", [P, ROWS, CH], F16)
        acc = [m.ps(f"acc{i}", [P, CH]) for i in range(2)]
        qps = [m.ps(f"qps{i}", [P, 4, P]) for i in range(2)]
        fps, cps = m.ps("fps", [P, CH]), m.ps("chunk_ps", [P, CH])

        def sems(*names):
            return [m.sem(n) for n in names]

        w_in_sem = sems("w_in0", "w_in1")
        bf_in, gain_in, wf_parts, f_ps, z_ready, f_act = sems("bf_in", "gain_in", "wf_parts", "f_ps", "z_ready", "f_act")
        w_hi_ready, w_lo_ready = sems("w_hi_ready", "w_lo_ready")
        acc_ready, sq_ready, hss_ready, hrs_ready, qn_ready = sems("acc_ready", "sq_ready", "hss_ready", "hrs_ready", "qn_ready")
        turned, th_ready, tl_ready, t_out = sems("turned", "th_ready", "tl_ready", "t_out")
        v_ready, hrt_ready = sems("v_ready", "hrt_ready")
        v_out = sems(*[f"v_out{i}" for i in range(4)])
        scanned, cum_ps, cum_ready, padded = sems("scanned", "cum_ps", "cum_ready", "padded")
        gains_ready, row_step = sems("gains_ready", "row_step")
        row_out = m.sem("row_out", soft=True)
        heads_first = m.sem("heads_first")
        NQK, NCH = 4, 6
        wv = w_in[0].rearrange("(k p) n -> p k n", p=P)

        m.start_counts()
        with nc.Block() as block:

            @block.sync
            def _(sp):
                def load(j):
                    for h in range(2):
                        sp.wait_ge(w_hi_ready, FROM + 2 * j - 1 + h)
                        sp.wait_ge(w_lo_ready, FROM + 2 * j - 1 + h)
                        sp.dma_start(stage[:, h], wv[:, h * HK:(h + 1) * HK, j * CH:(j + 1) * CH]).then_inc(w_in_sem[h], 16)

                for j in range(NQK):
                    load(j + 1)
                    to = (dram["q_hi"], dram["q_lo"]) if j < 2 else (dram["k_hi"], dram["k_lo"])
                    first = 4 * (j % 2)
                    for g in range(QC):
                        cols = slice(g * CH, (g + 1) * CH)
                        sp.wait_ge(th_ready, FROM + j * TT + 4 * g + 4)
                        sp.dma_start(to[0][first:first + 4, :, cols].rearrange("a p n -> p a n"), t_hi[:, :, cols]).then_inc(t_out, 16)
                        sp.wait_ge(tl_ready, FROM + j * TT + 4 * g + 4)
                        sp.dma_start(to[1][first:first + 4, :, cols].rearrange("a p n -> p a n"), t_lo[:, :, cols]).then_inc(t_out, 16)
                load(NQK + 1)
                sp.wait_ge(t_out, FROM + 16 * 2 * QC * NQK)
                sp.wait_ge(row_out, 32 * QC)
                for to, part in head_operands(K, dram, 0):
                    sp.dma_start(to, part).then_inc(heads_first, 16)
                sp.wait_ge(heads_first, FROM + 16 * 16)

            @block.gpsimd
            def _(pool):
                nc.gpsimd.memset(bf[:, :], 0.0).then_inc(padded, 1)
                nc.gpsimd.memset(wf_hi[:, :, :], 0.0).then_inc(padded, 1)
                nc.gpsimd.memset(wf_lo[:, :, :], 0.0).then_inc(padded, 1)
                nc.gpsimd.memset(chunk_before[:, :], 0.0).then_inc(padded, 1)
                nc.gpsimd.memset(krow[:, :, :], CS).then_inc(row_step, 1)
                nc.gpsimd.memset(qrow[:, 0:ROWS - 1, :], CS).then_inc(row_step, 1)
                nc.gpsimd.memset(qrow[:, ROWS - 1, :], 0.0).then_inc(row_step, 1)
                for i in range(1, QC):
                    pool.wait_ge(padded, FROM + 3 + i)
                    nc.gpsimd.affine_select(out=chunk_before[:, :], in_=chunk_before[:, :], compare_op=ALU.not_equal, fill=1.0,
                                            base=i * GR, pattern=[[-1, P]], channel_multiplier=1).then_inc(padded, 1)
                pool.wait_ge(gains_ready, FROM + 4)
                pool.wait_ge(cum_ready, FROM + 1)
                pool.wait_ge(row_step, FROM + 3)
                nc.gpsimd.tensor_scalar(krow[:, 2], cum[:, :], -1.0 / CS, None, ALU.mult).then_inc(row_step, 1)
                nc.gpsimd.tensor_scalar(rem[:, 0], cum[:, :], -1.0 / CS, None, ALU.mult).then_inc(row_step, 1)
                pool.wait_ge(row_step, FROM + 5)
                nc.gpsimd.tensor_tensor(rem[:, 0], rem[:, 0], krow[:, 2], ALU.subtract).then_inc(row_step, 1)
                pool.wait_ge(row_step, FROM + 6)
                nc.gpsimd.tensor_copy(krow[:, 3], rem[:, 0]).then_inc(row_step, 1)
                pool.wait_ge(row_step, FROM + 7)
                nc.gpsimd.tensor_tensor(krow[:, 4], rem[:, 0], krow[:, 3], ALU.subtract).then_inc(row_step, 1)
                nc.gpsimd.tensor_scalar(rem[:, 1], cum[:, :], bound[:, 1:2], 1.0 / CS, ALU.subtract, ALU.mult).then_inc(row_step, 1)
                pool.wait_ge(row_step, FROM + 9)
                nc.gpsimd.tensor_copy(qrow[:, 0], rem[:, 1]).then_inc(row_step, 1)
                pool.wait_ge(row_step, FROM + 10)
                nc.gpsimd.tensor_tensor(qrow[:, 1], rem[:, 1], qrow[:, 0], ALU.subtract).then_inc(row_step, 1)
                pool.wait_ge(row_step, FROM + 11)
                for g in range(QC):
                    rows, cols = slice(g * GR, g * GR + H), slice(g * CH, (g + 1) * CH)
                    pool.dma_start(dram["k_rows"][:, :, cols], krow[rows, :, :]).then_inc(row_out, 16)
                    pool.dma_start(dram["q_rows"][:, :, cols], qrow[rows, :, :]).then_inc(row_out, 16)
                pool.wait_ge(row_out, 32 * QC)

            @block.scalar
            def _(act):
                act.wait_ge(padded, FROM + 3)
                nc.scalar.activation(wf_hi[:, :, 0:H], wf[:, :, :], ACT.Copy, scale=WS).then_inc(wf_parts, 1)

                def hi(j, h):
                    if j >= 2:
                        act.wait_ge(acc_ready, FROM + (j - 1) * TT)
                    if j:
                        act.wait_ge(w_in_sem[h], FROM + 16 * j)
                    nc.scalar.activation(w_hi[:, j % 2, h * HK:(h + 1) * HK], stage[:, h], ACT.Copy, scale=WS).then_inc(w_hi_ready, 1)

                hi(0, 0)
                hi(0, 1)
                act.dma_start(grow[:, 0], q_gain[0].partition_broadcast(P)).then_inc(gain_in, 16)
                act.dma_start(grow[:, 1], k_gain[0].partition_broadcast(P)).then_inc(gain_in, 16)
                for half in range(2):
                    rows = slice(half * HD, (half + 1) * HD)
                    act.dma_start(gqk[rows, 0:1], q_gain[0].rearrange("(p a) -> p a", a=1)).then_inc(gain_in, 16)
                    act.dma_start(gqk[rows, 1:2], k_gain[0].rearrange("(p a) -> p a", a=1)).then_inc(gain_in, 16)
                for g in range(QC):
                    act.dma_start(bf[g * GR:g * GR + H, :], b_f[0].rearrange("(p a) -> p a", a=1)).then_inc(bf_in, 16)
                act.wait_ge(z_ready, FROM + 2)
                nc.scalar.activation(za[:, :], za[:, :], ACT.Exp, scale=-1.0).then_inc(f_act, 1)
                act.wait_ge(f_act, FROM + 1)
                nc.scalar.activation(za[:, :], za[:, :], ACT.Ln, bias=1.0).then_inc(f_act, 1)
                act.wait_ge(gains_ready, FROM + 1)
                for j in range(NQK):
                    base = j * TT

                    def square(t, p):
                        act.wait_ge(acc_ready, FROM + t + (base + 1))
                        since(act, hss_ready, t + (base - 1))
                        nc.scalar.activation(sq[:, p % 2], acc[p % 2][:, :], ACT.Square).then_inc(sq_ready, 1)
                        act.wait_ge(hss_ready, FROM + t + (base + 1))
                        nc.scalar.activation(hrt[:, p % 2], hss[:, p % 2], ACT.Sqrt, bias=K["eps"][:, 1:2]).then_inc(hrt_ready, 1)

                    def turn_hi(t, p):
                        act.wait_ge(turned, FROM + t + (base + 1))
                        if p == 0:
                            since(act, t_out, 32 * QC * j)
                        scale = gqk[:, 0:1] if j < 2 else 8.0
                        nc.scalar.activation(t_hi[:, :, bass.ds(t * P, P)], qps[p % 2][:, :, :], ACT.Copy, scale=scale).then_inc(th_ready, 1)

                    staggered(act, square, turn_hi, aside=lambda h: hi(j + 1, h))
                hi(NQK + 1, 0)
                hi(NQK + 1, 1)
                for j in range(NCH - NQK):
                    with act.Fori(0, TT // 4) as g:
                        for p in range(4):
                            act.wait_ge(acc_ready, FROM + g * 4 + ((NQK + j) * TT + p + 1))
                            act.wait_ge(v_out[p], FROM + g * 16 + 64 * j)
                            nc.scalar.activation(vt[:, p], acc[p % 2][:, :], ACT.Copy, scale=1.0 / WS).then_inc(v_ready, 1)
                            act.wait_ge(v_ready, FROM + g * 4 + (j * TT + p + 1))
                            act.dma_start(dram["v"][bass.ds(g * 4 * P + p * P, P), j * CH:(j + 1) * CH], vt[:, p]).then_inc(v_out[p], 16)
                for p in range(4):
                    act.wait_ge(v_out[p], FROM + 128)

            @block.tensor
            def _(pe):
                pe.wait_ge(wf_parts, FROM + 2)
                n = 0
                for a, b in ((u_hi, wf_hi), (u_hi, wf_lo), (u_lo, wf_hi)):
                    for k in range(KT):
                        for g in range(QC):
                            mm = nc.tensor.matmul(fps[g * GR:(g + 1) * GR, :], b[:, k], a[:, k, g * CH:(g + 1) * CH],
                                                  start=(n == 0), stop=(n == 3 * KT - 1), skip_group_check=True)
                        n += 1
                mm.then_inc(f_ps, 1)

                for j in range(NCH):
                    base = j * TT
                    pe.wait_ge(w_hi_ready, FROM + 2 * j + 2)
                    pe.wait_ge(w_lo_ready, FROM + 2 * j + 2)

                    def product(t, p):
                        since(pe, qn_ready, t + (base - 1))
                        n = 0
                        for a, b in ((u_hi, w_hi), (u_hi, w_lo), (u_lo, w_hi)):
                            for k in range(KT):
                                mm = nc.tensor.matmul(acc[p % 2][:, :], tile_cols(a[:, k], t), b[:, j % 2, k],
                                                      start=(n == 0), stop=(n == 3 * KT - 1))
                                n += 1
                        mm.then_inc(acc_ready, 1)

                    def turn(t, p):
                        pe.wait_ge(qn_ready, FROM + t + (base + 1))
                        since(pe, tl_ready, t + base)
                        for a in range(4):
                            mm = nc.tensor.transpose(qps[p % 2][:, a], qn[:, p % 2, a * P:(a + 1) * P], ident[:, :])
                        mm.then_inc(turned, 1)

                    if j < NQK:
                        staggered(pe, product, turn)
                    else:
                        jv = j - NQK
                        with pe.Fori(0, TT // 4) as g:
                            for p in range(4):
                                if p < 2 and jv == 0:
                                    pe.wait_ge(qn_ready, FROM + NQK * TT)
                                    pe.wait_ge(v_ready, FROM + g * 4)
                                else:
                                    pe.wait_ge(v_ready, FROM + g * 4 + (jv * TT + p - 1))
                                n = 0
                                for a, b in ((u_hi, w_hi), (u_hi, w_lo), (u_lo, w_hi)):
                                    for k in range(KT):
                                        mm = nc.tensor.matmul(acc[p % 2][:, :], tile_cols(a[:, k], g * 4 + p), b[:, j % 2, k],
                                                              start=(n == 0), stop=(n == 3 * KT - 1))
                                        n += 1
                                mm.then_inc(acc_ready, 1)
                    if j == 0:
                        pe.wait_ge(padded, FROM + 3 + QC)
                        pe.wait_ge(scanned, FROM + TPC + 1)
                        nc.tensor.matmul(cps[:, 0:1], chunk_before[:, :], upto_tile[:, TPC - 1:TPC], start=True, stop=True).then_inc(cum_ps, 1)

            @block.vector
            def _(dve):
                dve.wait_ge(wf_parts, FROM + 1)
                nc.vector.scalar_tensor_tensor(out=wf_lo[:, :, 0:H], in0=wf[:, :, :], scalar=WS, in1=wf_hi[:, :, 0:H],
                                               op0=ALU.mult, op1=ALU.subtract).then_inc(wf_parts, 1)
                def lo(j, h):
                    dve.wait_ge(w_hi_ready, FROM + 2 * j + h + 1)
                    ks = slice(h * HK, (h + 1) * HK)
                    nc.vector.scalar_tensor_tensor(out=w_lo[:, j % 2, ks], in0=stage[:, h], scalar=WS, in1=w_hi[:, j % 2, ks],
                                                   op0=ALU.mult, op1=ALU.subtract).then_inc(w_lo_ready, 1)

                lo(0, 0)
                lo(0, 1)
                dve.wait_ge(gain_in, FROM + 96)
                nc.vector.tensor_tensor(gqk[:, 0:1], gqk[:, 0:1], gqk[:, 1:2], ALU.mult).then_inc(gains_ready, 1)
                nc.vector.tensor_tensor(grow[:, 0], grow[:, 0], grow[:, 1], ALU.mult).then_inc(gains_ready, 1)
                dve.wait_ge(gains_ready, FROM + 2)
                nc.vector.tensor_reduce(bound[:, 0:1], grow[:, 0], AX.X, ALU.max, apply_absolute_value=True).then_inc(gains_ready, 1)
                dve.wait_ge(gains_ready, FROM + 3)
                nc.vector.tensor_scalar(bound[:, 1:2], bound[:, 0:1], float(HD) ** 0.5, None, ALU.mult).then_inc(gains_ready, 1)
                dve.wait_ge(gains_ready, FROM + 4)
                nc.vector.tensor_scalar(K["bound_i"][:, :], bound[:, 1:2], float(2 * WIDE), None, ALU.min).then_inc(gains_ready, 1)
                dve.wait_ge(gains_ready, FROM + 5)
                dve.wait_ge(f_ps, FROM + 1)
                dve.wait_ge(bf_in, FROM + 16 * QC)
                nc.vector.tensor_scalar(z[:, :], fps[:, :], 1.0 / WS, bf[:, 0:1], ALU.mult, ALU.add).then_inc(z_ready, 1)
                dve.wait_ge(z_ready, FROM + 1)
                nc.vector.scalar_tensor_tensor(out=za[:, :], in0=z[:, :], scalar=-1.0, in1=z[:, :],
                                               op0=ALU.mult, op1=ALU.max).then_inc(z_ready, 1)
                dve.wait_ge(z_ready, FROM + 2)
                nc.vector.tensor_scalar(z[:, :], z[:, :], 0.0, None, ALU.min).then_inc(z_ready, 1)
                dve.wait_ge(z_ready, FROM + 3)
                dve.wait_ge(f_act, FROM + 2)
                nc.vector.tensor_tensor(z[:, :], z[:, :], za[:, :], ALU.subtract).then_inc(z_ready, 1)
                dve.wait_ge(z_ready, FROM + 4)
                for i in range(TPC):
                    cols = slice(i * P, (i + 1) * P)
                    nc.vector.tensor_tensor_scan(cum[:, cols], K["ones"][:, :], z[:, cols], 0.0, ALU.mult, ALU.add).then_inc(scanned, 1)
                dve.wait_ge(scanned, FROM + TPC)
                tile_sum = cum[:, :].rearrange("p (t n) -> p t n", n=P)[:, :, P - 1]
                nc.vector.tensor_tensor_scan(upto_tile[:, :], K["ones"][:, 0:TPC], tile_sum, 0.0, ALU.mult, ALU.add).then_inc(scanned, 1)
                for j in range(NQK):
                    base = j * TT

                    def norm(t, p):
                        i = p % 2
                        dve.wait_ge(sq_ready, FROM + t + (base + 1))
                        nc.vector.tensor_reduce(hss[:, i], sq[:, i].rearrange("p (h d) -> p h d", d=HD), AX.X, ALU.add).then_inc(hss_ready, 1)
                        dve.wait_ge(hrt_ready, FROM + t + (base + 1))
                        nc.vector.reciprocal(hrs[:, i], hrt[:, i]).then_inc(hrs_ready, 1)
                        dve.wait_ge(hrs_ready, FROM + t + (base + 1))
                        since(dve, turned, t + (base - 1))
                        r = hrs[:, i].rearrange("p (h a) -> p h a", a=1).broadcast_to([P, 8, HD])
                        nc.vector.tensor_tensor(qn[:, i].rearrange("p (h d) -> p h d", d=HD),
                                                acc[i][:, :].rearrange("p (h d) -> p h d", d=HD), r, ALU.mult).then_inc(qn_ready, 1)

                    def turn_lo(t, p):
                        dve.wait_ge(th_ready, FROM + t + (base + 1))
                        scale = gqk[:, 0:1] if j < 2 else 8.0
                        cols = bass.ds(t * P, P)
                        nc.vector.scalar_tensor_tensor(out=t_lo[:, :, cols], in0=qps[p % 2][:, :, :], scalar=scale, in1=t_hi[:, :, cols],
                                                       op0=ALU.mult, op1=ALU.subtract).then_inc(tl_ready, 1)

                    staggered(dve, norm, turn_lo, aside=lambda h: lo(j + 1, h))
                    if j == 0:
                        dve.wait_ge(cum_ps, FROM + 1)
                        nc.vector.tensor_copy(start_sum[:, 0:1], cps[:, 0:1]).then_inc(scanned, 1)
                        dve.wait_ge(scanned, FROM + TPC + 2)
                        nc.vector.tensor_scalar(start_sum[:, 1:TPC], upto_tile[:, 0:TPC - 1], start_sum[:, 0:1], None, ALU.add).then_inc(scanned, 1)
                        dve.wait_ge(scanned, FROM + TPC + 3)
                        tiles = cum[:, :].rearrange("p (t n) -> p t n", n=P)
                        before = start_sum[:, :].rearrange("p (t a) -> p t a", a=1).broadcast_to([P, TPC, P])
                        nc.vector.tensor_tensor(tiles, tiles, before, ALU.add).then_inc(cum_ready, 1)
                lo(NQK + 1, 0)
                lo(NQK + 1, 1)


def first_heads(K):
    return K["t_hi"][:, 0:2], K["t_hi"][:, 2:4], K["t_lo"][:, 0:2], K["t_lo"][:, 2:4]


def out_weights(K):
    return K["t_hi"][:, :, :].bitcast(F32), K["t_lo"][:, :, :].bitcast(F32)


def head_operands(K, dram, pair, to=None):
    kA, kB, qA, qB = to or first_heads(K)
    extra = slice(HD, HD + ROWS)
    loads = []
    for a in range(2):
        rows = slice(a * HD, (a + 1) * HD)

        def pair_rows(t):
            return dram[t][bass.ds(pair, 1), rows, :].rearrange("a p n -> p (a n)")

        def head_rows(t):
            return dram[t][bass.ds(pair * 2 + a, 1), :, :].rearrange("a p n -> p (a n)")

        loads += [(kA[0:HD, a], pair_rows("k_hi")), (kA[HD:P, a], pair_rows("k_lo")),
                  (kB[0:HD, a], pair_rows("k_hi")), (kB[extra, a], head_rows("k_rows")),
                  (qA[0:HD, a], pair_rows("q_hi")), (qA[HD:P, a], pair_rows("q_hi")),
                  (qB[0:HD, a], pair_rows("q_lo")), (qB[extra, a], head_rows("q_rows"))]
    return loads


def maxima(nc, K, dram):
    with ExitStack() as ctx:
        m = Memory(nc, ctx)
        ident = K["ident"]
        kA, kB, qA, qB = (m.sb(n, [P, 2, S], F16)[:, :, :] for n in ("kA_", "kB_", "qA_", "qB_"))
        part = m.sb("part", [P, 2, TT, QC])
        top = m.sb("top", [P, PAIRS, 2 * TT])
        topT = m.sb("topT", [P, 2, P], F16)
        sps = [m.ps(f"msps{i}", [P, CH]) for i in range(2)]
        tps = m.ps("top_ps", [P, 2, P])
        heads_in, cleared, s_ready, part_ready, top_ready, turned, topT_ready, row_out, first_in = (
            m.sem(n + "_m") for n in ("heads_in", "cleared", "s_ready", "part_ready", "top_ready", "turned", "topT_ready", "row_out", "first_in"))
        steps = [(a, t, kc) for a in range(2) for t in range(TT) for kc in range(t // TPC + 1)]
        NS = len(steps)
        CK = HD + ROWS
        HALF = H // 2

        def width(t, kc):
            return min(CH, (t + 1) * P - kc * CH)

        def if_wide(eng, body):
            with eng.If(eng.value_load(K["bound_i"][0:1, 0:1], min_val=0, max_val=2 * WIDE) > WIDE):
                body()

        m.start_counts()
        with nc.Block() as block:

            @block.sync
            def _(sp):
                def body():
                    with sp.Fori(0, PAIRS) as pair_:
                        pair = sp.snap(pair_)
                        sp.wait_ge(s_ready, FROM + pair * NS)
                        for to, source in head_operands(K, dram, pair, (kA, kB, qA, qB)):
                            sp.dma_start(to, source).then_inc(heads_in, 16)
                    sp.wait_ge(topT_ready, FROM + 2)
                    for h in range(H):
                        rows = dram["q_rows"][h, ROWS - 1, :].rearrange("(t n) -> t n", n=P)
                        sp.dma_start(rows, topT[h % HALF * TT:(h % HALF + 1) * TT, h // HALF]).then_inc(row_out, 16)
                    sp.wait_ge(row_out, FROM + 16 * H)
                    qB0 = first_heads(K)[3]
                    for a in range(2):
                        sp.dma_start(qB0[HD:CK, a], dram["q_rows"][a]).then_inc(first_in, 16)
                    sp.wait_ge(first_in, FROM + 32)
                if_wide(sp, body)

            @block.tensor
            def _(pe):
                def body():
                    with pe.Fori(0, PAIRS) as pair:
                        pe.wait_ge(heads_in, FROM + pair * 256 + 256)
                        for i, (a, t, kc) in enumerate(steps):
                            out = sps[i % 2][:, 0:width(t, kc)]
                            qs, ks = slice(t * P, (t + 1) * P), slice(kc * CH, kc * CH + width(t, kc))
                            if i >= 2:
                                pe.wait_ge(part_ready, FROM + pair * NS + (i - 1))
                            else:
                                pe.wait_ge(part_ready, FROM + pair * NS)
                            nc.tensor.matmul(out, qA[:, a, qs], kA[:, a, ks], start=True, stop=False)
                            if kc == t // TPC:
                                nc.tensor.matmul(sps[i % 2][:, t % TPC * P:(t % TPC + 1) * P], K["big_ident"][:, :], K["mask_rows"][:, :],
                                                 start=False, stop=False, skip_group_check=True)
                            nc.tensor.matmul(out, qB[0:CK, a, qs], kB[0:CK, a, ks], start=False, stop=True).then_inc(s_ready, 1)
                    pe.wait_ge(top_ready, FROM + PAIRS)
                    tops = top[:, :, :].rearrange("p a n -> p (a n)")
                    for half in range(2):
                        nc.tensor.transpose(tps[:, half], tops[:, half * P:(half + 1) * P], ident[:, :]).then_inc(turned, 1)
                if_wide(pe, body)

            @block.vector
            def _(dve):
                def body():
                    nc.vector.memset(part[:, :, :, :], -FAR).then_inc(cleared, 1)
                    dve.wait_ge(cleared, FROM + 1)
                    with dve.Fori(0, PAIRS) as pair:
                        dve.wait_ge(top_ready, FROM + pair)
                        for i, (a, t, kc) in enumerate(steps):
                            dve.wait_ge(s_ready, FROM + pair * NS + (i + 1))
                            nc.vector.tensor_reduce(part[:, a, t, kc:kc + 1], sps[i % 2][:, 0:width(t, kc)], AX.X, ALU.max).then_inc(part_ready, 1)
                        dve.wait_ge(part_ready, FROM + pair * NS + NS)
                        nc.vector.tensor_reduce(one(top, pair), part[:, :, :, :].rearrange("p a t c -> p (a t) c"), AX.X, ALU.max).then_inc(top_ready, 1)
                    dve.wait_ge(turned, FROM + 2)
                    for half in range(2):
                        nc.vector.tensor_scalar(topT[:, half], tps[:, half], -1.0 / CS, None, ALU.mult).then_inc(topT_ready, 1)
                if_wide(dve, body)


def attend(nc, norm_gain, ada_w, ada_b, w_out, K, dram):
    with ExitStack() as ctx:
        m = Memory(nc, ctx)
        o_hi, o_lo = K["o_hi"], K["o_lo"]
        kA, kB, qA, qB = ([first, m.sb(n + "1", [P, 2, S], F16)[:, :, :]] for n, first in zip(("kA", "kB", "qA", "qB"), first_heads(K)))
        v = [m.sb(f"v{i}", [P, TT, P]) for i in range(2)]
        NPROB = 5
        prob = [m.sb(f"prob{i}", [P, 2, CH]) for i in range(NPROB)]
        den = [m.sb(f"den{i}", [P, 2, CH]) for i in range(2)]
        rden = m.sb("rden", [P, CH])
        sps = [m.ps(f"sps{i}", [P, 2, CH]) for i in range(2)]
        ops = [m.ps(f"ops{i}", [P, CH]) for i in range(2)]
        dps = m.ps("dps", [P, CH])
        NAS = 2
        cond, mod2 = K["cond"], K["mod2"]
        ada = m.sb("ada_rows", [P, NAS, 2, CH])
        ada_sum = m.sb("ada_sum", [P, CH])
        gain2 = ada[:, 0, :, :].rearrange("p a n -> p (a n)")
        mps = m.ps("mod_ps_bank", [P, CH])
        heads_in = [m.sem(f"heads_in{i}") for i in range(2)]
        v_in = [m.sem(f"v_in{i}") for i in range(2)]
        ada_in = [m.sem(f"ada_in{i}b") for i in range(NAS)]
        rows_in, gain_in, wo_in = m.sem("rows_in2"), m.sem("gain_in2"), m.sem("wo_in")
        ada_times, ada_summed, mod_ps, mod_ready, mod_scaled = (
            m.sem(n) for n in ("ada_times", "ada_summed", "mod_ps2", "mod_ready2", "mod_scaled2"))
        s_ready, p_ready, pv_done, den_step, den_bc = (m.sem(n) for n in ("s_ready", "p_ready", "pv_done", "den_step", "den_bc"))
        r_ready, o_ready, oh_ready, ol_ready = (m.sem(n) for n in ("r_ready", "o_ready", "oh_ready", "ol_ready"))
        av = ada_w[0].rearrange("(k p) n -> p k n", p=P)
        steps = [(qc, j) for qc in range(QC) for j in range(TPC * (qc + 1))]
        NS = len(steps)
        last_of = {qc: max(i for i, st in enumerate(steps) if st[0] == qc) for qc in range(QC)}
        LOADS = 2 * 8
        CK = HD + ROWS

        def left(i):
            qc, j = steps[i]
            return max(0, j - TPC * qc) * P

        m.start_counts()
        with nc.Block() as block:

            @block.sync
            def _(sp):
                def load(pair, sl):
                    for to, part in head_operands(K, dram, pair, (kA[sl], kB[sl], qA[sl], qB[sl])):
                        sp.dma_start(to, part).then_inc(heads_in[sl], 16)

                def load_v(pair, sl):
                    sp.dma_start(v[sl][:, :, :], dram["v"].rearrange("(t p) n -> p t n", p=P)[:, :, bass.ds(pair * P, P)]).then_inc(v_in[sl], 16)

                def load_ada(pair):
                    for k in range(0, KT, 2):
                        n = k // 2 % NAS
                        since(sp, ada_times, pair * KT + (k - 2 * NAS + 2))
                        sp.dma_start(ada[:, n], av[:, k:k + 2, bass.ds(pair * CH + 2 * D, CH)]).then_inc(ada_in[n], 16)

                load_v(0, 0)
                load(1, 1)
                load_v(1, 1)
                sp.dma_start(mod2[:, :, :].rearrange("p a n -> p (a n)"), ada_b[0, 2 * D:].partition_broadcast(P)).then_inc(rows_in, 16)
                load_ada(0)
                load_ada(1)
                with sp.Fori(1, PAIRS // 2) as g:
                    for sl in range(2):
                        pair = sp.snap(g * 2 + sl)
                        sp.wait_ge(pv_done, FROM + g * 2 * NS + (sl - 1) * NS)
                        load(pair, sl)
                        load_v(pair, sl)
                        load_ada(pair)
                sp.wait_ge(ada_times, FROM + PAIRS * KT)
                sp.dma_start(gain2, norm_gain[0, 1].partition_broadcast(P)).then_inc(gain_in, 16)
                sp.wait_ge(pv_done, FROM + (PAIRS - 1) * NS)
                for i, to in enumerate(out_weights(K)):
                    sp.dma_start(to, w_out[0].rearrange("(i k p) n -> i p k n", i=2, p=P)[i]).then_inc(wo_in, 16)
                sp.wait_ge(wo_in, FROM + 32)

            @block.gpsimd
            def _(pool):
                with pool.Fori(0, PAIRS) as pair:
                    for k in range(KT):
                        n = k // 2 % NAS
                        rows = ada[:, n, k % 2]
                        pool.wait_ge(ada_in[n], FROM + pair * 16 * (KT // 2 // NAS) + 16 * (k // 2 // NAS + 1))
                        if k == 0:
                            pool.wait_ge(mod_ps, FROM + pair)
                            nc.gpsimd.tensor_tensor(ada_sum[:, :], rows, cond[:, 0:1].broadcast_to([P, CH]), ALU.mult).then_inc(ada_times, 1)
                        else:
                            nc.gpsimd.tensor_tensor(rows, rows, cond[:, k:k + 1].broadcast_to([P, CH]), ALU.mult).then_inc(ada_summed, 1)
                            pool.wait_ge(ada_summed, FROM + pair * (KT - 1) + k)
                            pool.wait_ge(ada_times, FROM + pair * KT + k)
                            nc.gpsimd.tensor_tensor(ada_sum[:, :], ada_sum[:, :], rows, ALU.add).then_inc(ada_times, 1)
                pool.wait_ge(gain_in, FROM + 16)
                nc.gpsimd.tensor_scalar(gain2, gain2, float(D) ** 0.5, None, ALU.mult).then_inc(mod_scaled, 1)
                pool.wait_ge(mod_ready, FROM + PAIRS)
                nc.gpsimd.tensor_scalar(mod2[:, 2], mod2[:, 2], 1.0, None, ALU.add).then_inc(mod_scaled, 1)
                nc.gpsimd.tensor_scalar(mod2[:, 0], mod2[:, 0], 1.0 / WS, None, ALU.mult).then_inc(mod_scaled, 1)
                nc.gpsimd.tensor_scalar(mod2[:, 3], mod2[:, 3], 1.0 / WS, None, ALU.mult).then_inc(mod_scaled, 1)
                pool.wait_ge(mod_scaled, FROM + 4)
                nc.gpsimd.tensor_tensor(mod2[:, 2], mod2[:, 2], gain2, ALU.mult).then_inc(mod_scaled, 1)
                pool.wait_ge(mod_scaled, FROM + 5)

            @block.tensor
            def _(pe):
                with pe.Fori(0, PAIRS // 2) as g:
                    for sl in range(2):
                        step0 = g * 2 * NS + sl * NS
                        chunk0 = g * 2 * QC + sl * QC

                        def scores(i):
                            qc, j = steps[i]
                            w0 = left(i)
                            ks, qs = slice(j * P, (j + 1) * P), slice(qc * CH + w0, (qc + 1) * CH)
                            pe.wait_ge(p_ready, FROM + step0 + (i - 1))
                            for a in range(2):
                                out = sps[i % 2][:, a, w0:CH]
                                diag = j >= TPC * qc
                                nc.tensor.matmul(out, kA[sl][:, a, ks], qA[sl][:, a, qs], start=True, stop=False)
                                if diag:
                                    nc.tensor.matmul(sps[i % 2][:, a, w0:w0 + P], K["mask_rows"][:, :], K["big_ident"][:, :],
                                                     start=False, stop=False, skip_group_check=True)
                                mm = nc.tensor.matmul(out, kB[sl][0:CK, a, ks], qB[sl][0:CK, a, qs], start=False, stop=True)
                            mm.then_inc(s_ready, 1)

                        def weigh(i):
                            qc, j = steps[i]
                            w0 = left(i)
                            pe.wait_ge(p_ready, FROM + step0 + (i + 1))
                            if j == 0:
                                pe.wait_ge(o_ready, FROM + chunk0 + (qc - 1))
                            for a in range(2):
                                rows = slice(a * HD, (a + 1) * HD)
                                mm = nc.tensor.matmul(ops[qc % 2][rows, w0:CH], v[sl][:, j, rows], prob[(i + sl * NS) % NPROB][:, a, w0:CH],
                                                      start=(j == 0), stop=(i == last_of[qc]), skip_group_check=True)
                            mm.then_inc(pv_done, 1)

                        def denominators(qc):
                            pe.wait_ge(den_step, FROM + step0 + (last_of[qc] + 1))
                            pe.wait_ge(r_ready, FROM + chunk0 + qc)
                            for a in range(2):
                                rows = slice(a * HD, (a + 1) * HD)
                                mm = nc.tensor.matmul(dps[rows, :], K["ones"][:, 0:HD], den[qc % 2][:, a], start=True, stop=True, skip_group_check=True)
                            mm.then_inc(den_bc, 1)

                        pe.wait_ge(heads_in[sl], FROM + g * 16 * LOADS + 16 * LOADS * sl)
                        scores(0)
                        for i in range(NS):
                            if i + 1 < NS:
                                scores(i + 1)
                            if i == 0:
                                pe.wait_ge(v_in[sl], FROM + g * 16 + 16)
                            weigh(i)
                            qc, j = steps[i]
                            if j == 1 and qc:
                                denominators(qc - 1)
                            if i == last_of[QC - 2]:
                                pe.wait_ge(ada_times, FROM + g * 2 * KT + (sl + 1) * KT)
                                pe.wait_ge(mod_ready, FROM + g * 2 + sl)
                                nc.tensor.matmul(mps[:, :], K["ones"][:, :], ada_sum[:, :], start=True, stop=True).then_inc(mod_ps, 1)
                        denominators(QC - 1)

            @block.scalar
            def _(act):
                with act.Fori(0, PAIRS // 2) as g:
                    for sl in range(2):
                        step0 = g * 2 * NS + sl * NS
                        for i in range(NS):
                            w0 = left(i)
                            act.wait_ge(s_ready, FROM + step0 + (i + 1))
                            act.wait_ge(pv_done, FROM + step0 + (i - NPROB + 1))
                            act.wait_ge(den_step, FROM + step0 + (i - NPROB + 1))
                            nc.scalar.activation(prob[(i + sl * NS) % NPROB][:, :, w0:CH], sps[i % 2][:, :, w0:CH], ACT.Exp).then_inc(p_ready, 1)

            @block.vector
            def _(dve):
                with dve.Fori(0, PAIRS // 2) as g:
                    for sl in range(2):
                        step0 = g * 2 * NS + sl * NS
                        chunk0 = g * 2 * QC + sl * QC

                        def divide(qc):
                            pair = g * 2 + sl
                            n = chunk0 + (qc + 1)
                            dve.wait_ge(den_bc, FROM + n)
                            nc.vector.reciprocal(rden[:, :], dps[:, :]).then_inc(r_ready, 1)
                            dve.wait_ge(r_ready, FROM + n)
                            dve.wait_ge(pv_done, FROM + step0 + (last_of[qc] + 1))
                            nc.vector.tensor_tensor(rden[:, :], ops[qc % 2][:, :], rden[:, :], ALU.mult).then_inc(o_ready, 1)
                            dve.wait_ge(o_ready, FROM + n)
                            oh = one(o_hi, pair)[:, qc * CH:(qc + 1) * CH]
                            ol = one(o_lo, pair)[:, qc * CH:(qc + 1) * CH]
                            nc.vector.tensor_copy(oh, rden[:, :]).then_inc(oh_ready, 1)
                            dve.wait_ge(oh_ready, FROM + n)
                            nc.vector.tensor_tensor(ol, rden[:, :], oh, ALU.subtract).then_inc(ol_ready, 1)

                        for i in range(NS):
                            qc, j = steps[i]
                            w0 = left(i)
                            d = den[qc % 2][:, :, w0:CH]
                            pr = prob[(i + sl * NS) % NPROB][:, :, w0:CH]
                            dve.wait_ge(p_ready, FROM + step0 + (i + 1))
                            if j == 0:
                                dve.wait_ge(den_bc, FROM + chunk0 + (qc - 1))
                                nc.vector.tensor_copy(d, pr).then_inc(den_step, 1)
                            else:
                                dve.wait_ge(den_step, FROM + step0 + i)
                                nc.vector.tensor_tensor(d, d, pr, ALU.add).then_inc(den_step, 1)
                            if j == 2 and qc:
                                divide(qc - 1)
                            if i == last_of[QC - 2] + 5:
                                dve.wait_ge(mod_ps, FROM + g * 2 + (sl + 1))
                                dve.wait_ge(rows_in, FROM + 16)
                                m2 = mod2[:, :, :].rearrange("p a n -> p (a n)")[:, bass.ds(g * 2 * CH + sl * CH, CH)]
                                nc.vector.tensor_tensor(m2, m2, mps[:, :], ALU.add).then_inc(mod_ready, 1)
                        divide(QC - 1)
                dve.wait_ge(ol_ready, FROM + PAIRS * QC)


def merge(nc, x, router_w, K, dram):
    with ExitStack() as ctx:
        m = Memory(nc, ctx)
        o_hi, o_lo, mod2, ident, score = K["o_hi"], K["o_lo"], K["mod2"], K["ident"], K["score"]
        w_hi = m.sb("wo_hi", [P, PAIRS, D], F16)
        w_lo = m.sb("wo_lo", [P, PAIRS, D], F16)
        rw = m.sb("rw", [P, KT, E])
        xt = m.sb("xt2", [P, 2, D])
        ht = m.sb("ht", [P, 2, D])
        ut = m.sb("ut2", [P, 2, D])
        uT = m.sb("uT", [P, KT, P])
        dump = m.sb("dump2", [P, D])
        ssq = m.sb("ssq2", [P, TT])
        root = m.sb("root2", [P, TT])
        rstd = m.sb("rstd2", [P, TT])
        yps = [m.ps(f"yps{i}", [P, D]) for i in range(2)]
        tps = m.ps("tps2", [P, KT, P])
        rps = m.ps("rps", [P, 2, E])
        stage = [out_weights(K)[k // (PAIRS // 2)][:, k % (PAIRS // 2)] for k in range(PAIRS)]
        rw_in = m.sem("rw_in")
        x_in = [m.sem(f"x_in{i}b") for i in range(2)]
        h_out = [m.sem(f"h_out{i}") for i in range(2)]
        u_out = [m.sem(f"u_out{i}") for i in range(2)]
        names = "wo_hi_ready wo_lo_ready y_ready y_scaled h_ready square_done root_ready rstd_ready u_scaled u_ready u_turned uT_ready r_ready score_ready"
        s = {n: m.sem(n + "2") for n in names.split()}

        m.start_counts()
        with nc.Block() as block:

            @block.sync
            def _(sp):
                with sp.Fori(0, TT // 2) as g:
                    for p in range(2):
                        row = sp.snap(g * 2 * P + p * P)
                        sp.dma_start(xt[:, p], x[0, bass.ds(row, P), :]).then_inc(x_in[p], 16)
                    for p in range(2):
                        row = sp.snap(g * 2 * P + p * P)
                        sp.wait_ge(s["h_ready"], FROM + g * 2 + p + 1)
                        sp.dma_start(dram["sum"][bass.ds(row, P), :], ht[:, p]).then_inc(h_out[p], 16)
                        sp.wait_ge(s["u_ready"], FROM + g * 2 + p + 1)
                        sp.dma_start(dram["u2"][bass.ds(row, P), :], ut[:, p]).then_inc(u_out[p], 16)
                for p in range(2):
                    sp.wait_ge(h_out[p], FROM + 16 * (TT // 2))
                    sp.wait_ge(u_out[p], FROM + 16 * (TT // 2))

            @block.scalar
            def _(act):
                act.dma_start(rw[:, :, :], router_w.rearrange("(k p) n -> p k n", p=P)).then_inc(rw_in, 16)
                for k in range(PAIRS):
                    nc.scalar.activation(w_hi[:, k], stage[k], ACT.Copy, scale=WS).then_inc(s["wo_hi_ready"], 1)

                def square(t, p):
                    act.wait_ge(s["h_ready"], FROM + t + 1)
                    since(act, s["square_done"], t)
                    nc.scalar.activation(dump[:, :], ht[:, p % 2], ACT.Square, accum_out=ssq[:, bass.ds(t, 1)]).then_inc(s["square_done"], 1)
                    act.wait_ge(s["square_done"], FROM + t + 1)
                    nc.scalar.activation(root[:, bass.ds(t, 1)], ssq[:, bass.ds(t, 1)], ACT.Sqrt, bias=K["eps"][:, 0:1]).then_inc(s["root_ready"], 1)

                def turned(t, p):
                    act.wait_ge(s["u_turned"], FROM + t + 1)
                    since(act, s["r_ready"], t)
                    nc.scalar.activation(uT[:, :, :], tps[:, :, :], ACT.Copy).then_inc(s["uT_ready"], 1)

                def scores(t, p):
                    act.wait_ge(s["r_ready"], FROM + t + 1)
                    nc.scalar.activation(one(score, t), rps[:, p % 2], ACT.Copy).then_inc(s["score_ready"], 1)

                nc.scalar.activation(root[:, 0:1], K["eps"][:, 0:1], ACT.Sqrt).then_inc(s["wo_hi_ready"], 1)
                act.wait_ge(s["wo_hi_ready"], FROM + PAIRS + 1)
                square(0, 0)
                turned(0, 0)
                with act.Fori(0, (TT - 2) // 2) as g:
                    for p in range(2):
                        t, q = g * 2 + (1 + p), (1 + p) % 2
                        square(t, q)
                        scores(t - 1, 1 - q)
                        turned(t, q)
                square(TT - 1, 1)
                scores(TT - 2, 0)
                turned(TT - 1, 1)
                scores(TT - 1, 1)
                act.wait_ge(s["score_ready"], FROM + TT)

            @block.tensor
            def _(pe):
                def turn(t, p):
                    pe.wait_ge(s["u_ready"], FROM + t + 1)
                    since(pe, s["uT_ready"], t)
                    for k in range(KT):
                        mm = nc.tensor.transpose(tps[:, k], ut[:, p % 2, k * P:(k + 1) * P], ident[:, :])
                    mm.then_inc(s["u_turned"], 1)

                PARTS = ((o_hi, w_hi, "wo_hi_ready"), (o_hi, w_lo, "wo_lo_ready"), (o_lo, w_hi, "wo_hi_ready"))

                def project_first():
                    for k in range(PAIRS):
                        for n, (a, b, made) in enumerate(PARTS):
                            pe.wait_ge(s[made], FROM + k + 1)
                            for half in range(2):
                                cols = slice(half * CH, (half + 1) * CH)
                                mm = nc.tensor.matmul(yps[0][:, cols], a[:, k, 0:P], b[:, k, cols],
                                                      start=(k == 0 and n == 0), stop=(k == PAIRS - 1 and n == len(PARTS) - 1))
                    mm.then_inc(s["y_ready"], 1)

                def project_out(t, p, between=None):
                    since(pe, s["y_scaled"], t - 1)
                    for half in range(2):
                        cols = slice(half * CH, (half + 1) * CH)
                        for n, (a, b, _) in enumerate(PARTS):
                            for k in range(PAIRS):
                                mm = nc.tensor.matmul(yps[p % 2][:, cols], tile_cols(a[:, k], t), b[:, k, cols],
                                                      start=(n == 0 and k == 0), stop=(n == len(PARTS) - 1 and k == PAIRS - 1))
                        if half == 0 and between:
                            between()
                    mm.then_inc(s["y_ready"], 1)

                def router(t, p):
                    pe.wait_ge(s["uT_ready"], FROM + t + 1)
                    since(pe, s["score_ready"], t)
                    for k in range(KT):
                        mm = nc.tensor.matmul(rps[:, p % 2], uT[:, k], rw[:, k], start=(k == 0), stop=(k == KT - 1))
                    mm.then_inc(s["r_ready"], 1)

                def step(t, p, scores=True):
                    project_out(t + 1, (p + 1) % 2, between=(lambda: router(t - 1, (p + 1) % 2)) if scores else None)
                    turn(t, p)

                project_first()
                pe.wait_ge(rw_in, FROM + 16)
                step(0, 0, scores=False)
                with pe.Fori(0, (TT - 2) // 2) as g:
                    for p in range(2):
                        step(g * 2 + (1 + p), (1 + p) % 2)
                router(TT - 2, 0)
                turn(TT - 1, 1)
                router(TT - 1, 1)

            @block.vector
            def _(dve):
                for k in range(PAIRS):
                    dve.wait_ge(s["wo_hi_ready"], FROM + k + 1)
                    nc.vector.scalar_tensor_tensor(out=w_lo[:, k], in0=stage[k], scalar=WS, in1=w_hi[:, k],
                                                   op0=ALU.mult, op1=ALU.subtract).then_inc(s["wo_lo_ready"], 1)
                with dve.Fori(0, TT // 2) as g:
                    for p in range(2):
                        t = g * 2 + p
                        dve.wait_ge(s["y_ready"], FROM + t + 1)
                        dve.wait_ge(h_out[p], FROM + g * 16)
                        dve.wait_ge(u_out[p], FROM + g * 16)
                        nc.vector.tensor_tensor(ht[:, p], yps[p][:, :], mod2[:, 0], ALU.mult).then_inc(s["y_scaled"], 1)
                        dve.wait_ge(s["y_scaled"], FROM + t + 1)
                        dve.wait_ge(x_in[p], FROM + g * 16 + 16)
                        nc.vector.tensor_tensor(ht[:, p], ht[:, p], xt[:, p], ALU.add).then_inc(s["h_ready"], 1)
                        dve.wait_ge(s["root_ready"], FROM + t + 1)
                        nc.vector.reciprocal(rstd[:, bass.ds(t, 1)], root[:, bass.ds(t, 1)]).then_inc(s["rstd_ready"], 1)
                        dve.wait_ge(s["rstd_ready"], FROM + t + 1)
                        dve.wait_ge(s["u_turned"], FROM + g * 2)
                        nc.vector.scalar_tensor_tensor(out=ut[:, p], in0=ht[:, p], scalar=rstd[:, bass.ds(t, 1)], in1=mod2[:, 2],
                                                       op0=ALU.mult, op1=ALU.mult).then_inc(s["u_scaled"], 1)
                        dve.wait_ge(s["u_scaled"], FROM + t + 1)
                        nc.vector.tensor_tensor(ut[:, p], ut[:, p], mod2[:, 1], ALU.add).then_inc(s["u_ready"], 1)


def route(nc, router_b, source, K, dram):
    with ExitStack() as ctx:
        m = Memory(nc, ctx)
        score, table, stage, w_hi, w_lo = K["score"], K["table"], K["stage"], K["w_hi"], K["w_lo"]
        TE = [P, TT, E]
        rb = m.sb("rb", [P, E])
        sel = m.sb("sel", TE)
        pairs = m.sb("pairs", [P, 4, TT * G])
        gscore = m.sb("gscore", [P, TT, G])
        gwin = m.sb("gwin", [P, TT, G])
        best = m.sb("best", [P, TT])
        pick = [m.sb(f"pick{i}", TE) for i in range(2)]
        tmp = m.sb("tmp", TE)
        rank = m.sb("rank", TE)
        LEAD = TT // 2
        upto = [m.sb(f"upto{i}", [P, LEAD + TT, E]) for i in range(2)]
        sw = m.sb("sw", [P, 3, TT])
        rows = m.sb("rows", [P, 2, TT])
        rows_i = m.sb("rows_i", [P, 2, TT], I32)
        part_i = m.sb("part_i", [P, 2, TT], I32)
        place = m.sb("place", [P, 2, TT])
        at_place = m.sb("at_place", [P, 2 * TT, P])
        of_block = m.sb("of_block", [P, 2 * TT, 2, NBT])
        places = m.sb("places", [P, P])
        spare = m.sb("spare", [P, 1])
        pad = m.sb("pad", [P, 3, NBT])
        ends = m.sb("ends", [P, E])
        rev_e = m.sb("rev_e", [P, E])
        token1 = m.sb("token1", [P, TT])
        blk = m.sb("blk", [P, NBT])
        cnt_i = m.sb("cnt_i", [P, E], I32)
        nblk = m.sb("nblk", [P, E])
        first = m.sb("first", [P, E])
        past = m.sb("past", [P, NBT, E], F16)
        own = m.sb("own", [P, NBT])
        rps, nps, ips = m.ps("rank_ps", [P, 512]), m.ps("cnt_ps", [P, 512]), m.ps("info_ps", [P, 2, NBT])
        rb_in, scored, iotas, chain, picked, ranked, hot, info_ps = (
            m.sem(n) for n in ("rb_in", "scored", "iotas", "chain", "picked", "ranked", "hot", "info_ps"))
        first_in, first_hi, first_lo, spare_out = (
            m.sem(n) for n in ("first_in", "first_hi", "first_lo", "spare_out"))

        def spread(ap, n):
            return ap.rearrange("p (a b) -> p a b", b=1).broadcast_to([P, ap.shape[1], n])

        def over(ap, n):
            return ap.rearrange("p (b a) -> p b a", b=1).broadcast_to([P, n, ap.shape[1]])

        m.start_counts()
        with nc.Block() as block:

            @block.sync
            def _(sp):
                sp.dma_start(rb[:, :], router_b.partition_broadcast(P)).then_inc(rb_in, 16)
                for n in ("gate", "up"):
                    sp.dma_start(stage[n][:, :, :], source[n][0, 0].rearrange("(k p) n -> p k n", p=P)).then_inc(first_in, 16)
                    sp.wait_ge(first_in, FROM + (16 if n == "gate" else 32))
                sp.dma_start(stage["down"][:, :, :], source["down"][0, 0].rearrange("(k p) n -> p k n", p=P)).then_inc(first_in, 16)
                sp.dma_start(dram["sum"][S:S + P, :], K["mod2"][:, 0]).then_inc(spare_out, 16)
                sp.wait_ge(spare_out, FROM + 16)
                sp.wait_ge(first_in, FROM + 48)

            @block.gpsimd
            def _(pool):
                nc.gpsimd.iota(rev_e[:, :], pattern=[[-1, E]], base=E, channel_multiplier=0, allow_small_or_imprecise_dtypes=True).then_inc(iotas, 1)
                nc.gpsimd.iota(token1[:, :], pattern=[[P, TT]], base=1, channel_multiplier=1, allow_small_or_imprecise_dtypes=True).then_inc(iotas, 1)
                nc.gpsimd.iota(blk[:, :], pattern=[[1, NBT]], base=0, channel_multiplier=0, allow_small_or_imprecise_dtypes=True).then_inc(iotas, 1)
                nc.gpsimd.iota(places[:, :], pattern=[[1, P]], base=0, channel_multiplier=0, allow_small_or_imprecise_dtypes=True).then_inc(iotas, 1)
                nc.gpsimd.iota(spare[:, :], pattern=[[1, 1]], base=S + 1, channel_multiplier=1, allow_small_or_imprecise_dtypes=True).then_inc(iotas, 1)
                for i, n in enumerate(("gate", "up")):
                    pool.wait_ge(first_hi, FROM + 2 * i + 2)
                    nc.gpsimd.tensor_tensor(w_lo[n][:, 0:KT, :], stage[n][:, :, :], w_hi[n][:, 0:KT, :], ALU.subtract).then_inc(first_lo, 1)
                pool.wait_ge(first_lo, FROM + 2)

            @block.scalar
            def _(act):
                nc.scalar.activation(score[:, :, :], score[:, :, :], ACT.Sigmoid).then_inc(scored, 1)
                for i, n in enumerate(("gate", "up")):
                    act.wait_ge(first_in, FROM + 16 * (i + 1))
                    nc.scalar.activation(w_hi[n][:, 0:KT, :], stage[n][:, :, :], ACT.Copy, scale=WS).then_inc(first_hi, 1)
                    act.wait_ge(first_hi, FROM + 2 * i + 1)
                    nc.scalar.activation(stage[n][:, :, :], stage[n][:, :, :], ACT.Copy, scale=WS).then_inc(first_hi, 1)

            @block.tensor
            def _(pe):
                pe.wait_ge(picked, FROM + 1)
                rz = rps[:, 0:TT * E].rearrange("p (t e) -> p t e", e=E)
                nz = nps[:, 0:TT * E].rearrange("p (t e) -> p t e", e=E)
                nc.tensor.matmul(nz, K["ones"][:, :], tmp[:, :, :], start=True, stop=True).then_inc(ranked, 1)
                nc.tensor.matmul(rz, K["before"][:, :], tmp[:, :, :], start=True, stop=True).then_inc(ranked, 1)
                for i in range(2 * TT):
                    if i % TT == 0:
                        pe.wait_ge(hot, FROM + i // TT + 1)
                    mm = nc.tensor.matmul(ips[:, :, :], at_place[:, i], of_block[:, i], start=(i == 0), stop=(i == 2 * TT - 1))
                mm.then_inc(info_ps, 1)

            @block.vector
            def _(dve):
                made = [0]

                def then(ins):
                    made[0] += 1
                    ins.then_inc(chain, 1)
                    dve.wait_ge(chain, FROM + made[0])

                for up in upto:
                    then(nc.vector.memset(up[:, 0:LEAD], 0.0))
                tt, ts, stt, red = nc.vector.tensor_tensor, nc.vector.tensor_scalar, nc.vector.scalar_tensor_tensor, nc.vector.tensor_reduce
                dve.wait_ge(rb_in, FROM + 16)
                dve.wait_ge(scored, FROM + 1)
                then(tt(sel[:, :, :], score[:, :, :], over(rb[:, :], TT), ALU.add))
                lane = sel[:, :, :].rearrange("p t (g i) -> p (t g) i", i=4)
                a0, a1, a2, a3 = (lane[:, :, i] for i in range(4))
                b0, b1, b2, b3 = (pairs[:, i] for i in range(4))
                then(tt(b0, a0, a1, ALU.max))
                then(tt(b1, a0, a1, ALU.min))
                then(tt(b2, a2, a3, ALU.max))
                then(tt(b3, a2, a3, ALU.min))
                then(tt(b1, b1, b3, ALU.max))
                then(tt(b3, b0, b2, ALU.min))
                then(tt(b1, b1, b3, ALU.max))
                then(tt(b0, b0, b2, ALU.max))
                gs = gscore[:, :, :]
                then(tt(gs.rearrange("p t g -> p (t g)"), b0, b1, ALU.add))
                dve.wait_ge(iotas, FROM + 5)
                rev_g = over(rev_e[:, E - G:E], TT)
                then(red(best[:, :], gs, AX.X, ALU.max))
                then(tt(gwin[:, :, :], gs, spread(best[:, :], G), ALU.is_equal))
                then(tt(gwin[:, :, :], gwin[:, :, :], rev_g, ALU.mult))
                then(red(best[:, :], gwin[:, :, :], AX.X, ALU.max))
                then(tt(gwin[:, :, :], gwin[:, :, :], spread(best[:, :], G), ALU.is_equal))
                wide = gwin[:, :, :].rearrange("p t g -> p (t g)")
                then(tt(sel[:, :, :].rearrange("p t (g i) -> p (t g) i", i=4), lane, spread(wide, 4), ALU.mult))
                then(ts(wide, wide, 1.0, FAR, ALU.subtract, ALU.mult))
                then(tt(sel[:, :, :].rearrange("p t (g i) -> p (t g) i", i=4), lane, spread(wide, 4), ALU.add))
                for i in range(2):
                    pk = pick[i][:, :, :]
                    then(red(best[:, :], sel[:, :, :], AX.X, ALU.max))
                    then(tt(pk, sel[:, :, :], spread(best[:, :], E), ALU.is_equal))
                    then(tt(pk, pk, over(rev_e[:, :], TT), ALU.mult))
                    then(red(best[:, :], pk, AX.X, ALU.max))
                    then(tt(pk, pk, spread(best[:, :], E), ALU.is_equal))
                    if i == 0:
                        then(stt(out=sel[:, :, :], in0=pk, scalar=-2 * FAR, in1=sel[:, :, :], op0=ALU.mult, op1=ALU.add))
                    then(tt(tmp[:, :, :], pk, score[:, :, :], ALU.mult))
                    then(red(sw[:, i], tmp[:, :, :], AX.X, ALU.add))
                tt(tmp[:, :, :], pick[0][:, :, :], pick[1][:, :, :], ALU.add).then_inc(picked, 1)
                then(tt(sw[:, 2], sw[:, 0], sw[:, 1], ALU.add))
                then(nc.vector.reciprocal(sw[:, 2], sw[:, 2]))
                for i in range(2):
                    then(tt(sw[:, i], sw[:, i], sw[:, 2], ALU.mult))
                dve.wait_ge(ranked, FROM + 1)
                nz = nps[:, 0:TT * E].rearrange("p (t e) -> p t e", e=E)
                then(nc.vector.tensor_copy(upto[0][:, LEAD:], nz))
                reach, n = 1, 0
                while reach < TT:
                    then(tt(upto[1 - n][:, LEAD:], upto[n][:, LEAD:], upto[n][:, LEAD - reach:LEAD + TT - reach], ALU.add))
                    reach, n = reach * 2, 1 - n
                chosen, before = upto[n][:, LEAD + TT - 1], upto[n][:, LEAD - 1:LEAD - 1 + TT]
                dve.wait_ge(ranked, FROM + 2)
                then(ts(cnt_i[:, :], chosen, float(P - 1), float(P), ALU.add, ALU.max))
                then(ts(cnt_i[:, :], cnt_i[:, :], 7, None, ALU.arith_shift_right))
                then(nc.vector.tensor_copy(nblk[:, :], cnt_i[:, :]))
                then(nc.vector.tensor_tensor_scan(ends[:, :], K["ones"][:, 0:E], nblk[:, :], 0.0, ALU.mult, ALU.add))
                then(tt(first[:, :], ends[:, :], nblk[:, :], ALU.subtract))
                then(ts(first[:, :], first[:, :], float(P), None, ALU.mult))
                then(tt(rank[:, :, :], rps[:, 0:TT * E].rearrange("p (t e) -> p t e", e=E), over(first[:, :], TT), ALU.add))
                then(tt(rank[:, :, :], rank[:, :, :], before, ALU.add))
                for i in range(2):
                    then(tt(tmp[:, :, :], rank[:, :, :], pick[i][:, :, :], ALU.mult))
                    then(red(rows[:, i], tmp[:, :, :], AX.X, ALU.add))
                then(nc.vector.tensor_copy(rows_i[:, :, :], rows[:, :, :]))
                then(ts(part_i[:, :, :], rows_i[:, :, :], P - 1, None, ALU.bitwise_and))
                then(nc.vector.tensor_copy(place[:, :, :], part_i[:, :, :]))
                then(ts(part_i[:, :, :], rows_i[:, :, :], 7, None, ALU.arith_shift_right))
                then(nc.vector.tensor_copy(rows[:, :, :], part_i[:, :, :]))
                for i in range(2):
                    half = slice(i * TT, (i + 1) * TT)
                    is_block = of_block[:, half, 0]
                    then(tt(at_place[:, half], spread(place[:, i], P), over(places[:, :], TT), ALU.is_equal))
                    then(tt(is_block, spread(rows[:, i], NBT), over(blk[:, :], TT), ALU.is_equal))
                    then(tt(of_block[:, half, 1], is_block, spread(sw[:, i], NBT), ALU.mult))
                    tt(is_block, is_block, spread(token1[:, :], NBT), ALU.mult).then_inc(hot, 1)
                then(tt(past[:, :, :], over(ends[:, :], NBT), spread(blk[:, :], E), ALU.is_le))
                then(red(own[:, :], past[:, :, :], AX.X, ALU.add))
                then(ts(table[:, 0], own[:, :], float(E - 1), None, ALU.min))
                then(ts(table[:, 2], table[:, 0], 1, None, ALU.bitwise_and))
                then(ts(first[:, :], first[:, :], 1.0 / P, None, ALU.mult))
                then(tt(past[:, :, :], over(first[:, :], NBT), spread(blk[:, :], E), ALU.is_equal))
                then(red(own[:, :], past[:, :, :], AX.X, ALU.add))
                then(nc.vector.tensor_copy(table[:, 1], own[:, :]))
                then(nc.vector.tensor_copy(table[:, 3, 0:1], ends[:, E - 1:E]))
                dve.wait_ge(info_ps, FROM + 1)
                then(ts(pad[:, 0], ips[:, 0], 0.0, None, ALU.is_equal))
                then(nc.vector.tensor_copy(K["weight"][:, :], ips[:, 1]))
                then(stt(out=pad[:, 1], in0=pad[:, 0], scalar=-1.0, in1=ips[:, 0], op0=ALU.add, op1=ALU.add))
                then(nc.vector.tensor_copy(K["token"][:, :], pad[:, 1]))
                then(ts(pad[:, 0], pad[:, 0], spare[:, 0:1], -1.0, ALU.mult, ALU.add))
                then(tt(pad[:, 0], pad[:, 0], ips[:, 0], ALU.add))
                then(nc.vector.tensor_copy(K["target"][:, :], pad[:, 0]))


def experts(nc, source, K, dram):
    with ExitStack() as ctx:
        m = Memory(nc, ctx)
        ident, table, mod2 = K["ident"], K["table"], K["mod2"]
        stage, w_hi, w_lo = K["stage"], K["w_hi"], K["w_lo"]
        token, target, weight = K["token"], K["target"], K["weight"]
        MADE = {"gate": 1, "up": 1, "down": 0}
        idx = m.sb("idx", [P, 2], I32)
        idx_to = m.sb("idx_to", [P, 2], I32)
        xg = m.sb("xg", [P, 2, D])
        x_hi = m.sb("x_hi", [P, 2, KT, P], F16)
        x_lo = m.sb("x_lo", [P, 2, KT, P], F16)
        act_g = m.sb("act_g", [P, FF])
        hid = m.sb("hid", [P, 2, FF])
        h_hi = m.sb("h_hi", [P, FT, P], F16)
        h_lo = m.sb("h_lo", [P, FT, P], F16)
        ys = m.sb("ys", [P, 2, D])
        tps = m.ps("tps3", [P, KT, P])
        gps, ups = m.ps("gps", [P, FF]), m.ps("ups", [P, FF])
        hps = m.ps("hps", [P, FT, P])
        yps = m.ps("yps3", [P, D])
        w_in = {n: m.sem(f"{n}_in") for n in KINDS}
        hi_made = {n: m.sem(f"{n}_hi_made") for n in KINDS}
        lo_made = {n: m.sem(f"{n}_lo_made") for n in KINDS}
        x_in = [m.sem(f"xg_in{i}", soft=True) for i in range(2)]
        y_out = m.sem("y_out", soft=True)
        names = """to_ready all_added idx_ready idx_seen x_turned x_hi_ready x_lo_ready g_ready silu_ready up_ready
            hid_ready h_turned h_hi_ready h_lo_ready y_ready ys_ready"""
        s = {n: m.sem(n + "3") for n in names.split()}

        def blocks(eng, body):
            count = eng.snap(eng.value_load(table[0:1, 3, 0:1], min_val=E, max_val=NBK) + 1)
            for b in range(4):
                body(b, b % 2)
            with eng.Fori(2, NBK // 2) as g:
                for p in range(2):
                    with eng.If(g * 2 + p < count):
                        body(g * 2 + p, p)
            with eng.If(count > NBK):
                body(NBK, 0)

        def is_first(b):
            return isinstance(b, int) and b == 0

        def uses(b, p):
            return b * 8 - 8 * p

        def entry(eng, row, b, top):
            return eng.value_load(table[0:1, row, bass.ds(b, 1)], min_val=0, max_val=top)

        m.start_counts()
        with nc.Block() as block:

            @block.sync
            def _(sp):
                for p in range(2):
                    sp.wait_ge(x_in[p], 16)
                with sp.Fori(1, E) as e_:
                    e = sp.snap(e_)
                    for n in KINDS:
                        sp.wait_ge(lo_made[n], FROM + e - MADE[n])
                        sp.dma_start(stage[n][:, :, :], source[n][0, bass.ds(e, 1)].rearrange("a (k p) n -> p (a k) n", p=P)).then_inc(w_in[n], 16)

            @block.gpsimd
            def _(pool):
                def gather(b, p):
                    since(pool, s["x_turned"], b - 1)
                    nc.gpsimd.tensor_copy(idx[:, p:p + 1], token[:, bass.ds(b, 1)]).then_inc(s["idx_ready"], 1)
                    pool.wait_ge(s["idx_ready"], FROM + b + 1)
                    pool.sem_inc(s["idx_seen"], 1)
                    pool.indirect_dma_start(out=xg[:, p], out_offset=None, in_=dram["u2"],
                                            in_offset=bass.IndirectOffsetOnAxis(ap=idx[:, p:p + 1], axis=0)).then_inc(x_in[p], 16)

                def body(b, p):
                    gather(b + 2, p)
                    if not is_first(b):
                        nc.gpsimd.tensor_copy(idx_to[:, 1 - p:2 - p], target[:, bass.ds(b - 1, 1)]).then_inc(s["to_ready"], 1)
                        pool.wait_ge(s["to_ready"], FROM + b)
                        pool.wait_ge(s["ys_ready"], FROM + b)
                        if not isinstance(b, int) or b > 1:
                            pool.wait_ge(y_out, b * 16 - 16)
                        pool.sem_inc(s["idx_seen"], 1)
                        pool.indirect_dma_start(out=dram["sum"], out_offset=bass.IndirectOffsetOnAxis(ap=idx_to[:, 1 - p:2 - p], axis=0),
                                                in_=ys[:, 1 - p], in_offset=None, compute_op=ALU.add).then_inc(y_out, 16)

                gather(0, 0)
                gather(1, 1)
                blocks(pool, body)
                count = pool.value_load(table[0:1, 3, 0:1], min_val=E, max_val=NBK)
                pool.wait_ge(y_out, count * 16)
                pool.sem_inc(s["all_added"], 1)

            @block.tensor
            def _(pe):
                def turn(b, p):
                    pe.wait_ge(x_in[p], uses(b, p) + 16)
                    since(pe, s["x_lo_ready"], b)
                    for k in range(KT):
                        mm = nc.tensor.transpose(tps[:, k], xg[:, p, k * P:(k + 1) * P], ident[:, :])
                    mm.then_inc(s["x_turned"], 1)

                def turn_hidden(b, p):
                    pe.wait_ge(s["hid_ready"], FROM + b + 1)
                    for k in range(FT):
                        mm = nc.tensor.transpose(hps[:, k], hid[:, p, k * P:(k + 1) * P], ident[:, :])
                    mm.then_inc(s["h_turned"], 1)

                def product(out, x, w, kind, half, cols=slice(None)):
                    n = 0
                    K_ = TILES[kind]
                    for a, b in ((0, 0), (1, 0), (0, 1)):
                        for k in range(K_):
                            mm = nc.tensor.matmul(out, x[a][:, k], one(w[b], half * K_ + k)[:, cols], start=(n == 0), stop=(n == 3 * K_ - 1))
                            n += 1
                    return mm

                def body(b, p):
                    e = entry(pe, 0, b, E - 1)
                    half = entry(pe, 2, b, 1)
                    pe.wait_ge(s["x_lo_ready"], FROM + b + 1)
                    pe.wait_ge(lo_made["gate"], FROM + e)
                    since(pe, s["silu_ready"], b)
                    x = (x_hi[:, p], x_lo[:, p])
                    product(gps[:, :], x, (w_hi["gate"], w_lo["gate"]), "gate", half).then_inc(s["g_ready"], 1)
                    if not is_first(b):
                        turn_hidden(b - 1, 1 - p)
                    turn(b + 1, 1 - p)
                    pe.wait_ge(lo_made["up"], FROM + e)
                    product(ups[:, :], x, (w_hi["up"], w_lo["up"]), "up", half).then_inc(s["up_ready"], 1)
                    if not is_first(b):
                        e = entry(pe, 0, b - 1, E - 1)
                        half = entry(pe, 2, b - 1, 1)
                        pe.wait_ge(lo_made["down"], FROM + e + 1)
                        pe.wait_ge(s["h_lo_ready"], FROM + b)
                        since(pe, s["ys_ready"], b - 1)
                        for c in range(2):
                            cols = slice(c * CH, (c + 1) * CH)
                            mm = product(yps[:, cols], (h_hi[:, :, :], h_lo[:, :, :]), (w_hi["down"], w_lo["down"]), "down", half, cols)
                        mm.then_inc(s["y_ready"], 1)

                turn(0, 0)
                blocks(pe, body)

            @block.scalar
            def _(act):
                def part(n, number, row):
                    act.wait_ge(w_in[n], FROM + number * 16)
                    out = w_hi[n][:, bass.ds(row, TILES[n]), :]
                    nc.scalar.activation(out, stage[n][:, :, :], ACT.Copy, scale=WS).then_inc(hi_made[n], 1)

                def take_x(b, p):
                    act.wait_ge(s["x_turned"], FROM + b + 1)
                    since(act, s["up_ready"], b - 1)
                    nc.scalar.activation(x_hi[:, p], tps[:, :, :], ACT.Copy).then_inc(s["x_hi_ready"], 1)

                def body(b, p):
                    e = entry(act, 0, b, E - 1)
                    half = entry(act, 2, b, 1)
                    begins = entry(act, 1, b, 1)
                    rows = {n: (act.snap(half * TILES[n]), act.snap(TILES[n] - half * TILES[n])) for n in KINDS}
                    act.wait_ge(s["g_ready"], FROM + b + 1)
                    since(act, s["hid_ready"], b)
                    nc.scalar.activation(act_g[:, :], gps[:, :], ACT.Silu, scale=1.0 / WS).then_inc(s["silu_ready"], 1)
                    if not is_first(b):
                        act.wait_ge(s["h_turned"], FROM + b)
                        since(act, s["y_ready"], b - 1)
                        nc.scalar.activation(h_hi[:, :, :], hps[:, :, :], ACT.Copy).then_inc(s["h_hi_ready"], 1)
                    take_x(b + 1, 1 - p)
                    with act.If(begins > 0):
                        since(act, s["y_ready"], b - 1)
                        part("down", e, rows["down"][0])
                        with act.If(e < E - 1):
                            since(act, s["up_ready"], b)
                            part("gate", e + 1, rows["gate"][1])
                            part("up", e + 1, rows["up"][1])

                take_x(0, 0)
                blocks(act, body)

            @block.vector
            def _(dve):
                def part(n, number, row):
                    dve.wait_ge(hi_made[n], FROM + number + (1 - MADE[n]))
                    rows = bass.ds(row, TILES[n])
                    nc.vector.scalar_tensor_tensor(out=w_lo[n][:, rows, :], in0=stage[n][:, :, :], scalar=WS, in1=w_hi[n][:, rows, :],
                                                   op0=ALU.mult, op1=ALU.subtract).then_inc(lo_made[n], 1)

                def take_x(b, p):
                    dve.wait_ge(s["x_hi_ready"], FROM + b + 1)
                    nc.vector.tensor_tensor(x_lo[:, p], tps[:, :, :], x_hi[:, p], ALU.subtract).then_inc(s["x_lo_ready"], 1)

                def body(b, p):
                    e = entry(dve, 0, b, E - 1)
                    half = entry(dve, 2, b, 1)
                    begins = entry(dve, 1, b, 1)
                    rows = {n: (dve.snap(half * TILES[n]), dve.snap(TILES[n] - half * TILES[n])) for n in KINDS}
                    if not is_first(b):
                        dve.wait_ge(s["h_hi_ready"], FROM + b)
                        nc.vector.tensor_tensor(h_lo[:, :, :], hps[:, :, :], h_hi[:, :, :], ALU.subtract).then_inc(s["h_lo_ready"], 1)
                    take_x(b + 1, 1 - p)
                    with dve.If(begins > 0):
                        part("down", e, rows["down"][0])
                    dve.wait_ge(s["up_ready"], FROM + b + 1)
                    dve.wait_ge(s["silu_ready"], FROM + b + 1)
                    since(dve, s["h_turned"], b - 1)
                    nc.vector.scalar_tensor_tensor(out=hid[:, p], in0=ups[:, :], scalar=1.0 / WS, in1=act_g[:, :],
                                                   op0=ALU.mult, op1=ALU.mult).then_inc(s["hid_ready"], 1)
                    with dve.If(begins > 0):
                        with dve.If(e < E - 1):
                            part("gate", e + 1, rows["gate"][1])
                            part("up", e + 1, rows["up"][1])
                    if not is_first(b):
                        dve.wait_ge(s["y_ready"], FROM + b)
                        if not isinstance(b, int) or b > 2:
                            dve.wait_ge(y_out, b * 16 - 32)
                        nc.vector.scalar_tensor_tensor(out=ys[:, 1 - p], in0=yps[:, :], scalar=weight[:, bass.ds(b - 1, 1)], in1=mod2[:, 3],
                                                       op0=ALU.mult, op1=ALU.mult).then_inc(s["ys_ready"], 1)

                take_x(0, 0)
                blocks(dve, body)


def finish(nc, dram, out):
    with ExitStack() as ctx:
        m = Memory(nc, ctx)
        out_done = m.sem("out_done")
        m.start_counts()
        with nc.Block() as block:

            @block.sync
            def _(sp):
                N = 4
                for i in range(N):
                    rows = slice(i * S // N, (i + 1) * S // N)
                    sp.dma_start(out[0, rows, :], dram["sum"][rows, :]).then_inc(out_done, 16)
                sp.wait_ge(out_done, FROM + 16 * N)


def decoder_layer(nc, x, c, fox_w_in, fox_b_f, fox_q_gain, fox_k_gain, fox_w_out, norm_gain, ada_w, ada_b,
                  router_w, router_b, moe_w_gate, moe_w_up, moe_w_down, out):
    def scratch(name, shape, dt=F32):
        return nc.dram_tensor(name, shape, dt).ap()

    dram = {n: scratch("s_" + n, (PAIRS, P, S), F16) for n in ("q_hi", "q_lo", "k_hi", "k_lo")}
    dram |= {n: scratch("s_" + n, (H, ROWS, S), F16) for n in ("q_rows", "k_rows")}
    dram |= {n: scratch("s_" + n, (S, D)) for n in ("v", "u2")}
    dram["sum"] = scratch("s_sum", (S + P, D))
    source = {"gate": moe_w_gate, "up": moe_w_up, "down": moe_w_down}
    with ExitStack() as ctx:
        m = Memory(nc, ctx)
        K = {n: m.sb(n, [P, P]) for n in ("ident", "ones", "before")}
        K |= {n: m.sb(n, [P, P], F16) for n in ("mask_rows", "big_ident")}
        K["eps"] = m.sb("eps", [P, 2])
        K["cond"] = m.sb("cond", [P, KT])
        K["mod2"] = m.sb("mod2", [P, 4, D])
        K["score"] = m.sb("score", [P, TT, E])
        K["table"] = m.sb("table", [P, 4, NBT], I32)
        K["bound_i"] = m.sb("bound_i", [P, 1], I32)
        with ExitStack() as middle:
            mm = Memory(nc, middle)
            K["t_hi"], K["t_lo"] = mm.sb("t_hi", [P, 4, S], F16), mm.sb("t_lo", [P, 4, S], F16)
            with ExitStack() as inner:
                mi = Memory(nc, inner)
                K["u_hi"], K["u_lo"] = mi.sb("u_hi", [P, KT, S], F16), mi.sb("u_lo", [P, KT, S], F16)
                K["w_stage"], K["wf"] = mi.sb("w_stage", [P, 2, KT // 2, CH]), mi.sb("wf", [P, KT, H])
                modulate(nc, x, c, norm_gain, ada_w, ada_b, fox_w_in, K)
                project(nc, fox_w_in, fox_b_f, fox_q_gain, fox_k_gain, K, dram)
            with ExitStack() as inner:
                mi = Memory(nc, inner)
                K["o_hi"], K["o_lo"] = mi.sb("o_hi", [P, PAIRS, S], F16), mi.sb("o_lo", [P, PAIRS, S], F16)
                maxima(nc, K, dram)
                attend(nc, norm_gain, ada_w, ada_b, fox_w_out, K, dram)
                merge(nc, x, router_w, K, dram)
        K["token"], K["target"] = m.sb("token", [P, NBT], I32), m.sb("target", [P, NBT], I32)
        K["weight"] = m.sb("weight", [P, NBT])
        K["stage"] = {n: m.sb(f"{n}_stage", [P, TILES[n], WIDTH[n]]) for n in KINDS}
        for part in ("hi", "lo"):
            K["w_" + part] = {n: m.sb(f"{n}_{part}", [P, 2 * TILES[n], WIDTH[n]], F16) for n in KINDS}
        route(nc, router_b, source, K, dram)
        experts(nc, source, K, dram)
        finish(nc, dram, out)


_INS = ['x', 'c', 'fox_w_in', 'fox_b_f', 'fox_q_gain', 'fox_k_gain', 'fox_w_out', 'norm_gain', 'ada_w', 'ada_b',
        'router_w', 'router_b', 'moe_w_gate', 'moe_w_up', 'moe_w_down']


def kernel(**inputs):
    import numpy as _np
    import concourse.bacc as _bacc
    from concourse import mybir as _mybir
    from concourse.bass_utils import run_bass_kernel_spmd as _run

    nc = _bacc.Bacc("TRN2", target_bir_lowering=False, num_devices=1)
    arrays, args = {}, []
    for name in _INS:
        a = _np.ascontiguousarray(inputs[name])
        arrays[f"in_{name}_dram"] = a
        args.append(nc.dram_tensor(f"in_{name}_dram", a.shape, _mybir.dt.from_np(a.dtype), kind="ExternalInput").ap())
    out = nc.dram_tensor("out_0_dram", (1, S, D), _mybir.dt.float32, kind="ExternalOutput").ap()
    decoder_layer(nc, *args, out)
    r = _run(nc, [arrays], core_ids=[0])
    return r.results[0]["out_0_dram"]
```
